# Optimizing a Trainium2 kernel written in Bass

```python
import math
import jax, jax.numpy as jnp
from jax import lax
import numpy as np

D_MODEL = 1024
BATCH = 1
SEQ = 4096
DEPTH = 1
DEC_BATCH = 1
DEC_SEQ = 64
PAST_LEN = 4096

CHUNK = 64
RET_HEADS = 4
RET_DK = D_MODEL // 8
RET_DV = D_MODEL // 8
RET_WIDTH = RET_HEADS * RET_DV
ATT_HEAD_DIM = 64
ATT_Q_HEADS = (D_MODEL // 2) // ATT_HEAD_DIM
ATT_KV_HEADS = 2
ATT_GROUP = ATT_Q_HEADS // ATT_KV_HEADS
ATT_WIDTH = ATT_Q_HEADS * ATT_HEAD_DIM
WINDOW = 128
MIX_WIDTH = RET_WIDTH + ATT_WIDTH
IN_WIDTH = (2 * RET_HEADS * RET_DK + RET_HEADS * RET_DV + RET_WIDTH
            + ATT_WIDTH + 2 * ATT_KV_HEADS * ATT_HEAD_DIM + ATT_WIDTH)
ROPE_BASE = 10000.0
NORM_EPS = 1e-6
GN_EPS = 1e-5

kernel_name = "hymba_retention_swa_sink_stream_step"

def _rmsnorm(x, g):
    xf = x.astype(jnp.float32)
    y = xf * lax.rsqrt(jnp.mean(xf * xf, axis=-1, keepdims=True) + NORM_EPS)
    return (y * g.astype(jnp.float32)).astype(x.dtype)

def _head_norm(o):
    mu = jnp.mean(o, axis=-1, keepdims=True)
    var = jnp.mean(jnp.square(o - mu), axis=-1, keepdims=True)
    return (o - mu) * lax.rsqrt(var + GN_EPS)

def _rope(x, pos):
    d = x.shape[-1]
    inv = 1.0 / (ROPE_BASE ** (jnp.arange(0, d, 2, dtype=jnp.float32) / d))
    ang = pos.astype(jnp.float32)[:, None] * inv[None, :]
    cos = jnp.cos(ang)[None, :, None, :]
    sin = jnp.sin(ang)[None, :, None, :]
    x1, x2 = x[..., : d // 2], x[..., d // 2:]
    return jnp.concatenate([x1 * cos - x2 * sin, x1 * sin + x2 * cos], axis=-1)

def _log_gamma():
    return jnp.log(1.0 - 2.0 ** (-5.0 - jnp.arange(RET_HEADS, dtype=jnp.float32)))

def _retention_chunk(R, q, k, v):
    lg = _log_gamma()
    L = q.shape[1]
    idx = jnp.arange(L, dtype=jnp.float32)
    diff = idx[:, None] - idx[None, :]
    decay = jnp.where(diff[None] >= 0, jnp.exp(jnp.maximum(diff, 0.0)[None] * lg[:, None, None]), 0.0)
    s = jnp.einsum('bqhd,bkhd->bhqk', q, k) * decay[None]
    inner = jnp.einsum('bhqk,bkhv->bqhv', s, v)
    q_dec = jnp.exp((idx + 1.0)[:, None] * lg[None, :])[None, :, :, None]
    cross = jnp.einsum('bqhd,bhdv->bqhv', q, R) * q_dec
    k_dec = jnp.exp((L - 1.0 - idx)[:, None] * lg[None, :])[None, :, :, None]
    R_new = jnp.exp(L * lg)[None, :, None, None] * R + jnp.einsum('bkhd,bkhv->bhdv', k * k_dec, v)
    return R_new, inner + cross

def _retention_prompt(q, k, v):
    B, S, H, _ = q.shape
    nc = S // CHUNK

    def to_chunks(t):
        return t.reshape(B, nc, CHUNK, H, t.shape[-1]).transpose(1, 0, 2, 3, 4)

    R0 = jnp.zeros((B, H, RET_DK, RET_DV), jnp.float32)

    def step(R, inp):
        qc, kc, vc = inp
        return _retention_chunk(R, qc, kc, vc)

    R, o = lax.scan(step, R0, (to_chunks(q), to_chunks(k), to_chunks(v)))
    o = o.transpose(1, 0, 2, 3, 4).reshape(B, S, H, RET_DV)
    return o, R

def _sink_attend(q, k, v, sink, mask):
    s = jnp.einsum('...qhgd,...khd->...hgqk', q, k).astype(jnp.float32) * (ATT_HEAD_DIM ** -0.5)
    if mask is not None:
        s = jnp.where(mask, s, -jnp.inf)
    sk = sink.astype(jnp.float32).reshape(ATT_KV_HEADS, ATT_GROUP)[:, :, None, None]
    m = jnp.maximum(jnp.max(s, axis=-1, keepdims=True), sk)
    p = jnp.exp(s - m)
    denom = jnp.sum(p, axis=-1, keepdims=True) + jnp.exp(sk - m)
    return jnp.einsum('...hgqk,...khd->...qhgd', (p / denom).astype(v.dtype), v)

def _swa_prompt(q, k, v, sink):
    B, S = k.shape[0], k.shape[1]
    nc = S // CHUNK
    nwc = WINDOW // CHUNK
    qb = q.reshape(B, nc, CHUNK, ATT_KV_HEADS, ATT_GROUP, ATT_HEAD_DIM)
    pad = ((0, 0), (WINDOW, 0), (0, 0), (0, 0))
    kp = jnp.pad(k, pad).reshape(B, nc + nwc, CHUNK, ATT_KV_HEADS, ATT_HEAD_DIM)
    vp = jnp.pad(v, pad).reshape(B, nc + nwc, CHUNK, ATT_KV_HEADS, ATT_HEAD_DIM)
    kb = jnp.concatenate([kp[:, j:j + nc] for j in range(nwc + 1)], axis=2)
    vb = jnp.concatenate([vp[:, j:j + nc] for j in range(nwc + 1)], axis=2)
    kpos = jnp.arange(nc)[:, None] * CHUNK - WINDOW + jnp.arange(WINDOW + CHUNK)[None, :]
    mask = (kpos >= 0)[:, None, None, None, :]
    o = _sink_attend(qb, kb, vb, sink, mask)
    return o.reshape(B, S, ATT_WIDTH)

def _in_proj(h, w_in):
    z = h @ w_in
    B, L, _ = z.shape
    sizes = [RET_HEADS * RET_DK, RET_HEADS * RET_DK, RET_HEADS * RET_DV, RET_WIDTH,
             ATT_WIDTH, ATT_KV_HEADS * ATT_HEAD_DIM, ATT_KV_HEADS * ATT_HEAD_DIM, ATT_WIDTH]
    offs = list(np.cumsum(sizes)[:-1])
    rq, rk, rv, rg, aq, ak, av, ag = jnp.split(z, offs, axis=-1)
    rq = rq.reshape(B, L, RET_HEADS, RET_DK)
    rk = rk.reshape(B, L, RET_HEADS, RET_DK)
    rv = rv.reshape(B, L, RET_HEADS, RET_DV)
    aq = aq.reshape(B, L, ATT_KV_HEADS, ATT_GROUP, ATT_HEAD_DIM)
    ak = ak.reshape(B, L, ATT_KV_HEADS, ATT_HEAD_DIM)
    av = av.reshape(B, L, ATT_KV_HEADS, ATT_HEAD_DIM)
    return rq, rk, rv, rg, aq, ak, av, ag

def _layer(x, c, pos, ret_state, k_buf, v_buf, norm_g, w_ada, b_ada, w_in, sink, w_out):
    B, L, _ = x.shape
    mod = jax.nn.silu(c) @ w_ada + b_ada
    shift, scale, gate = jnp.split(mod[:, None, :], 3, axis=-1)
    h = _rmsnorm(x, norm_g) * (1.0 + scale) + shift
    rq, rk, rv, rg, aq, ak, av, ag = _in_proj(h, w_in)
    rq = _rope(rq.astype(jnp.float32), pos)
    rk = _rope(rk.astype(jnp.float32), pos) * (RET_DK ** -0.5)
    rv = rv.astype(jnp.float32)
    if ret_state is None:
        r_out, r_state = _retention_prompt(rq, rk, rv)
    else:
        r_state, r_out = _retention_chunk(ret_state.astype(jnp.float32), rq, rk, rv)
    r_out = _head_norm(r_out).reshape(B, L, RET_WIDTH).astype(x.dtype) * jax.nn.silu(rg)
    if k_buf is None:
        a_out = _swa_prompt(aq, ak, av, sink)
        new_k, new_v = ak[:, -WINDOW:], av[:, -WINDOW:]
    else:
        kf = jnp.concatenate([k_buf.astype(ak.dtype), ak], axis=1)
        vf = jnp.concatenate([v_buf.astype(av.dtype), av], axis=1)
        a_out = _sink_attend(aq, kf, vf, sink, None).reshape(B, L, ATT_WIDTH)
        new_k, new_v = kf[:, -WINDOW:], vf[:, -WINDOW:]
    a_out = a_out * jax.nn.silu(ag)
    y = jnp.concatenate([r_out, a_out], axis=-1) @ w_out
    x = x + gate * y
    return x, r_state, new_k, new_v

def setup_inputs(seed: int = 0) -> dict:
    key = jax.random.key(seed)
    ks = jax.random.split(key, 16)
    f = jnp.float32
    D = D_MODEL
    x_prompt = jax.random.normal(ks[0], (BATCH, SEQ, D), f)
    x_sample = jax.random.normal(ks[1], (DEC_BATCH, DEC_SEQ, D), f)
    c_prompt = jax.random.normal(ks[2], (BATCH, D), f)
    c_sample = jax.random.normal(ks[3], (DEC_BATCH, D), f)
    state_ret = 0.5 * jax.random.normal(ks[4], (DEPTH, DEC_BATCH, RET_HEADS, RET_DK, RET_DV), f)
    cache_k = jax.random.normal(ks[5], (DEPTH, DEC_BATCH, WINDOW, ATT_KV_HEADS, ATT_HEAD_DIM), f)
    cache_v = jax.random.normal(ks[6], (DEPTH, DEC_BATCH, WINDOW, ATT_KV_HEADS, ATT_HEAD_DIM), f)
    norm_g = 1.0 + 0.02 * jax.random.normal(ks[7], (DEPTH, D), f)
    w_ada = 0.5 * jax.random.normal(ks[8], (DEPTH, D, 3 * D), f) * D ** -0.5
    b_ada = 0.01 * jax.random.normal(ks[9], (DEPTH, 3 * D), f)
    w_in = jax.random.normal(ks[10], (DEPTH, D, IN_WIDTH), f) * D ** -0.5
    sink = 0.5 * jax.random.normal(ks[11], (DEPTH, ATT_Q_HEADS), f)
    w_out = jax.random.normal(ks[12], (DEPTH, MIX_WIDTH, D), f) * MIX_WIDTH ** -0.5
    final_g = 1.0 + 0.02 * jax.random.normal(ks[13], (D,), f)
    return {"x_prompt": x_prompt, "x_sample": x_sample, "c_prompt": c_prompt, "c_sample": c_sample,
            "state_ret": state_ret, "cache_k": cache_k, "cache_v": cache_v,
            "norm_g": norm_g, "w_ada": w_ada, "b_ada": b_ada, "w_in": w_in, "sink": sink,
            "w_out": w_out, "final_g": final_g}

def reference(x_prompt, x_sample, c_prompt, c_sample, state_ret, cache_k, cache_v,
              norm_g, w_ada, b_ada, w_in, sink, w_out, final_g):
    pos_p = jnp.arange(x_prompt.shape[1])
    pos_s = PAST_LEN + jnp.arange(x_sample.shape[1])
    xp, xs = x_prompt, x_sample
    rp, kp, vp, rs, ks_, vs = [], [], [], [], [], []
    for l in range(DEPTH):
        xp, r1, k1, v1 = _layer(xp, c_prompt, pos_p, None, None, None,
                                norm_g[l], w_ada[l], b_ada[l], w_in[l], sink[l], w_out[l])
        xs, r2, k2, v2 = _layer(xs, c_sample, pos_s, state_ret[l], cache_k[l], cache_v[l],
                                norm_g[l], w_ada[l], b_ada[l], w_in[l], sink[l], w_out[l])
        rp.append(r1.astype(x_prompt.dtype)); kp.append(k1); vp.append(v1)
        rs.append(r2.astype(state_ret.dtype)); ks_.append(k2); vs.append(v2)
    y_prompt = _rmsnorm(xp, final_g)
    y_sample = _rmsnorm(xs, final_g)
    return (y_prompt, y_sample, jnp.stack(rp), jnp.stack(kp), jnp.stack(vp),
            jnp.stack(rs), jnp.stack(ks_), jnp.stack(vs))


_drawn_inputs = setup_inputs


def setup_inputs(seed=0):
    import zlib

    import numpy as np

    out = dict(_drawn_inputs(seed))
    spreads = {}
    factors = {'sink': 38.765, 'final_g': 7.524}
    for name, (base, spread) in spreads.items():
        noise = np.random.default_rng([zlib.crc32(name.encode()), seed]).standard_normal(out[name].shape)
        drawn = base * np.exp(spread * noise) if base else spread * noise
        out[name] = __import__('jax').numpy.asarray(drawn.astype(out[name].dtype))
    for name, factor in factors.items():
        out[name] = (out[name] * factor).astype(out[name].dtype)
    return out
```

```python
from contextlib import ExitStack

import concourse.bass as bass
from concourse import mybir

F32 = mybir.dt.float32
F32R = mybir.dt.float32r
ALU = mybir.AluOpType
ACT = mybir.ActivationFunctionType

P = 128
D = 1024
KC = D // P
SEQ = 4096
NT = SEQ // P
SAMPLE = NT
HALF = P // 2
COLS = 512
RH = 4
DK = 128
HD = 64
QH = 8
IN_W = 3328
OFF_RQ, OFF_RK, OFF_RV, OFF_RG, OFF_AQ, OFF_KV, OFF_AG = 0, 512, 1024, 1536, 2048, 2560, 2816
KV = 256
NORM_EPS = 1e-6
GN_EPS = 1e-5
GAMMA = [1.0 - 2.0 ** (-5 - h) for h in range(RH)]
SCORE_SCALE = HD ** -0.5
MASKED = -1e30


def build_program(nc, x_prompt, x_sample, c_prompt, c_sample, state_ret, cache_k, cache_v, norm_g, w_ada,
                  b_ada, w_in, sink, w_out, final_g, rope_tab, ident_tab, decay_tab, qdec_tab, vdec_tab,
                  mask_tab, y_prompt, y_sample, ret_prompt, k_prompt, v_prompt, ret_sample, k_sample,
                  v_sample, h_dram, yr_dram, gate_dram):
    ctx = ExitStack()
    with ctx:
        def sb(name, shape, dt=F32, where=ctx):
            return where.enter_context(nc.sbuf_tensor(name, shape, dt))

        def sem(name):
            return ctx.enter_context(nc.semaphore(name))

        wh = sb("wh", [P, 4, KC, COLS], F32R)
        wl = sb("wl", [P, 4, KC, COLS], F32R)
        hf = sb("hf", [P, KC, P])
        hh0 = sb("hh0", [P, KC, P], F32R)
        hl0 = sb("hl0", [P, KC, P], F32R)
        xt0 = sb("xt0", [P, D])
        ident = sb("ident", [P, P])
        small = sb("small", [P, 40])
        neg_half = small[:, 0:8]
        ssq = small[:, 8:10]
        meansq = small[:, 10:11]
        rstd = small[:, 11:12]
        gn_var = small[:, 12:16]
        gn_rstd = small[:, 16:20]
        norm_eps = small[:, 20:21]
        gn_eps = small[:, 21:25]
        zero = small[:, 25:26]
        spare = small[:, 26:27]

        phase_a = ExitStack()
        stage23 = sb("stage23", [P, 2, 2048], F32, phase_a)
        stage01 = sb("stage01", [P, 2, 2048], F32, phase_a)
        hh1 = sb("hh1", [P, KC, P], F32R, phase_a)
        hl1 = sb("hl1", [P, KC, P], F32R, phase_a)
        xn = sb("xn", [P, D], F32, phase_a)
        rope = sb("rope", [P, 192], F32, phase_a)
        swap = sb("swap", [P, COLS], F32, phase_a)
        q_row = sb("q_row", [P, COLS], F32, phase_a)
        k_row = sb("k_row", [P, COLS], F32, phase_a)
        q_t = sb("q_t", [P, COLS], F32, phase_a)
        k_t = sb("k_t", [P, COLS], F32, phase_a)
        v_row = sb("v_row", [P, COLS], F32, phase_a)
        v_dec = sb("v_dec", [P, COLS], F32, phase_a)
        s_t = sb("s_t", [P, COLS], F32, phase_a)
        state = sb("state", [P, COLS], F32, phase_a)
        state_s = sb("state_s", [P, COLS], F32, phase_a)
        r_gate = sb("r_gate", [P, COLS], F32, phase_a)
        r_out = sb("r_out", [P, COLS], F32, phase_a)
        yr_t = sb("yr_t", [P, COLS], F32, phase_a)
        decay = sb("decay", [P, COLS], F32, phase_a)
        qdec = sb("qdec", [P, COLS], F32, phase_a)
        tiny_a = sb("tiny_a", [P, 176], F32, phase_a)
        vdec = tiny_a[:, 0:4]
        gn_stats = tiny_a[:, 4:28].rearrange("p (h s) -> p h s", h=RH)
        gn_mv = tiny_a[:, 28:36].rearrange("p (h s) -> p h s", h=RH)
        c_in = tiny_a[:, 36:52].rearrange("p (c k) -> p c k", c=2)
        c_th = tiny_a[:, 52:68].rearrange("p (c k) -> p c k", c=2)
        c_silu = tiny_a[:, 68:84].rearrange("p (k c) -> p k c", c=2)
        g_col = tiny_a[:, 84:92]
        b_col = tiny_a[:, 92:108]
        h_scale = tiny_a[:, 108:124].rearrange("p (k c) -> p k c", c=2)
        h_shift = tiny_a[:, 124:140].rearrange("p (k c) -> p k c", c=2)
        mod_rows = s_t
        bias_rows = sb("bias_rows", [P, COLS], F32, phase_a)
        phase_a.close()

        wkvh = sb("wkvh", [P, KC, KV], F32R)
        wkvl = sb("wkvl", [P, KC, KV], F32R)
        p_t = sb("p_t", [P, 8, P])
        s_row = sb("s_row", [P, 4, 2 * P])
        o_part = sb("o_part", [P, COLS])
        ya_row = sb("ya_row", [P, COLS])
        gate_s = sb("gate_s", [P, D])
        gate_p = sb("gate_p", [P, D])
        xt1 = sb("xt1", [P, D])
        yr_in = sb("yr_in", [P, 4, P])
        yh = sb("yh", [P, KC, P], F32R)
        yl = sb("yl", [P, KC, P], F32R)
        aq_row = sb("aq_row", [P, COLS])
        kv_rows = [sb(f"kv_row{u}", [P, 3 * P]) for u in range(2)]
        v_prev = sb("v_prev", [P, P])
        aq_t = sb("aq_t", [P, 4, P])
        ak_t = sb("ak_t", [P, 2, 2 * P])
        a_gates = [sb(f"a_gate{u}", [P, COLS]) for u in range(2)]
        o_part1 = sb("o_part1", [P, COLS])
        fin_g = sb("fin_g", [P, D])
        mask = sb("mask", [P, 2, 2 * P])
        kv_cache = sb("kv_cache", [P, 3 * P])
        tiny_b = sb("tiny_b", [P, 64])
        neg_sink = tiny_b[:, 0:8]
        s_max = tiny_b[:, 8:16]
        s_bias = tiny_b[:, 16:24]
        sink_arg = tiny_b[:, 24:32]
        sink_exp = tiny_b[:, 32:40]
        row_sum = tiny_b[:, 40:48]
        den = tiny_b[:, 48:56]
        rden = tiny_b[:, 56:64]
        xts = [xt0, xt1]
        hhs, hls = [hh0, hh1], [hl0, hl1]
        stages = [stage01[:, 0], stage01[:, 1], stage23[:, 0], stage23[:, 1]]

        bank = [ctx.enter_context(nc.psum_tensor(f"bank{i}", [P, COLS], F32)) for i in range(8)]
        za0, za1, xb0, xb1, qs_b, ky_b, out_b, upd_b = bank
        zb0, zb1, zb2, s0_b, s1_b, t0_b, t1_b, pv_b = bank

        c_loaded, mod_loaded, tab_loaded, state_loaded = (sem(n) for n in ("c_loaded", "mod_loaded", "tab_loaded", "state_loaded"))
        stage_loaded = [sem(f"stage{n}_loaded") for n in range(4)]
        c_tanh, c_ready, const_set, ada_used, mod_rows_out, mod_transposed, mod_ready = (
            sem(n) for n in ("c_tanh", "c_ready", "const_set", "ada_used", "mod_rows_out",
                             "mod_transposed", "mod_ready"))
        w_hi_done, w_lo_done, gate_rows, gate_stored, b_rows_loaded = (
            sem(n) for n in ("w_hi_done", "w_lo_done", "gate_rows", "gate_stored", "b_rows_loaded"))
        x_loaded, rope_loaded, h_stored, yr_stored = (sem(n) for n in ("x_loaded", "rope_loaded", "h_stored", "yr_stored"))
        ssq_done, rstd_mean, rstd_done, xn_done, x_transposed, h_done, hi_done, lo_done = (
            sem(n) for n in ("ssq_done", "rstd_mean", "rstd_done", "xn_done", "x_transposed", "h_done", "hi_done", "lo_done"))
        za_ready = sem("za_ready")
        zq_read, q_done, q_transposed, qt_done, zk_read, k_done, k_transposed, kt_done = (
            sem(n) for n in ("zq_read", "q_done", "q_transposed", "qt_done", "zk_read", "k_done", "k_transposed", "kt_done"))
        q_mul, k_mul = sem("q_mul"), sem("k_mul")
        vdec_done, v_done, rg_tanh, rg_done, s_ready, st_done, out_ready, upd_ready, state_done = (
            sem(n) for n in ("vdec_done", "v_done", "rg_tanh", "rg_done", "s_ready", "st_done", "out_ready",
                             "upd_ready", "state_done"))
        gn_stat_done, gn_mv_done, gn_var_done, gn_rstd_done, gn_done, yr_done, yr_transposed, yrt_done = (
            sem(n) for n in ("gn_stat_done", "gn_mv_done", "gn_var_done", "gn_rstd_done", "gn_done", "yr_done",
                             "yr_transposed", "yrt_done"))
        state_out = sem("state_out")
        fixed_loaded, hb_loaded, yr_loaded, cache_loaded, newer_loaded, kv_out = (
            sem(n) for n in ("fixed_loaded", "hb_loaded", "yr_loaded", "cache_loaded", "newer_loaded", "kv_out"))
        xb_loaded = [sem(f"xb{u}_loaded") for u in range(2)]
        y_stored = [sem(f"y{u}_stored") for u in range(2)]
        b_set, b_split, bh_hi, zb_ready = (sem(n) for n in ("b_set", "b_split", "bh_hi", "zb_ready"))
        kv_done, aq_done, qk_transposed, aqt_done, akt_done, k_shifted, v_shifted = (
            sem(n) for n in ("kv_done", "aq_done", "qk_transposed", "aqt_done", "akt_done", "k_shifted", "v_shifted"))
        sb_ready, s_masked, bias_done, sarg_done, exp_done, p_transposed, pt0_done, pt1_done, pv_ready = (
            sem(n) for n in ("sb_ready", "s_masked", "bias_done", "sarg_done", "exp_done", "p_transposed", "pt0_done",
                             "pt1_done", "pv_ready"))
        ag_tanh, ag_done, den_done, rden_done, pv_scaled, ya_done, ya_transposed, ya_hi, ya_lo = (
            sem(n) for n in ("ag_tanh", "ag_done", "den_done", "rden_done", "pv_scaled", "ya_done", "ya_transposed",
                             "ya_hi", "ya_lo"))
        yr_hi, yr_split, yr_used, o0_ready, o1_ready, o0_read, o1_read, x0_added, x1_added = (
            sem(n) for n in ("yr_hi", "yr_split", "yr_used", "o0_ready", "o1_ready", "o0_read", "o1_read", "x0_added",
                             "x1_added"))
        fsq0_done, fsq_done, fsum_done, fmean_done, frstd_done, fin_done = (
            sem(n) for n in ("fsq0_done", "fsq_done", "fsum_done", "fmean_done", "frstd_done", "fin_done"))
        block = ctx.enter_context(nc.Block())

        def wait(eng, s, value):
            if not (isinstance(value, int) and value <= 0):
                eng.wait_ge(s, value)

        def heads(ap, n=RH):
            return ap.rearrange("p (h d) -> p h d", h=n)

        w_in_k = w_in.rearrange("(k p) n -> p k n", p=P)
        w_out_k = w_out.rearrange("(k p) n -> p k n", p=P)
        w_ada_k = w_ada.rearrange("(p k) n -> p k n", k=KC)
        pieces = [("ada", w_ada_k[:, k, 0:2 * D]) for k in range(KC)]
        pieces += [("w", w_in_k[:, 4 * s:4 * s + 4, off:off + COLS], g, 4 * s)
                   for g, off in enumerate((OFF_RQ, OFF_RK, OFF_RV, OFF_RG)) for s in range(2)]
        pieces += [("gate", w_ada_k[:, 2 * s:2 * s + 2, 2 * D:3 * D]) for s in range(4)]
        N_EARLY = len(pieces)
        pieces += [("kv", w_in_k[:, :, OFF_KV:OFF_KV + KV])]
        pieces += [("w", w_in_k[:, 4 * s:4 * s + 4, off:off + COLS], g, 4 * s)
                   for g, off in ((0, OFF_AQ), (1, OFF_AG)) for s in range(2)]
        pieces += [("w", w_out_k[:, 4 * s:4 * s + 4, off:off + COLS], g, 4 * s)
                   for g, off in ((2, 0), (3, COLS)) for s in range(2)]
        slot_of, turn_of, turns = [], [], [0] * 4
        for n in range(len(pieces)):
            s = n % 4 if n < N_EARLY else n % 2
            slot_of.append(s)
            turns[s] += 1
            turn_of.append(turns[s])
        split_pieces = [n for n, p in enumerate(pieces) if p[0] in ("w", "kv")]
        split_no = {n: i for i, n in enumerate(split_pieces)}
        ada_no = {n: i for i, n in enumerate(n for n, p in enumerate(pieces) if p[0] in ("ada", "gate"))}

        def stage_view(n):
            ap = stages[slot_of[n]]
            if pieces[n][0] == "ada":
                return ap
            width = {"w": COLS, "gate": D, "kv": KV}[pieces[n][0]]
            return ap.rearrange("p (k n) -> p k n", n=width)

        def wait_piece_used(eng, n):
            if n in split_no:
                eng.wait_ge(w_lo_done, split_no[n] + 1)
            else:
                eng.wait_ge(ada_used, ada_no[n] + 1)

        def load_piece(eng, n):
            before = [m for m in range(n) if slot_of[m] == slot_of[n]]
            if before:
                wait_piece_used(eng, before[-1])
            eng.dma_start(stage_view(n), pieces[n][1]).then_inc(stage_loaded[slot_of[n]], 16)

        def arrived(eng, n):
            eng.wait_ge(stage_loaded[slot_of[n]], 16 * turn_of[n])

        def part_of(n, low):
            if pieces[n][0] == "kv":
                return (wkvl if low else wkvh)[:, :, :]
            g, k = pieces[n][2:]
            return (wl if low else wh)[:, g, k:k + 4, :]

        def free_of_phase_a(eng, n):
            if n > N_EARLY:
                eng.wait_ge(za_ready, 4 * SAMPLE + pieces[n][2] + 1)

        def split_hi(act, n):
            arrived(act, n)
            free_of_phase_a(act, n)
            nc.scalar.activation(part_of(n, False), stage_view(n), ACT.Copy).then_inc(w_hi_done, 1)

        def split_lo(dve, n):
            dve.wait_ge(w_hi_done, split_no[n] + 1)
            nc.vector.tensor_tensor(part_of(n, True), stage_view(n), part_of(n, False).bitcast(F32),
                                    ALU.subtract).then_inc(w_lo_done, 1)

        FIRST_W, FIRST_GATE = KC, KC + 8

        def phase_tiles(eng, slot, last):
            slot(0, 0)
            slot(0, 1)
            with eng.Fori(1, NT // 2 - 1) as i:
                slot(i, 0)
                slot(i, 1)
            for t in range(NT - 2, last + 1):
                slot(t // 2, t % 2)

        def key_rows(rows, e):
            return rows[:, 0:2 * P].rearrange("p (g e d) -> p g e d", g=2, e=2)[:, :, e, :]

        def cached(rows, half, newer):
            at = slice(HALF * half, HALF * (half + 1))
            of = slice(HALF * newer, HALF * (newer + 1))
            keys = cache_k[of, :].rearrange("p (g d) -> p g d", g=2)
            return [(key_rows(rows, e)[at], keys) for e in range(2)] + [(rows[at, 2 * P:3 * P], cache_v[of, :])]

        def static(i):
            return isinstance(i, int)

        @block.sync
        def _(sp):
            for c, src in enumerate((c_prompt, c_sample)):
                sp.dma_start(c_in[:, c, :], src.rearrange("b (p k) -> (b p) k", k=KC)).then_inc(c_loaded, 16)
            sp.dma_start(ident[:, :], ident_tab).then_inc(c_loaded, 16)
            sp.dma_start(xt0[:, :], x_prompt[0:P, :]).then_inc(x_loaded, 16)
            for n in range(4):
                load_piece(sp, n)
            with nc.allow_non_contiguous_dma(reason="a few short columns"):
                sp.dma_start(g_col, norm_g.rearrange("a (k p) -> (a p) k", p=P)).then_inc(mod_loaded, 16)
                sp.dma_start(b_col, b_ada[:, 0:2 * D].rearrange("a (k p) -> (a p) k", p=P)).then_inc(mod_loaded, 16)
            for n in range(4, FIRST_W + 2):
                load_piece(sp, n)
            sp.dma_start(rope[:, :], rope_tab[0]).then_inc(rope_loaded, 16)
            sp.dma_start(decay[:, :], decay_tab).then_inc(tab_loaded, 16)
            sp.dma_start(qdec[:, :], qdec_tab.partition_broadcast(P)).then_inc(tab_loaded, 16)
            sp.dma_start(vdec, vdec_tab).then_inc(tab_loaded, 16)
            for n in range(FIRST_W + 2, FIRST_W + 4):
                load_piece(sp, n)
            sp.wait_ge(xn_done, 1)
            sp.dma_start(xt0[:, :], x_prompt[P:2 * P, :]).then_inc(x_loaded, 16)
            for n in range(FIRST_W + 4, FIRST_GATE):
                load_piece(sp, n)
            sp.dma_start(heads(state_s[:, :]), state_ret.rearrange("h k v -> k h v")).then_inc(state_loaded, 16)
            sp.wait_ge(h_done, 1)
            sp.dma_start(h_dram[0], hf[:, :, :].rearrange("p k r -> p (k r)")).then_inc(h_stored, 16)

            def slot(i, u):
                t = 2 * i + u
                if not static(i) or t + 2 <= SAMPLE:
                    wait(sp, xn_done, t + 2)
                    if static(i) and t + 2 == SAMPLE:
                        sp.wait_ge(b_set, 1)
                        sp.dma_start(xt0[HALF:P, :], x_sample).then_inc(x_loaded, 16)
                    else:
                        sp.dma_start(xt0[:, :], x_prompt[bass.ts(t + 2, P), :]).then_inc(x_loaded, 16)
                if not static(i) or t + 1 <= SAMPLE:
                    wait(sp, h_done, t + 2)
                    sp.dma_start(h_dram[t + 1], hf[:, :, :].rearrange("p k r -> p (k r)")).then_inc(h_stored, 16)
                    wait(sp, zk_read, t + 1)
                    sp.dma_start(rope[:, :], rope_tab[t + 1]).then_inc(rope_loaded, 16)
                if not static(i) or t >= 1:
                    wait(sp, yrt_done, t)
                    sp.dma_start(yr_dram[t - 1], yr_t[:, :]).then_inc(yr_stored, 16)
                if static(i) and t == 0:
                    for n in range(FIRST_GATE, N_EARLY):
                        load_piece(sp, n)
                    for j in range(2):
                        sp.dma_start(bias_rows[32 * j:32 * j + 2, :],
                                     b_ada[:, 2 * D + j * COLS:2 * D + (j + 1) * COLS].partition_broadcast(2)
                                     ).then_inc(b_rows_loaded, 16)
                if static(i) and t == 1:
                    sp.wait_ge(gate_rows, 1)
                    for j in range(2):
                        sp.dma_start(gate_dram[:, j * COLS:(j + 1) * COLS], bias_rows[32 * j:32 * j + 2, :]
                                     ).then_inc(gate_stored, 16)
                    for n in range(N_EARLY, N_EARLY + 2):
                        load_piece(sp, n)
                if static(i) and t == SAMPLE:
                    sp.wait_ge(state_done, NT)
                    sp.dma_start(ret_prompt.rearrange("h k v -> k h v"), heads(state[:, :])).then_inc(state_out, 16)

            phase_tiles(sp, slot, SAMPLE + 1)
            sp.wait_ge(state_done, NT + 1)
            sp.dma_start(ret_sample.rearrange("h k v -> k h v"), heads(state_s[:, :])).then_inc(state_out, 16)

            sp.wait_ge(h_stored, 16 * (SAMPLE + 1))
            sp.wait_ge(lo_done, SAMPLE + 1)
            sp.dma_start(hf[:, :, :].rearrange("p k r -> p (k r)"), h_dram[0]).then_inc(hb_loaded, 16)
            for n in range(N_EARLY + 2, N_EARLY + 5):
                load_piece(sp, n)
            sp.wait_ge(yr_stored, 16 * (SAMPLE + 1))
            sp.wait_ge(gate_stored, 32)
            sp.wait_ge(state_out, 32)
            sp.wait_ge(yr_done, SAMPLE + 1)
            sp.dma_start(mask[:, :, :], mask_tab).then_inc(fixed_loaded, 16)
            sp.dma_start(neg_sink, sink.partition_broadcast(P)).then_inc(fixed_loaded, 16)
            sp.dma_start(gate_p[:, :], gate_dram[0:1, :].partition_broadcast(P)).then_inc(fixed_loaded, 16)
            sp.dma_start(fin_g[:, :], final_g.partition_broadcast(P)).then_inc(fixed_loaded, 16)
            for n in range(N_EARLY + 5, len(pieces)):
                load_piece(sp, n)
            for half in range(2):
                for dst, src in cached(kv_cache, half, 0):
                    sp.dma_start(dst, src).then_inc(cache_loaded, 16)
            sp.wait_ge(w_lo_done, len(split_pieces))
            sp.dma_start(gate_s[:, :], gate_dram[1:2, :].partition_broadcast(P)).then_inc(fixed_loaded, 16)

            def slot_b(i, u):
                t = 2 * i + u
                front = not static(i) or t <= SAMPLE
                if not static(i) or t >= 2:
                    wait(sp, fin_done, t - 1)
                    if static(i) and t - 2 == SAMPLE:
                        sp.dma_start(y_sample, xts[u][HALF:P, :]).then_inc(y_stored[u], 16)
                    else:
                        sp.dma_start(y_prompt[bass.ts(t - 2, P), :], xts[u][:, :]).then_inc(y_stored[u], 16)
                if front:
                    wait(sp, y_stored[u], 16 * i)
                    if static(i) and t == SAMPLE:
                        wait(sp, pv_ready, 2 * (t - 1))
                        wait(sp, v_shifted, t - 1)
                        for dst, src in cached(kv_rows[u], 0, 1):
                            sp.dma_start(dst, src).then_inc(newer_loaded, 16)
                        sp.wait_ge(b_set, 3)
                        sp.dma_start(xts[u][HALF:P, :], x_sample).then_inc(xb_loaded[u], 16)
                    else:
                        sp.dma_start(xts[u][:, :], x_prompt[bass.ts(t, P), :]).then_inc(xb_loaded[u], 16)
                    wait(sp, yr_split, t)
                    sp.dma_start(yr_in[:, :, :].rearrange("p k r -> p (k r)"), yr_dram[t]).then_inc(yr_loaded, 16)
                if not static(i) or t + 1 <= SAMPLE:
                    wait(sp, b_split, t + 1)
                    sp.dma_start(hf[:, :, :].rearrange("p k r -> p (k r)"), h_dram[t + 1]).then_inc(hb_loaded, 16)
                if static(i) and t in (NT - 1, SAMPLE):
                    sp.wait_ge(kv_done, t + 1)
                    if t == SAMPLE:
                        sp.wait_ge(newer_loaded, 3 * 16)
                    k_new, v_new = (k_prompt, v_prompt) if t == NT - 1 else (k_sample, v_sample)
                    sp.dma_start(k_new.rearrange("p (g d) -> p g d", g=2), key_rows(kv_rows[u], 0)).then_inc(kv_out, 16)
                    sp.dma_start(v_new, kv_rows[u][:, 2 * P:3 * P]).then_inc(kv_out, 16)

            phase_tiles(sp, slot_b, SAMPLE + 2)
            sp.wait_ge(kv_out, 64)
            sp.wait_ge(y_stored[0], 16 * (NT // 2 + 1))
            sp.wait_ge(y_stored[1], 16 * (NT // 2))
            sp.wait_ge(state_out, 32)

        @block.gpsimd
        def _(pool):
            nc.gpsimd.memset(neg_half, -0.5)
            nc.gpsimd.memset(norm_eps, NORM_EPS)
            nc.gpsimd.memset(gn_eps, GN_EPS)
            nc.gpsimd.memset(zero, 0.0).then_inc(const_set, 1)
            nc.gpsimd.memset(state[:, :], 0.0).then_inc(const_set, 1)

            def prep(i, u):
                t = 2 * i + u
                wait(pool, ssq_done, t + 1)
                nc.gpsimd.tensor_tensor(meansq, ssq[:, 0:1], norm_eps, ALU.add).then_inc(rstd_mean, 1)
                wait(pool, rstd_mean, t + 1)
                wait(pool, xn_done, t)
                nc.gpsimd.tensor_tensor(rstd, meansq, neg_half[:, 0:1], ALU.pow).then_inc(rstd_done, 1)

            def slot(i, u):
                t = 2 * i + u
                if not static(i) or t + 1 <= SAMPLE:
                    prep(i + (u + 1) // 2, (u + 1) % 2)
                if not static(i) or t >= 1:
                    wait(pool, gn_mv_done, t)
                    wait(pool, gn_done, t - 1)
                    nc.gpsimd.tensor_tensor(gn_var, gn_mv[:, :, 1], gn_eps, ALU.add).then_inc(gn_var_done, 1)
                    wait(pool, gn_var_done, t)
                    nc.gpsimd.tensor_tensor(gn_rstd, gn_var, neg_half[:, 0:4], ALU.pow).then_inc(gn_rstd_done, 1)
                if static(i) and t == NT - 2:
                    pool.wait_ge(xn_done, NT)
                    nc.gpsimd.memset(xt0[0:HALF, :], 0.0).then_inc(b_set, 1)

            pool.wait_ge(const_set, 2)
            prep(0, 0)
            phase_tiles(pool, slot, SAMPLE + 1)

            pool.wait_ge(yr_stored, 16 * (SAMPLE + 1))
            pool.wait_ge(yr_done, SAMPLE + 1)
            pool.wait_ge(state_out, 32)
            nc.gpsimd.memset(ak_t[:, :, 0:P], 0.0)
            nc.gpsimd.memset(v_prev[:, :], 0.0).then_inc(b_set, 1)

            def slot_b(i, u):
                t = 2 * i + u
                front = not static(i) or t <= SAMPLE
                back = not static(i) or 1 <= t <= SAMPLE + 1
                if front and (not static(i) or 1 <= t < SAMPLE):
                    wait(pool, sb_ready, 2 * t)
                    wait(pool, akt_done, t)
                    nc.gpsimd.tensor_tensor(ak_t[:, :, 0:P], ak_t[:, :, P:2 * P],
                                            zero.unsqueeze(1).to_broadcast([P, 2, P]), ALU.add).then_inc(k_shifted, 1)
                if front and (not static(i) or t >= 1):
                    wait(pool, pv_ready, 2 * t)
                    if static(i) and t == SAMPLE:
                        pool.wait_ge(cache_loaded, 6 * 16)
                        nc.gpsimd.tensor_copy(v_prev[:, :], kv_cache[:, 2 * P:3 * P]).then_inc(v_shifted, 1)
                    else:
                        nc.gpsimd.tensor_tensor(v_prev[:, :], kv_rows[1 - u][:, 2 * P:3 * P], zero.to_broadcast([P, P]),
                                                ALU.add).then_inc(v_shifted, 1)
                if static(i) and t == SAMPLE:
                    pool.wait_ge(y_stored[0], 16 * (NT // 2))
                    nc.gpsimd.memset(xt0[0:HALF, :], 0.0).then_inc(b_set, 1)
                if back:
                    xr = xts[1 - u]
                    wait(pool, xb_loaded[1 - u], 16 * (i + u))
                    wait(pool, o0_read, t)
                    nc.gpsimd.tensor_tensor(xr[:, 0:COLS], xr[:, 0:COLS], o_part[:, :], ALU.add).then_inc(x0_added, 1)
                    wait(pool, o1_read, t)
                    nc.gpsimd.tensor_tensor(xr[:, COLS:D], xr[:, COLS:D], o_part1[:, :], ALU.add).then_inc(x1_added, 1)
                    wait(pool, fsq_done, t)
                    wait(pool, fin_done, t - 1)
                    nc.gpsimd.tensor_tensor(meansq, ssq[:, 0:1], ssq[:, 1:2], ALU.add).then_inc(fsum_done, 1)
                    wait(pool, fsum_done, t)
                    nc.gpsimd.tensor_tensor(meansq, meansq, norm_eps, ALU.add).then_inc(fmean_done, 1)
                    wait(pool, fmean_done, t)
                    nc.gpsimd.tensor_tensor(rstd, meansq, neg_half[:, 0:1], ALU.pow).then_inc(frstd_done, 1)

            phase_tiles(pool, slot_b, SAMPLE + 2)

        @block.scalar
        def _(act):
            act.wait_ge(c_loaded, 48)
            nc.scalar.activation(c_th, c_in, ACT.Tanh, scale=0.5).then_inc(c_tanh, 1)

            def square(i, u):
                t = 2 * i + u
                wait(act, x_loaded, 16 * (t + 1))
                wait(act, x_transposed, t)
                wait(act, rstd_mean, t)
                nc.scalar.activation(xn[:, :], xt0[:, :], ACT.Square, scale=D ** -0.5, accum_out=ssq[:, 0:1]).then_inc(ssq_done, 1)

            def modulate(i, u, sample=False):
                t = 2 * i + u
                wait(act, x_transposed, t + 1)
                wait(act, h_stored, 16 * t)
                wait(act, lo_done, t)
                c, lo = (1, HALF) if sample else (0, 0)
                if sample:
                    for b, src in enumerate((xb0, xb1)):
                        nc.scalar.activation(hf[:, 4 * b:4 * b + 4, 0:HALF], heads(src[:, :])[:, :, 0:HALF], ACT.Copy)
                for k in range(KC):
                    src = (xb0 if k < 4 else xb1)[:, (k % 4) * P + lo:(k % 4 + 1) * P]
                    last = nc.scalar.activation(hf[:, k, lo:P], src, ACT.Identity, bias=h_shift[:, k, c:c + 1],
                                                scale=h_scale[:, k, c:c + 1])
                last.then_inc(h_done, 1)

            def slot(i, u):
                t = 2 * i + u
                front = not static(i) or t <= SAMPLE
                back = not static(i) or t >= 1
                nxt = (i + (u + 1) // 2, (u + 1) % 2)
                if not static(i) or t + 1 <= SAMPLE:
                    square(*nxt)
                    modulate(*nxt, sample=static(i) and t + 1 == SAMPLE)
                if static(i) and t == 0:
                    for n in range(FIRST_W + 6, FIRST_GATE):
                        split_hi(act, n)
                if front:
                    wait(act, vdec_done, t + 1)
                    wait(act, out_ready, t)
                    nc.scalar.activation(v_row[:, :], za0[:, :], ACT.Copy).then_inc(v_done, 1)
                if back:
                    wait(act, yr_transposed, t)
                    wait(act, yr_stored, 16 * (t - 1))
                    nc.scalar.activation(yr_t[:, :], ky_b[:, :], ACT.Copy).then_inc(yrt_done, 1)
                if front:
                    wait(act, k_transposed, t + 1)
                    wait(act, s_ready, t)
                    nc.scalar.activation(k_t[:, :], ky_b[:, :], ACT.Copy).then_inc(kt_done, 1)
                    wait(act, za_ready, 4 * t + 4)
                    wait(act, yr_done, t)
                    nc.scalar.activation(r_gate[:, :], za1[:, :], ACT.Tanh, scale=0.5).then_inc(rg_tanh, 1)

            square(0, 0)
            act.wait_ge(mod_ready, 1)
            modulate(0, 0)
            for n in range(FIRST_W, FIRST_W + 6):
                split_hi(act, n)
            phase_tiles(act, slot, SAMPLE + 1)

            for n in range(N_EARLY, N_EARLY + 5):
                split_hi(act, n)
            act.wait_ge(b_set, 2)

            def softmax(i, u, half):
                t = 2 * i + u
                n = 2 * t + half + 1
                wait(act, bias_done, n)
                for j in range(4):
                    h = 4 * half + j
                    nc.scalar.activation(s_row[:, j, :], s_row[:, j, :], ACT.Exp, bias=s_bias[:, h:h + 1],
                                         scale=SCORE_SCALE, accum_out=row_sum[:, h:h + 1])
                wait(act, sarg_done, n)
                nc.scalar.activation(sink_exp[:, 4 * half:4 * half + 4], sink_arg[:, 4 * half:4 * half + 4],
                                     ACT.Exp).then_inc(exp_done, 1)

            def p_out(i, u, half):
                t = 2 * i + u
                wait(act, p_transposed, 2 * t + half + 1)
                wait(act, pv_ready, 2 * t + half)
                nc.scalar.activation(p_t[:, 0:4, :].rearrange("p b r -> p (b r)"), t0_b[:, :], ACT.Copy).then_inc(pt0_done, 1)

            def slot_b(i, u):
                t = 2 * i + u
                front = not static(i) or t <= SAMPLE
                back = not static(i) or 1 <= t <= SAMPLE + 1
                prev = (i + (u - 1) // 2, (u + 1) % 2)
                if front:
                    wait(act, zb_ready, 3 * t + 1)
                    wait(act, pv_ready, 2 * (t - 1))
                    wait(act, v_shifted, t - 1)
                    lo = HALF if static(i) and t == SAMPLE else 0
                    keys = zb0[lo:P, 0:P].rearrange("p (g d) -> p g d", g=2).unsqueeze(2).to_broadcast([P - lo, 2, 2, HD])
                    nc.scalar.activation(kv_rows[u][lo:P, 0:2 * P].rearrange("p (g e d) -> p g e d", g=2, e=2), keys, ACT.Copy)
                    nc.scalar.activation(kv_rows[u][lo:P, 2 * P:3 * P], zb0[lo:P, P:2 * P], ACT.Copy).then_inc(kv_done, 1)
                if back:
                    softmax(*prev, 0)
                if front:
                    wait(act, zb_ready, 3 * t + 2)
                    wait(act, qk_transposed, t)
                    nc.scalar.activation(aq_row[:, :], zb1[:, :], ACT.Copy).then_inc(aq_done, 1)
                if static(i) and t == 0:
                    for n in range(N_EARLY + 5, len(pieces)):
                        split_hi(act, n)
                if back:
                    p_out(*prev, 0)
                    softmax(*prev, 1)
                if front:
                    wait(act, zb_ready, 3 * t + 3)
                    wait(act, ya_done, t - 1)
                    nc.scalar.activation(a_gates[u][:, :], zb2[:, :], ACT.Tanh, scale=0.5).then_inc(ag_tanh, 1)
                if back:
                    p_out(*prev, 1)
                    wait(act, ya_transposed, t)
                    wait(act, o1_ready, t - 1)
                    nc.scalar.activation(yh[:, 4:8, :].rearrange("p k r -> p (k r)"), s0_b[:, :], ACT.Copy).then_inc(ya_hi, 1)
                if front:
                    wait(act, qk_transposed, t + 1)
                    wait(act, sb_ready, 2 * t)
                    nc.scalar.activation(aq_t[:, :, :].rearrange("p k r -> p (k r)"), t0_b[:, :], ACT.Copy).then_inc(aqt_done, 1)
                    if static(i) and t == SAMPLE:
                        nc.scalar.activation(ak_t[:, :, 0:P], t1_b[:, 2 * P:4 * P].rearrange("p (g r) -> p g r", g=2), ACT.Copy)
                    else:
                        wait(act, k_shifted, t)
                    nc.scalar.activation(ak_t[:, :, P:2 * P], t1_b[:, 0:2 * P].rearrange("p (g r) -> p g r", g=2),
                                         ACT.Copy).then_inc(akt_done, 1)
                if back:
                    xr = xts[1 - u]
                    wait(act, x0_added, t)
                    wait(act, ag_done, t + 1 if front else t)
                    wait(act, fsum_done, t - 1)
                    nc.scalar.activation(zb2[:, :], xr[:, 0:COLS], ACT.Square, scale=D ** -0.5, accum_out=ssq[:, 0:1]).then_inc(fsq0_done, 1)
                    wait(act, x1_added, t)
                    wait(act, fsq0_done, t)
                    nc.scalar.activation(zb2[:, :], xr[:, COLS:D], ACT.Square, scale=D ** -0.5, accum_out=ssq[:, 1:2]).then_inc(fsq_done, 1)

            phase_tiles(act, slot_b, SAMPLE + 1)

        @block.vector
        def _(dve):
            V = nc.vector
            dve.wait_ge(c_tanh, 1)
            cT = c_in.rearrange("p c k -> p k c")
            tT = c_th.rearrange("p c k -> p k c")
            V.scalar_tensor_tensor(c_silu, tT, 1.0, cT, ALU.add, ALU.mult).then_inc(c_ready, 1)
            dve.wait_ge(c_ready, 1)
            V.tensor_scalar(c_silu, c_silu, 0.5, None, ALU.mult).then_inc(c_ready, 1)
            V.memset(mod_rows[:, :], 0.0).then_inc(c_ready, 1)

            def normalise(i, u):
                t = 2 * i + u
                wait(dve, rstd_done, t + 1)
                V.tensor_scalar(xn[:, :], xt0[:, :], rstd, None, ALU.mult).then_inc(xn_done, 1)

            def split_h(i, u):
                t = 2 * i + u
                wait(dve, h_done, t + 1)
                wait(dve, za_ready, 4 * (t - 1))
                V.tensor_copy(hhs[u][:, :, :], hf[:, :, :]).then_inc(hi_done, 1)
                wait(dve, hi_done, t + 1)
                V.tensor_tensor(hls[u][:, :, :], hf[:, :, :], hhs[u][:, :, :].bitcast(F32), ALU.subtract).then_inc(lo_done, 1)

            def rotate(t, z, row, zread, mul, done):
                z4 = z[:, :].rearrange("p (h e d) -> p h e d", h=RH, e=2)
                sin = rope[:, 64:192].rearrange("p (e d) -> p e d", e=2).unsqueeze(1).to_broadcast([P, RH, 2, 64])
                cos = rope[:, 0:64].unsqueeze(1).to_broadcast([P, 2 * RH, 64])
                V.tensor_tensor(swap[:, :].rearrange("p (h e d) -> p h e d", h=RH, e=2), z4[:, :, ::-1, :], sin,
                                ALU.mult).then_inc(mul, 1)
                V.tensor_tensor(heads(row[:, :], 8), heads(z[:, :], 8), cos, ALU.mult).then_inc(zread, 1)
                wait(dve, mul, t + 1)
                wait(dve, zread, t + 1)
                V.tensor_tensor(row[:, :], row[:, :], swap[:, :], ALU.add).then_inc(done, 1)

            def slot(i, u):
                t = 2 * i + u
                front = not static(i) or t <= SAMPLE
                back = not static(i) or t >= 1
                nxt = (i + (u + 1) // 2, (u + 1) % 2)
                more = not static(i) or t + 1 <= SAMPLE
                if more:
                    normalise(*nxt)
                if front:
                    wait(dve, za_ready, 4 * t + 1)
                    wait(dve, rope_loaded, 16 * (t + 1))
                    wait(dve, q_transposed, t)
                    wait(dve, k_done, t)
                    rotate(t, za0, q_row, zq_read, q_mul, q_done)
                if static(i) and t == 0:
                    for n in range(FIRST_W + 4, FIRST_W + 6):
                        split_lo(dve, n)
                if back:
                    wait(dve, out_ready, t)
                    wait(dve, gn_mv_done, t - 1)
                    for h in range(RH):
                        last = V.bn_stats(gn_stats[:, h, :], out_b[:, h * DK:(h + 1) * DK])
                    last.then_inc(gn_stat_done, 1)
                    wait(dve, gn_stat_done, t)
                    wait(dve, gn_var_done, t - 1)
                    wait(dve, upd_ready, t)
                    st = state_s if static(i) and t - 1 == SAMPLE else state
                    for h in range(RH):
                        cols = slice(h * DK, (h + 1) * DK)
                        last = V.scalar_tensor_tensor(st[:, cols], st[:, cols], GAMMA[h] ** P, upd_b[:, cols], ALU.mult, ALU.add)
                    last.then_inc(state_done, 1)
                    for h in range(RH):
                        last = V.bn_aggr(gn_mv[:, h, :], gn_stats[:, h, :])
                    last.then_inc(gn_mv_done, 1)
                    wait(dve, gn_rstd_done, t)
                    wait(dve, yr_transposed, t - 1)
                    for h in range(RH):
                        cols = slice(h * DK, (h + 1) * DK)
                        last = V.tensor_scalar(r_out[:, cols], out_b[:, cols], gn_mv[:, h, 0:1], gn_rstd[:, h:h + 1],
                                               ALU.subtract, ALU.mult)
                    last.then_inc(gn_done, 1)
                    wait(dve, gn_done, t)
                    wait(dve, rg_done, t)
                    V.scalar_tensor_tensor(r_out[:, :], r_out[:, :], 0.5, r_gate[:, :], ALU.mult, ALU.mult).then_inc(yr_done, 1)
                if more:
                    split_h(*nxt)
                if front:
                    wait(dve, za_ready, 4 * t + 2)
                    wait(dve, upd_ready, t)
                    wait(dve, q_done, t + 1)
                    rotate(t, za1, k_row, zk_read, k_mul, k_done)
                    if static(i) and t == 0:
                        dve.wait_ge(tab_loaded, 48)
                    wait(dve, q_transposed, t + 1)
                    wait(dve, out_ready, t)
                    V.tensor_tensor(q_t[:, :], qs_b[:, :], qdec[:, :], ALU.mult).then_inc(qt_done, 1)
                if static(i) and t == 0:
                    for n in range(FIRST_W + 6, FIRST_GATE):
                        split_lo(dve, n)
                    dve.wait_ge(state_loaded, 16)
                    for h in range(RH):
                        V.tensor_scalar(state_s[:, h * DK:(h + 1) * DK], state_s[:, h * DK:(h + 1) * DK],
                                        GAMMA[h] ** -HALF, None, ALU.mult)
                if front:
                    wait(dve, za_ready, 4 * t + 3)
                    V.tensor_tensor(heads(v_dec[:, :]), heads(za0[:, :]), vdec.unsqueeze(2).to_broadcast([P, RH, DK]),
                                    ALU.mult).then_inc(vdec_done, 1)
                    wait(dve, rg_tanh, t + 1)
                    V.scalar_tensor_tensor(r_gate[:, :], r_gate[:, :], 1.0, za1[:, :], ALU.add, ALU.mult).then_inc(rg_done, 1)
                    wait(dve, s_ready, t + 1)
                    wait(dve, out_ready, t)
                    V.tensor_tensor(s_t[:, :], qs_b[:, :], decay[:, :], ALU.mult).then_inc(st_done, 1)
                if static(i) and t == 1:
                    dve.wait_ge(ada_used, KC + 4)
                    dve.wait_ge(b_rows_loaded, 32)
                    for j in range(2):
                        rows = slice(32 * j, 32 * j + 2)
                        last = V.tensor_tensor(bias_rows[rows, :], upd_b[rows, :], bias_rows[rows, :], ALU.add)
                    last.then_inc(gate_rows, 1)

            normalise(0, 0)
            dve.wait_ge(ada_used, KC)
            dve.wait_ge(c_ready, 3)
            for j in range(4):
                last = V.tensor_copy(mod_rows[32 * j:32 * j + 2, :], out_b[32 * j:32 * j + 2, :])
            last.then_inc(mod_rows_out, 1)
            dve.wait_ge(mod_transposed, 1)
            dve.wait_ge(mod_loaded, 32)
            turned = upd_b[:, :].rearrange("p (b r) -> p b r", b=4)
            for j in range(4):
                dst = (h_shift if j < 2 else h_scale)[:, 4 * (j % 2):4 * (j % 2) + 4, :]
                bias = b_col[:, 4 * j:4 * j + 4].unsqueeze(2).to_broadcast([P, 4, 2])
                last = V.tensor_tensor(dst, turned[:, :, 32 * j:32 * j + 2], bias, ALU.add)
            last.then_inc(mod_rows_out, 1)
            dve.wait_ge(mod_rows_out, 2)
            V.scalar_tensor_tensor(h_scale, h_scale, 1.0, g_col.unsqueeze(2).to_broadcast([P, KC, 2]), ALU.add,
                                   ALU.mult).then_inc(mod_ready, 1)
            split_h(0, 0)
            for n in range(FIRST_W, FIRST_W + 4):
                split_lo(dve, n)
            phase_tiles(dve, slot, SAMPLE + 1)

            def split_hb(i, u):
                t = 2 * i + u
                wait(dve, hb_loaded, 16 * (t + 1))
                wait(dve, zb_ready, 3 * t)
                V.tensor_copy(hh0[:, :, :], hf[:, :, :]).then_inc(bh_hi, 1)
                wait(dve, bh_hi, t + 1)
                V.tensor_tensor(hl0[:, :, :], hf[:, :, :], hh0[:, :, :].bitcast(F32), ALU.subtract).then_inc(b_split, 1)

            split_lo(dve, N_EARLY)
            split_hb(0, 0)
            for n in range(N_EARLY + 1, N_EARLY + 5):
                split_lo(dve, n)
            dve.wait_ge(b_set, 2)
            dve.wait_ge(fixed_loaded, 64)
            V.tensor_scalar(neg_sink, neg_sink, -1.0, None, ALU.mult).then_inc(const_set, 1)
            dve.wait_ge(const_set, 3)

            def mask_max(i, u, half):
                t = 2 * i + u
                n = 2 * t + half + 1
                wait(dve, p_transposed, n - 1)
                wait(dve, sb_ready, n)
                wait(dve, sarg_done, n - 1)
                m = mask[:, 1 if static(i) and t == 0 else 0, :]
                V.memset(spare, 0.0)
                for j in range(4):
                    h = 4 * half + j
                    src = (s1_b if j % 2 else s0_b)[:, (j // 2) * 256:(j // 2 + 1) * 256]
                    last = V.tensor_tensor_reduce(out=s_row[:, j, :], in0=src, in1=m, scale=1.0, scalar=MASKED,
                                                  op0=ALU.add, op1=ALU.max, accum_out=s_max[:, h:h + 1])
                last.then_inc(s_masked, 1)
                hs = slice(4 * half, 4 * half + 4)
                wait(dve, s_masked, n)
                wait(dve, exp_done, n - 2)
                V.scalar_tensor_tensor(s_bias[:, hs], s_max[:, hs], -SCORE_SCALE, neg_sink[:, hs], ALU.mult,
                                       ALU.min).then_inc(bias_done, 1)
                wait(dve, bias_done, n)
                V.tensor_tensor(sink_arg[:, hs], s_bias[:, hs], neg_sink[:, hs], ALU.subtract).then_inc(sarg_done, 1)

            def p_out(i, u, half):
                t = 2 * i + u
                wait(dve, p_transposed, 2 * t + half + 1)
                wait(dve, pv_ready, 2 * t + half)
                V.tensor_copy(p_t[:, 4:8, :].rearrange("p b r -> p (b r)"), t1_b[:, :]).then_inc(pt1_done, 1)

            def final(i, u):
                t = 2 * i + u
                wait(dve, frstd_done, t + 1)
                V.scalar_tensor_tensor(xts[u][:, :], xts[u][:, :], rstd, fin_g[:, :], ALU.mult, ALU.mult).then_inc(fin_done, 1)

            def slot_b(i, u):
                t = 2 * i + u
                front = not static(i) or t <= SAMPLE
                back = not static(i) or 1 <= t <= SAMPLE + 1
                prev = (i + (u - 1) // 2, (u + 1) % 2)
                nxt = (i + (u + 1) // 2, (u + 1) % 2)
                if back:
                    mask_max(*prev, 0)
                if not static(i) or t >= 2:
                    final(i - 1, u)
                if static(i) and t == 0:
                    for n in range(N_EARLY + 5, len(pieces)):
                        split_lo(dve, n)
                if back:
                    p_out(*prev, 0)
                    mask_max(*prev, 1)
                if front:
                    wait(dve, ag_tanh, t + 1)
                    V.scalar_tensor_tensor(a_gates[u][:, :], a_gates[u][:, :], 1.0, zb2[:, :], ALU.add,
                                           ALU.mult).then_inc(ag_done, 1)
                if back:
                    p_out(*prev, 1)
                    wait(dve, exp_done, 2 * t)
                    wait(dve, pv_scaled, t - 1)
                    V.tensor_tensor(den, row_sum, sink_exp, ALU.add).then_inc(den_done, 1)
                    wait(dve, den_done, t)
                    V.reciprocal(rden, den).then_inc(rden_done, 1)
                    wait(dve, rden_done, t)
                    wait(dve, pv_ready, 2 * t)
                    wait(dve, ya_transposed, t - 1)
                    V.tensor_tensor(heads(ya_row[:, :], QH), heads(pv_b[:, :], QH),
                                    rden.unsqueeze(2).to_broadcast([P, QH, HD]), ALU.mult).then_inc(pv_scaled, 1)
                    wait(dve, pv_scaled, t)
                    V.scalar_tensor_tensor(ya_row[:, :], ya_row[:, :], 0.5, a_gates[1 - u][:, :], ALU.mult,
                                           ALU.mult).then_inc(ya_done, 1)
                if not static(i) or t + 1 <= SAMPLE:
                    split_hb(*nxt)
                if back:
                    wait(dve, ya_hi, t)
                    V.tensor_tensor(yl[:, 4:8, :].rearrange("p k r -> p (k r)"), s0_b[:, :],
                                    yh[:, 4:8, :].rearrange("p k r -> p (k r)").bitcast(F32), ALU.subtract).then_inc(ya_lo, 1)
                if front:
                    wait(dve, yr_loaded, 16 * (t + 1))
                    wait(dve, yr_used, t)
                    V.tensor_copy(yh[:, 0:4, :], yr_in[:, :, :]).then_inc(yr_hi, 1)
                    wait(dve, yr_hi, t + 1)
                    V.tensor_tensor(yl[:, 0:4, :], yr_in[:, :, :], yh[:, 0:4, :].bitcast(F32), ALU.subtract).then_inc(yr_split, 1)
                if back:
                    if static(i) and t == SAMPLE + 1:
                        dve.wait_ge(fixed_loaded, 80)
                        gate = gate_s
                    else:
                        gate = gate_p
                    wait(dve, o0_ready, t)
                    wait(dve, x0_added, t - 1)
                    V.tensor_tensor(o_part[:, :], zb0[:, :], gate[:, 0:COLS], ALU.mult).then_inc(o0_read, 1)
                    wait(dve, o1_ready, t)
                    wait(dve, x1_added, t - 1)
                    V.tensor_tensor(o_part1[:, :], zb1[:, :], gate[:, COLS:D], ALU.mult).then_inc(o1_read, 1)

            phase_tiles(dve, slot_b, SAMPLE + 2)

        @block.tensor
        def _(pe):
            mm = nc.tensor.matmul

            def dense(out, xh, xl, weights, part=(0, 1, 2), chunks=range(KC), first=True, last=True):
                w_hi, w_lo = weights
                passes = [(xh, w_hi), (xh, w_lo), (xl, w_hi)]
                for n in part:
                    a, b = passes[n]
                    for k in chunks:
                        ins = mm(out, a[:, k, :], b[:, k, :], start=first and n == part[0] and k == chunks[0],
                                 stop=last and n == part[-1] and k == chunks[-1])
                return ins

            def group(g):
                return wh[:, g], wl[:, g]

            def transpose_x(i, u):
                t = 2 * i + u
                wait(pe, xn_done, t + 1)
                wait(pe, h_done, t)
                for k in range(KC):
                    last = nc.tensor.transpose((xb0 if k < 4 else xb1)[:, (k % 4) * P:(k % 4 + 1) * P],
                                               xn[:, k * P:(k + 1) * P], ident[:, :])
                last.then_inc(x_transposed, 1)

            pe.wait_ge(c_ready, 2)
            pe.wait_ge(c_loaded, 48)
            transpose_x(0, 0)
            for k in range(KC):
                arrived(pe, k)
                for j in range(4):
                    last = mm(out_b[32 * j:32 * j + 2, :], c_silu[:, k, :], stages[slot_of[k]][:, j * COLS:(j + 1) * COLS],
                              start=k == 0, stop=k == KC - 1, tile_position=(0, 32 * j))
                last.then_inc(ada_used, 1)
            pe.wait_ge(mod_rows_out, 1)
            for b in range(4):
                last = nc.tensor.transpose(upd_b[:, b * P:(b + 1) * P], mod_rows[:, b * P:(b + 1) * P], ident[:, :])
            last.then_inc(mod_transposed, 1)

            def slot(i, u):
                t = 2 * i + u
                front = not static(i) or t <= SAMPLE
                back = not static(i) or t >= 1
                h_hi, h_lo = hhs[u], hls[u]
                if front:
                    wait(pe, lo_done, t + 1)
                    wait(pe, v_done, t)
                    if static(i) and t == 0:
                        pe.wait_ge(w_lo_done, 2)
                    dense(za0[:, :], h_hi, h_lo, group(0)).then_inc(za_ready, 1)
                if back:
                    wait(pe, st_done, t)
                    wait(pe, state_done, t - 1)
                    wait(pe, gn_done, t - 1)
                    wait(pe, v_done, t)
                    st = state_s if static(i) and t - 1 == SAMPLE else state
                    for h in range(RH):
                        c = slice(h * DK, (h + 1) * DK)
                        mm(out_b[:, c], s_t[:, c], v_row[:, c], start=True, stop=False)
                        last = mm(out_b[:, c], q_t[:, c], st[:, c], start=False, stop=True)
                    last.then_inc(out_ready, 1)
                    for h in range(RH):
                        c = slice(h * DK, (h + 1) * DK)
                        last = mm(upd_b[:, c], k_row[:, c], v_dec[:, c], start=True, stop=True)
                    last.then_inc(upd_ready, 1)
                if not static(i) or t + 1 <= SAMPLE:
                    transpose_x(i + (u + 1) // 2, (u + 1) % 2)
                if front:
                    wait(pe, rg_done, t)
                    if static(i) and t == 0:
                        pe.wait_ge(w_lo_done, 4)
                    dense(za1[:, :], h_hi, h_lo, group(1)).then_inc(za_ready, 1)
                    wait(pe, q_done, t + 1)
                    wait(pe, st_done, t)
                    for h in range(RH):
                        c = slice(h * DK, (h + 1) * DK)
                        last = nc.tensor.transpose(qs_b[:, c], q_row[:, c], ident[:, :])
                    last.then_inc(q_transposed, 1)
                    wait(pe, zq_read, t + 1)
                    if static(i) and t == 0:
                        pe.wait_ge(w_lo_done, 6)
                    dense(za0[:, :], h_hi, h_lo, group(2)).then_inc(za_ready, 1)
                if back:
                    wait(pe, yr_done, t)
                    wait(pe, kt_done, t)
                    for h in range(RH):
                        c = slice(h * DK, (h + 1) * DK)
                        last = nc.tensor.transpose(ky_b[:, c], r_out[:, c], ident[:, :])
                    last.then_inc(yr_transposed, 1)
                if front:
                    wait(pe, zk_read, t + 1)
                    if static(i) and t == 0:
                        pe.wait_ge(w_lo_done, 8)
                    dense(za1[:, :], h_hi, h_lo, group(3), part=(0, 1), last=False)
                    wait(pe, k_done, t + 1)
                    wait(pe, yrt_done, t)
                    for h in range(RH):
                        c = slice(h * DK, (h + 1) * DK)
                        last = nc.tensor.transpose(ky_b[:, c], k_row[:, c], ident[:, :])
                    last.then_inc(k_transposed, 1)
                    dense(za1[:, :], h_hi, h_lo, group(3), part=(2,), first=False).then_inc(za_ready, 1)
                    wait(pe, qt_done, t + 1)
                    wait(pe, kt_done, t + 1)
                    for h in range(RH):
                        c = slice(h * DK, (h + 1) * DK)
                        last = mm(qs_b[:, c], k_t[:, c], q_t[:, c], start=True, stop=True)
                    last.then_inc(s_ready, 1)
                if static(i) and t == 1:
                    pe.wait_ge(state_done, 1)
                    for s in range(4):
                        n = FIRST_GATE + s
                        arrived(pe, n)
                        for kk in range(2):
                            for j in range(2):
                                last = mm(upd_b[32 * j:32 * j + 2, :], c_silu[:, 2 * s + kk, :],
                                          stage_view(n)[:, kk, j * COLS:(j + 1) * COLS], start=s == 0 and kk == 0,
                                          stop=s == 3 and kk == 1, tile_position=(0, 32 * j))
                        last.then_inc(ada_used, 1)
                    pe.wait_ge(gate_rows, 1)

            phase_tiles(pe, slot, SAMPLE + 1)

            def scores(i, u, half):
                t = 2 * i + u
                if half == 0:
                    wait(pe, aqt_done, t + 1)
                    wait(pe, akt_done, t + 1)
                    wait(pe, ya_lo, t)
                wait(pe, s_masked, 2 * t + half)
                for j in range(4):
                    h = 4 * half + j
                    rows = slice(HD * (h % 2), HD * (h % 2) + HD)
                    last = mm((s1_b if j % 2 else s0_b)[:, (j // 2) * 256:(j // 2 + 1) * 256], aq_t[rows, h // 2, :],
                              ak_t[rows, half, :], start=True, stop=True)
                last.then_inc(sb_ready, 1)

            def turn_p(i, u, half):
                t = 2 * i + u
                wait(pe, exp_done, 2 * t + half + 1)
                wait(pe, pt0_done, 2 * t + half)
                wait(pe, pt1_done, 2 * t + half)
                for j in range(4):
                    for s in range(2):
                        b = 2 * j + s
                        last = nc.tensor.transpose((t0_b if b < 4 else t1_b)[:, (b % 4) * P:(b % 4 + 1) * P],
                                                   s_row[:, j, s * P:(s + 1) * P], ident[:, :])
                last.then_inc(p_transposed, 1)

            def weigh(i, u, half):
                t = 2 * i + u
                wait(pe, pt0_done, 2 * t + half + 1)
                wait(pe, pt1_done, 2 * t + half + 1)
                if half == 0:
                    wait(pe, v_shifted, t)
                    wait(pe, pv_scaled, t)
                for j in range(4):
                    h = 4 * half + j
                    dst = pv_b[:, h * HD:(h + 1) * HD]
                    mm(dst, p_t[:, 2 * j, :], v_prev[:, half * HD:(half + 1) * HD], start=True, stop=False)
                    last = mm(dst, p_t[:, 2 * j + 1, :], kv_rows[u][:, 2 * P + half * HD:2 * P + (half + 1) * HD],
                              start=False, stop=True)
                last.then_inc(pv_ready, 1)

            def slot_b(i, u):
                t = 2 * i + u
                front = not static(i) or t <= SAMPLE
                back = not static(i) or t >= 1
                prev = (i + (u - 1) // 2, (u + 1) % 2)
                if front:
                    wait(pe, b_split, t + 1)
                    wait(pe, o0_read, t - 1)
                    if static(i) and t == 0:
                        pe.wait_ge(w_lo_done, 9)
                        pe.wait_ge(v_done, SAMPLE + 1)
                    dense(zb0[:, 0:KV], hh0, hl0, (wkvh, wkvl)).then_inc(zb_ready, 1)
                if back:
                    scores(*prev, 0)
                if front:
                    wait(pe, o1_read, t - 1)
                    if static(i) and t == 0:
                        pe.wait_ge(w_lo_done, 11)
                        pe.wait_ge(rg_done, SAMPLE + 1)
                    dense(zb1[:, :], hh0, hl0, group(0)).then_inc(zb_ready, 1)
                if back:
                    turn_p(*prev, 0)
                    scores(*prev, 1)
                if front:
                    wait(pe, ag_done, t)
                    wait(pe, fsq_done, t - 1)
                    if static(i) and t == 0:
                        pe.wait_ge(w_lo_done, 13)
                    dense(zb2[:, :], hh0, hl0, group(1), part=(0,), last=False)
                if back:
                    weigh(*prev, 0)
                if front:
                    dense(zb2[:, :], hh0, hl0, group(1), part=(1, 2), first=False).then_inc(zb_ready, 1)
                if back:
                    turn_p(*prev, 1)
                    wait(pe, yr_split, t)
                    wait(pe, kv_done, t + 1 if front else t)
                    if static(i) and t == 1:
                        pe.wait_ge(w_lo_done, len(split_pieces))
                    dense(zb0[:, :], yh, yl, group(2), chunks=range(4), last=False)
                    weigh(*prev, 1)
                    wait(pe, aq_done, t + 1 if front else t)
                    dense(zb1[:, :], yh, yl, group(3), chunks=range(4), last=False).then_inc(yr_used, 1)
                    wait(pe, ya_done, t)
                    wait(pe, s_masked, 2 * t)
                    for b in range(4):
                        last = nc.tensor.transpose(s0_b[:, b * P:(b + 1) * P], ya_row[:, b * P:(b + 1) * P], ident[:, :])
                    last.then_inc(ya_transposed, 1)
                if front:
                    wait(pe, aq_done, t + 1)
                    wait(pe, kv_done, t + 1)
                    wait(pe, pt0_done, 2 * t)
                    wait(pe, pt1_done, 2 * t)
                    for b in range(4):
                        nc.tensor.transpose(t0_b[:, b * P:(b + 1) * P], aq_row[:, b * P:(b + 1) * P], ident[:, :])
                    sources = [kv_rows[u]]
                    if static(i) and t == SAMPLE:
                        pe.wait_ge(cache_loaded, 6 * 16)
                        pe.wait_ge(newer_loaded, 3 * 16)
                        sources.append(kv_cache)
                    for s, src in enumerate(sources):
                        for g in range(2):
                            last = nc.tensor.transpose(t1_b[:, (2 * s + g) * P:(2 * s + g + 1) * P],
                                                       src[:, g * P:(g + 1) * P], ident[:, :])
                    last.then_inc(qk_transposed, 1)
                if back:
                    wait(pe, ya_lo, t)
                    dense(zb0[:, :], yh, yl, group(2), chunks=range(4, 8), first=False).then_inc(o0_ready, 1)
                    dense(zb1[:, :], yh, yl, group(3), chunks=range(4, 8), first=False).then_inc(o1_ready, 1)

            phase_tiles(pe, slot_b, SAMPLE + 1)


def tables():
    import numpy as np
    f = np.float32
    inv = f(1) / np.power(10000.0, (np.arange(0, DK, 2, dtype=f) / f(DK)).astype(np.float64)).astype(f)
    row = np.arange((NT + 1) * P).astype(f)
    row[SAMPLE * P + HALF:] = SEQ + np.arange(HALF)
    ang = (row[:, None] * inv[None, :]).astype(np.float64)
    cos, sin = np.cos(ang), np.sin(ang)
    rope = np.concatenate([cos, -sin, sin], axis=1).astype(f).reshape(NT + 1, P, 192)
    p = np.arange(P)
    g = np.array(GAMMA)
    causal = (p[:, None] <= p[None, :]).astype(np.float64)
    decay = np.concatenate([causal * g[h] ** -(p[:, None] + 1.0) * DK ** -0.5 for h in range(RH)], axis=1).astype(f)
    qdec = np.concatenate([g[h] ** (p + 1.0) for h in range(RH)]).astype(f)[None, :]
    vdec = np.stack([g[h] ** (P - 1.0 - p) * DK ** -0.5 for h in range(RH)], axis=1).astype(f)
    key = np.arange(2 * P)[None, :]
    seen = np.where(p[:, None] < HALF, key < P + HALF, key >= HALF)
    mask = np.stack([np.where(seen, 0.0, MASKED), np.where(seen & (key >= P), 0.0, MASKED)], axis=1).astype(f)
    return {"rope_tab": rope, "ident_tab": np.eye(P, dtype=f), "decay_tab": decay, "qdec_tab": qdec, "vdec_tab": vdec,
            "mask_tab": mask}


_OUTS = [("y_prompt", (SEQ, D), (1, SEQ, D)), ("y_sample", (HALF, D), (1, HALF, D)),
         ("ret_prompt", (RH, DK, DK), (1, 1, RH, DK, DK)), ("k_prompt", (P, P), (1, 1, P, 2, HD)),
         ("v_prompt", (P, P), (1, 1, P, 2, HD)), ("ret_sample", (RH, DK, DK), (1, 1, RH, DK, DK)),
         ("k_sample", (P, P), (1, 1, P, 2, HD)), ("v_sample", (P, P), (1, 1, P, 2, HD))]
_SHAPES = {"x_prompt": (SEQ, D), "x_sample": (HALF, D), "c_prompt": (1, D), "c_sample": (1, D),
           "state_ret": (RH, DK, DK), "cache_k": (P, P), "cache_v": (P, P), "norm_g": (1, D), "w_ada": (D, 3 * D),
           "b_ada": (1, 3 * D), "w_in": (D, IN_W), "sink": (1, QH), "w_out": (D, D), "final_g": (1, D)}


def kernel(**inputs):
    import numpy as np
    import concourse.bacc as bacc
    from concourse.bass_utils import run_bass_kernel_spmd

    nc = bacc.Bacc("TRN2", target_bir_lowering=False, num_devices=1, dynamic_dma_scratch_size=1024)
    arrays, args = {}, []
    given = {n: np.ascontiguousarray(inputs[n]).reshape(s) for n, s in _SHAPES.items()}
    given.update(tables())
    for name, a in given.items():
        arrays["in_" + name] = a
        args.append(nc.dram_tensor("in_" + name, a.shape, F32, kind="ExternalInput").ap())
    for i, (name, shape, _) in enumerate(_OUTS):
        args.append(nc.dram_tensor(f"out_{i}", shape, F32, kind="ExternalOutput").ap())
    args.append(nc.dram_tensor("h_scratch", (NT + 1, P, D), F32, kind="Internal").ap())
    args.append(nc.dram_tensor("yr_scratch", (NT + 1, P, COLS), F32, kind="Internal").ap())
    args.append(nc.dram_tensor("gate_scratch", (2, D), F32, kind="Internal").ap())
    build_program(nc, *args)
    r = run_bass_kernel_spmd(nc, [arrays], core_ids=[0])
    return tuple(r.results[0][f"out_{i}"].reshape(full) for i, (_, _, full) in enumerate(_OUTS))
```

```python
from contextlib import ExitStack

import concourse.bass as bass
from concourse import mybir

F32 = mybir.dt.float32
F32R = mybir.dt.float32r
ALU = mybir.AluOpType
ACT = mybir.ActivationFunctionType

P = 128
D = 1024
KC = D // P
SEQ = 4096
NT = SEQ // P
SAMPLE = NT
HALF = P // 2
COLS = 512
RH = 4
DK = 128
HD = 64
QH = 8
IN_W = 3328
OFF_RQ, OFF_RK, OFF_RV, OFF_RG, OFF_AQ, OFF_KV, OFF_AG = 0, 512, 1024, 1536, 2048, 2560, 2816
KV = 256
NORM_EPS = 1e-6
GN_EPS = 1e-5
GAMMA = [1.0 - 2.0 ** (-5 - h) for h in range(RH)]
SCORE_SCALE = HD ** -0.5
MASKED = -1e30


def build_program(nc, x_prompt, x_sample, c_prompt, c_sample, state_ret, cache_k, cache_v, norm_g, w_ada,
                  b_ada, w_in, sink, w_out, final_g, rope_tab, ident_tab, decay_tab, qdec_tab, vdec_tab,
                  mask_tab, y_prompt, y_sample, ret_prompt, k_prompt, v_prompt, ret_sample, k_sample,
                  v_sample, h_dram, yr_dram, gate_dram):
    ctx = ExitStack()
    with ctx:
        def sb(name, shape, dt=F32, where=ctx):
            return where.enter_context(nc.sbuf_tensor(name, shape, dt))

        def sem(name):
            return ctx.enter_context(nc.semaphore(name))

        wh = sb("wh", [P, 4, KC, COLS], F32R)
        wl = sb("wl", [P, 4, KC, COLS], F32R)
        hf = sb("hf", [P, KC, P])
        hh0 = sb("hh0", [P, KC, P], F32R)
        hl0 = sb("hl0", [P, KC, P], F32R)
        xt0 = sb("xt0", [P, D])
        ident = sb("ident", [P, P])
        small = sb("small", [P, 40])
        neg_half = small[:, 0:8]
        ssq = small[:, 8:10]
        meansq = small[:, 10:11]
        rstd = small[:, 11:12]
        gn_var = small[:, 12:16]
        gn_rstd = small[:, 16:20]
        norm_eps = small[:, 20:21]
        gn_eps = small[:, 21:25]
        zero = small[:, 25:26]
        spare = small[:, 26:27]

        phase_a = ExitStack()
        stage23 = sb("stage23", [P, 2, 2048], F32, phase_a)
        stage01 = sb("stage01", [P, 2, 2048], F32, phase_a)
        hh1 = sb("hh1", [P, KC, P], F32R, phase_a)
        hl1 = sb("hl1", [P, KC, P], F32R, phase_a)
        xn = sb("xn", [P, D], F32, phase_a)
        rope = sb("rope", [P, 192], F32, phase_a)
        swap = sb("swap", [P, COLS], F32, phase_a)
        q_row = sb("q_row", [P, COLS], F32, phase_a)
        k_row = sb("k_row", [P, COLS], F32, phase_a)
        q_t = sb("q_t", [P, COLS], F32, phase_a)
        k_t = sb("k_t", [P, COLS], F32, phase_a)
        v_row = sb("v_row", [P, COLS], F32, phase_a)
        v_dec = sb("v_dec", [P, COLS], F32, phase_a)
        s_t = sb("s_t", [P, COLS], F32, phase_a)
        state = sb("state", [P, COLS], F32, phase_a)
        state_s = sb("state_s", [P, COLS], F32, phase_a)
        r_gate = sb("r_gate", [P, COLS], F32, phase_a)
        r_out = sb("r_out", [P, COLS], F32, phase_a)
        yr_t = sb("yr_t", [P, COLS], F32, phase_a)
        decay = sb("decay", [P, COLS], F32, phase_a)
        qdec = sb("qdec", [P, COLS], F32, phase_a)
        tiny_a = sb("tiny_a", [P, 176], F32, phase_a)
        vdec = tiny_a[:, 0:4]
        gn_stats = tiny_a[:, 4:28].rearrange("p (h s) -> p h s", h=RH)
        gn_mv = tiny_a[:, 28:36].rearrange("p (h s) -> p h s", h=RH)
        c_in = tiny_a[:, 36:52].rearrange("p (c k) -> p c k", c=2)
        c_th = tiny_a[:, 52:68].rearrange("p (c k) -> p c k", c=2)
        c_silu = tiny_a[:, 68:84].rearrange("p (k c) -> p k c", c=2)
        g_col = tiny_a[:, 84:92]
        b_col = tiny_a[:, 92:108]
        h_scale = tiny_a[:, 108:124].rearrange("p (k c) -> p k c", c=2)
        h_shift = tiny_a[:, 124:140].rearrange("p (k c) -> p k c", c=2)
        mod_rows = s_t
        c_wide = yr_t[:, 0:KC * 32].rearrange("p (k c) -> p k c", k=KC)
        bias_rows = sb("bias_rows", [P, COLS], F32, phase_a)
        phase_a.close()

        wkvh = sb("wkvh", [P, KC, KV], F32R)
        wkvl = sb("wkvl", [P, KC, KV], F32R)
        p_t = sb("p_t", [P, 2, 4, P])
        s_row = sb("s_row", [P, 4, 2 * P])
        o_part = sb("o_part", [P, COLS])
        gate_t = sb("gate_t", [P, COLS])
        ya_f = sb("ya_f", [P, COLS])
        o_part1 = sb("o_part1", [P, COLS])
        out_gate = sb("out_gate", [P, D])
        xt1 = sb("xt1", [P, D])
        yr_in = sb("yr_in", [P, 4, P])
        yh = sb("yh", [P, KC, P], F32R)
        yl = sb("yl", [P, KC, P], F32R)
        aq_row = sb("aq_row", [P, QH, 2, HD], F32R)
        kv_rows = [sb(f"kv_row{u}", [P, 3 * P]) for u in range(2)]
        v_prev = sb("v_prev", [P, P])
        aq_t = sb("aq_t", [P, QH, P], F32R)
        ak_h = sb("ak_h", [P, 2, 2 * P], F32R)
        ak_l = sb("ak_l", [P, 2, 2 * P], F32R)
        a_gates = [sb(f"a_gate{u}", [P, COLS]) for u in range(2)]
        fin_g = sb("fin_g", [P, D])
        mask = sb("mask", [P, 2, 2 * P])
        kv_cache = sb("kv_cache", [P, 3 * P])
        tiny_b = sb("tiny_b", [P, 64])
        neg_sink = tiny_b[:, 0:8]
        s_max = tiny_b[:, 8:16]
        s_bias = tiny_b[:, 16:24]
        sink_arg = tiny_b[:, 24:32]
        sink_exp = tiny_b[:, 32:40]
        row_sum = tiny_b[:, 40:48]
        den = tiny_b[:, 48:56]
        rden = tiny_b[:, 56:64]
        xts = [xt0, xt1]
        hhs, hls = [hh0, hh1], [hl0, hl1]
        stages = [stage01[:, 0], stage01[:, 1], stage23[:, 0], stage23[:, 1]]

        bank = [ctx.enter_context(nc.psum_tensor(f"bank{i}", [P, COLS], F32)) for i in range(8)]
        za0, za1, xb0, xb1, qs_b, ky_b, out_b, upd_b = bank
        zb0, zb1, zb2, s0_b, s1_b, t0_b, t1_b, pv_b = bank

        c_loaded, mod_loaded, tab_loaded, state_loaded = (sem(n) for n in ("c_loaded", "mod_loaded", "tab_loaded", "state_loaded"))
        stage_loaded = [sem(f"stage{n}_loaded") for n in range(4)]
        c_tanh, c_ready, const_set, ada_used, mod_rows_out, mod_transposed, mod_ready = (
            sem(n) for n in ("c_tanh", "c_ready", "const_set", "ada_used", "mod_rows_out",
                             "mod_transposed", "mod_ready"))
        w_hi_done, w_lo_done, gate_rows, gate_stored, b_rows_loaded = (
            sem(n) for n in ("w_hi_done", "w_lo_done", "gate_rows", "gate_stored", "b_rows_loaded"))
        x_loaded, rope_loaded, h_stored, yr_stored = (sem(n) for n in ("x_loaded", "rope_loaded", "h_stored", "yr_stored"))
        ssq_done, rstd_mean, rstd_done, xn_done, x_transposed, h_done, hi_done, lo_done = (
            sem(n) for n in ("ssq_done", "rstd_mean", "rstd_done", "xn_done", "x_transposed", "h_done", "hi_done", "lo_done"))
        za_ready = sem("za_ready")
        zq_read, q_done, q_transposed, qt_done, zk_read, k_done, k_transposed, kt_done = (
            sem(n) for n in ("zq_read", "q_done", "q_transposed", "qt_done", "zk_read", "k_done", "k_transposed", "kt_done"))
        q_mul, k_mul = sem("q_mul"), sem("k_mul")
        vdec_done, v_done, rg_tanh, rg_done, s_ready, st_done, out_ready, upd_ready, state_done = (
            sem(n) for n in ("vdec_done", "v_done", "rg_tanh", "rg_done", "s_ready", "st_done", "out_ready",
                             "upd_ready", "state_done"))
        gn_stat_done, gn_mv_done, gn_var_done, gn_rstd_done, gn_done, yr_done, yr_transposed, yrt_done = (
            sem(n) for n in ("gn_stat_done", "gn_mv_done", "gn_var_done", "gn_rstd_done", "gn_done", "yr_done",
                             "yr_transposed", "yrt_done"))
        state_out, wide_set = sem("state_out"), sem("wide_set")
        fixed_loaded, hb_loaded, yr_loaded, cache_loaded, newer_loaded, kv_out = (
            sem(n) for n in ("fixed_loaded", "hb_loaded", "yr_loaded", "cache_loaded", "newer_loaded", "kv_out"))
        xb_loaded = [sem(f"xb{u}_loaded") for u in range(2)]
        y_stored = [sem(f"y{u}_stored") for u in range(2)]
        b_set, b_split, bh_hi, zb_ready = (sem(n) for n in ("b_set", "b_split", "bh_hi", "zb_ready"))
        kv_done, aq_hi, aq_lo, qk_transposed, aqt_done, ak_hi, ak_lo, k_shifted, v_shifted = (
            sem(n) for n in ("kv_done", "aq_hi", "aq_lo", "qk_transposed", "aqt_done", "ak_hi", "ak_lo", "k_shifted",
                             "v_shifted"))
        sb_ready, s_masked, bias_done, sarg_done, exp_done, p_transposed, pt0_done, pt1_done, pv_ready = (
            sem(n) for n in ("sb_ready", "s_masked", "bias_done", "sarg_done", "exp_done", "p_transposed", "pt0_done",
                             "pt1_done", "pv_ready"))
        ag_tanh, ag_done, den_done, rden_done, gate_scaled, gate_turned, ya_done, ya_hi, ya_lo = (
            sem(n) for n in ("ag_tanh", "ag_done", "den_done", "rden_done", "gate_scaled", "gate_turned", "ya_done",
                             "ya_hi", "ya_lo"))
        gate_out = sem("gate_out")
        yr_hi, yr_split, yr_used, o0_ready, o1_ready, o0_read, o1_read, x0_added, x1_added = (
            sem(n) for n in ("yr_hi", "yr_split", "yr_used", "o0_ready", "o1_ready", "o0_read", "o1_read", "x0_added",
                             "x1_added"))
        fsq0_done, fsq_done, fsum_done, fmean_done, frstd_done, fin_done = (
            sem(n) for n in ("fsq0_done", "fsq_done", "fsum_done", "fmean_done", "frstd_done", "fin_done"))
        block = ctx.enter_context(nc.Block())

        def wait(eng, s, value):
            if not (isinstance(value, int) and value <= 0):
                eng.wait_ge(s, value)

        def heads(ap, n=RH):
            return ap.rearrange("p (h d) -> p h d", h=n)

        w_in_k = w_in.rearrange("(k p) n -> p k n", p=P)
        w_out_k = w_out.rearrange("(k p) n -> p k n", p=P)
        w_out_a = [w_out[COLS + g * KV:COLS + (g + 1) * KV, :].rearrange("(j d) n -> d j n", d=HD) for g in range(2)]
        w_ada_k = w_ada.rearrange("(p k) n -> p k n", k=KC)
        pieces = [("ada", w_ada_k[:, k, 0:2 * D]) for k in range(KC)]
        pieces += [("w", w_in_k[:, 4 * s:4 * s + 4, off:off + COLS], g, 4 * s)
                   for g, off in enumerate((OFF_RQ, OFF_RK, OFF_RV, OFF_RG)) for s in range(2)]
        pieces += [("gate", w_ada_k[:, 2 * s:2 * s + 2, 2 * D:3 * D]) for s in range(4)]
        N_EARLY = len(pieces)
        pieces += [("kv", w_in_k[:, :, OFF_KV:OFF_KV + KV])]
        pieces += [("w", w_in_k[:, 4 * s:4 * s + 4, off:off + COLS], g, 4 * s)
                   for g, off in ((0, OFF_AQ), (1, OFF_AG)) for s in range(2)]
        for g, off in ((2, 0), (3, COLS)):
            pieces += [("w", w_out_k[:, 0:4, off:off + COLS], g, 0)]
            pieces += [("w", [w[:, :, off:off + COLS] for w in w_out_a], g, 4)]
        slot_of, turn_of, turns = [], [], [0] * 4
        for n in range(len(pieces)):
            s = n % 4 if n < N_EARLY else n % 2
            slot_of.append(s)
            turns[s] += len(pieces[n][1]) if isinstance(pieces[n][1], list) else 1
            turn_of.append(turns[s])
        split_pieces = [n for n, p in enumerate(pieces) if p[0] in ("w", "kv")]
        split_no = {n: i for i, n in enumerate(split_pieces)}
        ada_no = {n: i for i, n in enumerate(n for n, p in enumerate(pieces) if p[0] in ("ada", "gate"))}

        def stage_view(n):
            ap = stages[slot_of[n]]
            if pieces[n][0] == "ada":
                return ap
            width = {"w": COLS, "gate": D, "kv": KV}[pieces[n][0]]
            return ap.rearrange("p (k n) -> p k n", n=width)

        def wait_piece_used(eng, n):
            if n in split_no:
                eng.wait_ge(w_lo_done, split_no[n] + 1)
            else:
                eng.wait_ge(ada_used, ada_no[n] + 1)

        def load_piece(eng, n):
            before = [m for m in range(n) if slot_of[m] == slot_of[n]]
            if before:
                wait_piece_used(eng, before[-1])
            if isinstance(pieces[n][1], list):
                for g, src in enumerate(pieces[n][1]):
                    eng.dma_start(stage_view(n)[g * HD:(g + 1) * HD], src).then_inc(stage_loaded[slot_of[n]], 16)
            else:
                eng.dma_start(stage_view(n), pieces[n][1]).then_inc(stage_loaded[slot_of[n]], 16)

        def arrived(eng, n):
            eng.wait_ge(stage_loaded[slot_of[n]], 16 * turn_of[n])

        def part_of(n, low):
            if pieces[n][0] == "kv":
                return (wkvl if low else wkvh)[:, :, :]
            g, k = pieces[n][2:]
            return (wl if low else wh)[:, g, k:k + 4, :]

        def free_of_phase_a(eng, n):
            if n > N_EARLY:
                eng.wait_ge(za_ready, 4 * SAMPLE + pieces[n][2] + 1)

        def split_hi(act, n):
            arrived(act, n)
            free_of_phase_a(act, n)
            nc.scalar.activation(part_of(n, False), stage_view(n), ACT.Copy).then_inc(w_hi_done, 1)

        def split_lo(dve, n):
            dve.wait_ge(w_hi_done, split_no[n] + 1)
            nc.vector.tensor_tensor(part_of(n, True), stage_view(n), part_of(n, False).bitcast(F32),
                                    ALU.subtract).then_inc(w_lo_done, 1)

        FIRST_W, FIRST_GATE = KC, KC + 8
        B_KV, B_Q, B_GATE, B_OUT, B_OUT_LATE = N_EARLY, N_EARLY + 1, N_EARLY + 3, N_EARLY + 5, N_EARLY + 7

        def phase_tiles(eng, slot, last):
            slot(0, 0)
            slot(0, 1)
            with eng.Fori(1, NT // 2 - 1) as i:
                slot(i, 0)
                slot(i, 1)
            for t in range(NT - 2, last + 1):
                slot(t // 2, t % 2)

        def key_rows(rows, e):
            return rows[:, 0:2 * P].rearrange("p (g e d) -> p g e d", g=2, e=2)[:, :, e, :]

        def cached(rows, half, newer):
            at = slice(HALF * half, HALF * (half + 1))
            of = slice(HALF * newer, HALF * (newer + 1))
            keys = cache_k[of, :].rearrange("p (g d) -> p g d", g=2)
            return [(key_rows(rows, e)[at], keys) for e in range(2)] + [(rows[at, 2 * P:3 * P], cache_v[of, :])]

        def by_pairs(ap):
            return ap.rearrange("p (g j d) -> p j g d", g=2, j=4)

        def static(i):
            return isinstance(i, int)

        @block.sync
        def _(sp):
            for c, src in enumerate((c_prompt, c_sample)):
                sp.dma_start(c_in[:, c, :], src.rearrange("b (p k) -> (b p) k", k=KC)).then_inc(c_loaded, 16)
            sp.dma_start(ident[:, :], ident_tab).then_inc(c_loaded, 16)
            sp.dma_start(xt0[:, :], x_prompt[0:P, :]).then_inc(x_loaded, 16)
            for n in range(4):
                load_piece(sp, n)
            with nc.allow_non_contiguous_dma(reason="a few short columns"):
                sp.dma_start(g_col, norm_g.rearrange("a (k p) -> (a p) k", p=P)).then_inc(mod_loaded, 16)
                sp.dma_start(b_col, b_ada[:, 0:2 * D].rearrange("a (k p) -> (a p) k", p=P)).then_inc(mod_loaded, 16)
            for n in range(4, FIRST_W + 2):
                load_piece(sp, n)
            sp.dma_start(rope[:, :], rope_tab[0]).then_inc(rope_loaded, 16)
            sp.dma_start(decay[:, :], decay_tab).then_inc(tab_loaded, 16)
            sp.dma_start(qdec[:, :], qdec_tab.partition_broadcast(P)).then_inc(tab_loaded, 16)
            sp.dma_start(vdec, vdec_tab).then_inc(tab_loaded, 16)
            for n in range(FIRST_W + 2, FIRST_W + 4):
                load_piece(sp, n)
            sp.wait_ge(xn_done, 1)
            sp.dma_start(xt0[:, :], x_prompt[P:2 * P, :]).then_inc(x_loaded, 16)
            for n in range(FIRST_W + 4, FIRST_GATE):
                load_piece(sp, n)
            sp.dma_start(heads(state_s[:, :]), state_ret.rearrange("h k v -> k h v")).then_inc(state_loaded, 16)
            sp.wait_ge(h_done, 1)
            sp.dma_start(h_dram[0], hf[:, :, :].rearrange("p k r -> p (k r)")).then_inc(h_stored, 16)

            def slot(i, u):
                t = 2 * i + u
                if static(i) and t == SAMPLE:
                    for n in range(B_GATE, B_OUT):
                        load_piece(sp, n)
                    sp.wait_ge(h_stored, 16 * (SAMPLE + 1))
                    sp.wait_ge(lo_done, SAMPLE + 1)
                    sp.dma_start(hf[:, :, :].rearrange("p k r -> p (k r)"), h_dram[0]).then_inc(hb_loaded, 16)
                if not static(i) or t + 2 <= SAMPLE:
                    wait(sp, xn_done, t + 2)
                    if static(i) and t + 2 == SAMPLE:
                        sp.wait_ge(b_set, 1)
                        sp.dma_start(xt0[HALF:P, :], x_sample).then_inc(x_loaded, 16)
                    else:
                        sp.dma_start(xt0[:, :], x_prompt[bass.ts(t + 2, P), :]).then_inc(x_loaded, 16)
                if not static(i) or t + 1 <= SAMPLE:
                    wait(sp, h_done, t + 2)
                    sp.dma_start(h_dram[t + 1], hf[:, :, :].rearrange("p k r -> p (k r)")).then_inc(h_stored, 16)
                    wait(sp, zk_read, t + 1)
                    sp.dma_start(rope[:, :], rope_tab[t + 1]).then_inc(rope_loaded, 16)
                if static(i) and t == SAMPLE + 1:
                    sp.wait_ge(b_split, 1)
                    sp.dma_start(hf[:, :, :].rearrange("p k r -> p (k r)"), h_dram[1]).then_inc(hb_loaded, 16)
                if not static(i) or t >= 1:
                    wait(sp, yrt_done, t)
                    sp.dma_start(yr_dram[t - 1], yr_t[:, :]).then_inc(yr_stored, 16)
                if static(i) and t == 0:
                    for n in range(FIRST_GATE, N_EARLY):
                        load_piece(sp, n)
                    for j in range(2):
                        sp.dma_start(bias_rows[32 * j:32 * j + 2, :],
                                     b_ada[:, 2 * D + j * COLS:2 * D + (j + 1) * COLS].partition_broadcast(2)
                                     ).then_inc(b_rows_loaded, 16)
                if static(i) and t == 1:
                    sp.wait_ge(gate_rows, 1)
                    for j in range(2):
                        sp.dma_start(gate_dram[:, j * COLS:(j + 1) * COLS], bias_rows[32 * j:32 * j + 2, :]
                                     ).then_inc(gate_stored, 16)
                    for n in range(B_KV, B_Q + 1):
                        load_piece(sp, n)
                if static(i) and t == NT - 2:
                    load_piece(sp, B_Q + 1)
                if static(i) and t == SAMPLE:
                    sp.wait_ge(state_done, NT)
                    sp.dma_start(ret_prompt.rearrange("h k v -> k h v"), heads(state[:, :])).then_inc(state_out, 16)
                    for n in range(B_OUT, B_OUT_LATE):
                        load_piece(sp, n)

            phase_tiles(sp, slot, SAMPLE + 1)
            sp.wait_ge(state_done, NT + 1)
            sp.dma_start(ret_sample.rearrange("h k v -> k h v"), heads(state_s[:, :])).then_inc(state_out, 16)

            for n in range(B_OUT_LATE, len(pieces)):
                load_piece(sp, n)
            sp.wait_ge(yr_stored, 16 * (SAMPLE + 1))
            sp.wait_ge(gate_stored, 32)
            sp.wait_ge(state_out, 32)
            sp.wait_ge(yr_done, SAMPLE + 1)
            sp.dma_start(yr_in[:, :, :].rearrange("p k r -> p (k r)"), yr_dram[0]).then_inc(yr_loaded, 16)
            sp.dma_start(mask[:, :, :], mask_tab).then_inc(fixed_loaded, 16)
            with nc.allow_non_contiguous_dma(reason="eight sinks, in the heads' order of the pairs"):
                for g in range(2):
                    sp.dma_start(neg_sink.rearrange("p (j g) -> p j g", g=2)[:, :, g],
                                 sink[:, 4 * g:4 * g + 4].partition_broadcast(P)).then_inc(fixed_loaded, 16)
            sp.dma_start(out_gate[:, :], gate_dram[0:1, :].partition_broadcast(P)).then_inc(fixed_loaded, 16)
            sp.dma_start(fin_g[:, :], final_g.partition_broadcast(P)).then_inc(fixed_loaded, 16)

            def slot_b(i, u):
                t = 2 * i + u
                front = not static(i) or t <= SAMPLE
                if not static(i) or t >= 2:
                    wait(sp, fin_done, t - 1)
                    if static(i) and t - 2 == SAMPLE:
                        sp.dma_start(y_sample, xts[u][HALF:P, :]).then_inc(y_stored[u], 16)
                    else:
                        sp.dma_start(y_prompt[bass.ts(t - 2, P), :], xts[u][:, :]).then_inc(y_stored[u], 16)
                if static(i) and t == SAMPLE + 1:
                    sp.wait_ge(o1_read, NT)
                    sp.dma_start(out_gate[:, :], gate_dram[1:2, :].partition_broadcast(P)).then_inc(fixed_loaded, 16)
                if front:
                    if not (static(i) and t == 0):
                        wait(sp, yr_split, t)
                        sp.dma_start(yr_in[:, :, :].rearrange("p k r -> p (k r)"), yr_dram[t]).then_inc(yr_loaded, 16)
                    wait(sp, y_stored[u], 16 * i)
                    if static(i) and t == SAMPLE:
                        wait(sp, pv_ready, 2 * (t - 1))
                        wait(sp, v_shifted, t - 1)
                        for dst, src in cached(kv_rows[u], 0, 1):
                            sp.dma_start(dst, src).then_inc(newer_loaded, 16)
                        sp.wait_ge(b_set, 3)
                        sp.dma_start(xts[u][HALF:P, :], x_sample).then_inc(xb_loaded[u], 16)
                    else:
                        sp.dma_start(xts[u][:, :], x_prompt[bass.ts(t, P), :]).then_inc(xb_loaded[u], 16)
                if not static(i) or 1 <= t < SAMPLE:
                    wait(sp, b_split, t + 1)
                    sp.dma_start(hf[:, :, :].rearrange("p k r -> p (k r)"), h_dram[t + 1]).then_inc(hb_loaded, 16)
                if static(i) and t == 0:
                    for half in range(2):
                        for dst, src in cached(kv_cache, half, 0):
                            sp.dma_start(dst, src).then_inc(cache_loaded, 16)
                if static(i) and t in (NT - 1, SAMPLE):
                    sp.wait_ge(kv_done, t + 1)
                    if t == SAMPLE:
                        sp.wait_ge(newer_loaded, 3 * 16)
                    k_new, v_new = (k_prompt, v_prompt) if t == NT - 1 else (k_sample, v_sample)
                    sp.dma_start(k_new.rearrange("p (g d) -> p g d", g=2), key_rows(kv_rows[u], 0)).then_inc(kv_out, 16)
                    sp.dma_start(v_new, kv_rows[u][:, 2 * P:3 * P]).then_inc(kv_out, 16)

            phase_tiles(sp, slot_b, SAMPLE + 2)
            sp.wait_ge(kv_out, 64)
            sp.wait_ge(y_stored[0], 16 * (NT // 2 + 1))
            sp.wait_ge(y_stored[1], 16 * (NT // 2))
            sp.wait_ge(state_out, 32)

        @block.gpsimd
        def _(pool):
            nc.gpsimd.memset(c_wide, 0.0).then_inc(wide_set, 1)
            nc.gpsimd.memset(neg_half, -0.5)
            nc.gpsimd.memset(norm_eps, NORM_EPS)
            nc.gpsimd.memset(gn_eps, GN_EPS)
            nc.gpsimd.memset(zero, 0.0).then_inc(const_set, 1)
            nc.gpsimd.memset(state[:, :], 0.0).then_inc(const_set, 1)

            def prep(i, u):
                t = 2 * i + u
                wait(pool, ssq_done, t + 1)
                nc.gpsimd.tensor_tensor(meansq, ssq[:, 0:1], norm_eps, ALU.add).then_inc(rstd_mean, 1)
                wait(pool, rstd_mean, t + 1)
                wait(pool, xn_done, t)
                nc.gpsimd.tensor_tensor(rstd, meansq, neg_half[:, 0:1], ALU.pow).then_inc(rstd_done, 1)

            def slot(i, u):
                t = 2 * i + u
                if not static(i) or t + 1 <= SAMPLE:
                    prep(i + (u + 1) // 2, (u + 1) % 2)
                if not static(i) or t >= 1:
                    wait(pool, gn_mv_done, t)
                    wait(pool, gn_done, t - 1)
                    nc.gpsimd.tensor_tensor(gn_var, gn_mv[:, :, 1], gn_eps, ALU.add).then_inc(gn_var_done, 1)
                    wait(pool, gn_var_done, t)
                    nc.gpsimd.tensor_tensor(gn_rstd, gn_var, neg_half[:, 0:4], ALU.pow).then_inc(gn_rstd_done, 1)
                if static(i) and t == NT - 2:
                    pool.wait_ge(xn_done, NT)
                    nc.gpsimd.memset(xt0[0:HALF, :], 0.0).then_inc(b_set, 1)

            pool.wait_ge(const_set, 2)
            prep(0, 0)
            phase_tiles(pool, slot, SAMPLE + 1)

            pool.wait_ge(yr_stored, 16 * (SAMPLE + 1))
            pool.wait_ge(yr_done, SAMPLE + 1)
            pool.wait_ge(state_out, 32)
            for ak in (ak_h, ak_l):
                nc.gpsimd.tensor_tensor(ak[:, :, 0:P], zero.unsqueeze(1).to_broadcast([P, 2, P]),
                                        zero.unsqueeze(1).to_broadcast([P, 2, P]), ALU.add)
            nc.gpsimd.memset(v_prev[:, :], 0.0).then_inc(b_set, 1)

            def slot_b(i, u):
                t = 2 * i + u
                front = not static(i) or t <= SAMPLE
                back = not static(i) or 1 <= t <= SAMPLE + 1
                if front and (not static(i) or 1 <= t < SAMPLE):
                    wait(pool, sb_ready, 2 * t)
                    wait(pool, ak_hi, t)
                    wait(pool, ak_lo, t)
                    for ak in (ak_h, ak_l):
                        last = nc.gpsimd.tensor_tensor(ak[:, :, 0:P], ak[:, :, P:2 * P].bitcast(F32),
                                                       zero.unsqueeze(1).to_broadcast([P, 2, P]), ALU.add)
                    last.then_inc(k_shifted, 1)
                if front and (not static(i) or t >= 1):
                    wait(pool, pv_ready, 2 * t)
                    if static(i) and t == SAMPLE:
                        pool.wait_ge(cache_loaded, 6 * 16)
                        nc.gpsimd.tensor_copy(v_prev[:, :], kv_cache[:, 2 * P:3 * P]).then_inc(v_shifted, 1)
                    else:
                        nc.gpsimd.tensor_tensor(v_prev[:, :], kv_rows[1 - u][:, 2 * P:3 * P], zero.to_broadcast([P, P]),
                                                ALU.add).then_inc(v_shifted, 1)
                if static(i) and t == SAMPLE:
                    pool.wait_ge(y_stored[0], 16 * (NT // 2))
                    nc.gpsimd.memset(xt0[0:HALF, :], 0.0).then_inc(b_set, 1)
                if back:
                    xr = xts[1 - u]
                    wait(pool, xb_loaded[1 - u], 16 * (i + u))
                    wait(pool, o0_read, t)
                    nc.gpsimd.tensor_tensor(xr[:, 0:COLS], xr[:, 0:COLS], o_part[:, :], ALU.add).then_inc(x0_added, 1)
                    wait(pool, o1_read, t)
                    nc.gpsimd.tensor_tensor(xr[:, COLS:D], xr[:, COLS:D], o_part1[:, :], ALU.add).then_inc(x1_added, 1)
                    wait(pool, fsq_done, t)
                    wait(pool, fin_done, t - 1)
                    nc.gpsimd.tensor_tensor(meansq, ssq[:, 0:1], ssq[:, 1:2], ALU.add).then_inc(fsum_done, 1)
                    wait(pool, fsum_done, t)
                    nc.gpsimd.tensor_tensor(meansq, meansq, norm_eps, ALU.add).then_inc(fmean_done, 1)
                    wait(pool, fmean_done, t)
                    nc.gpsimd.tensor_tensor(rstd, meansq, neg_half[:, 0:1], ALU.pow).then_inc(frstd_done, 1)

            phase_tiles(pool, slot_b, SAMPLE + 2)

        @block.scalar
        def _(act):
            act.wait_ge(c_loaded, 48)
            nc.scalar.activation(c_th, c_in, ACT.Tanh, scale=0.5).then_inc(c_tanh, 1)

            def square(i, u):
                t = 2 * i + u
                wait(act, x_loaded, 16 * (t + 1))
                wait(act, x_transposed, t)
                wait(act, rstd_mean, t)
                nc.scalar.activation(xn[:, :], xt0[:, :], ACT.Square, scale=D ** -0.5, accum_out=ssq[:, 0:1]).then_inc(ssq_done, 1)

            def modulate(i, u, sample=False):
                t = 2 * i + u
                wait(act, x_transposed, t + 1)
                wait(act, h_stored, 16 * t)
                wait(act, lo_done, t)
                c, lo = (1, HALF) if sample else (0, 0)
                if sample:
                    for b, src in enumerate((xb0, xb1)):
                        nc.scalar.activation(hf[:, 4 * b:4 * b + 4, 0:HALF], heads(src[:, :])[:, :, 0:HALF], ACT.Copy)
                for k in range(KC):
                    src = (xb0 if k < 4 else xb1)[:, (k % 4) * P + lo:(k % 4 + 1) * P]
                    last = nc.scalar.activation(hf[:, k, lo:P], src, ACT.Identity, bias=h_shift[:, k, c:c + 1],
                                                scale=h_scale[:, k, c:c + 1])
                last.then_inc(h_done, 1)

            def slot(i, u):
                t = 2 * i + u
                front = not static(i) or t <= SAMPLE
                back = not static(i) or t >= 1
                nxt = (i + (u + 1) // 2, (u + 1) % 2)
                if not static(i) or t + 1 <= SAMPLE:
                    square(*nxt)
                    if static(i) and t == 0:
                        for n in range(FIRST_W + 4, FIRST_GATE):
                            split_hi(act, n)
                    modulate(*nxt, sample=static(i) and t + 1 == SAMPLE)
                if static(i) and t == SAMPLE:
                    for n in range(B_Q, B_OUT):
                        split_hi(act, n)
                if front:
                    wait(act, vdec_done, t + 1)
                    wait(act, out_ready, t)
                    nc.scalar.activation(v_row[:, :], za0[:, :], ACT.Copy).then_inc(v_done, 1)
                if static(i) and t == SAMPLE + 1:
                    for n in range(B_OUT, B_OUT_LATE):
                        split_hi(act, n)
                if back:
                    wait(act, yr_transposed, t)
                    wait(act, yr_stored, 16 * (t - 1))
                    nc.scalar.activation(yr_t[:, :], ky_b[:, :], ACT.Copy).then_inc(yrt_done, 1)
                if front:
                    wait(act, k_transposed, t + 1)
                    wait(act, s_ready, t)
                    nc.scalar.activation(k_t[:, :], ky_b[:, :], ACT.Copy).then_inc(kt_done, 1)
                    wait(act, za_ready, 4 * t + 4)
                    wait(act, yr_done, t)
                    nc.scalar.activation(r_gate[:, :], za1[:, :], ACT.Tanh, scale=0.5).then_inc(rg_tanh, 1)
                if static(i) and t == NT - 2:
                    split_hi(act, B_KV)

            square(0, 0)
            split_hi(act, FIRST_W)
            act.wait_ge(mod_ready, 1)
            modulate(0, 0)
            for n in range(FIRST_W + 1, FIRST_W + 4):
                split_hi(act, n)
            phase_tiles(act, slot, SAMPLE + 1)

            act.wait_ge(b_set, 2)

            def softmax(i, u, half):
                t = 2 * i + u
                n = 2 * t + half + 1
                wait(act, bias_done, n)
                for j in range(4):
                    h = 4 * half + j
                    nc.scalar.activation(s_row[:, j, :], s_row[:, j, :], ACT.Exp, bias=s_bias[:, h:h + 1],
                                         scale=SCORE_SCALE, accum_out=row_sum[:, h:h + 1])
                wait(act, sarg_done, n)
                nc.scalar.activation(sink_exp[:, 4 * half:4 * half + 4], sink_arg[:, 4 * half:4 * half + 4],
                                     ACT.Exp).then_inc(exp_done, 1)

            def p_out(i, u, half):
                t = 2 * i + u
                wait(act, p_transposed, 2 * t + half + 1)
                wait(act, pv_ready, 2 * t + half)
                nc.scalar.activation(p_t[:, 0].rearrange("p b r -> p (b r)"), t0_b[:, :], ACT.Copy).then_inc(pt0_done, 1)

            def slot_b(i, u):
                t = 2 * i + u
                front = not static(i) or t <= SAMPLE
                back = not static(i) or 1 <= t <= SAMPLE + 1
                prev = (i + (u - 1) // 2, (u + 1) % 2)
                if front:
                    wait(act, zb_ready, 3 * t + 1)
                    wait(act, pv_ready, 2 * (t - 1))
                    wait(act, v_shifted, t - 1)
                    lo = HALF if static(i) and t == SAMPLE else 0
                    keys = zb0[lo:P, 0:P].rearrange("p (g d) -> p g d", g=2).unsqueeze(2).to_broadcast([P - lo, 2, 2, HD])
                    nc.scalar.activation(kv_rows[u][lo:P, 0:2 * P].rearrange("p (g e d) -> p g e d", g=2, e=2), keys, ACT.Copy)
                    nc.scalar.activation(kv_rows[u][lo:P, 2 * P:3 * P], zb0[lo:P, P:2 * P], ACT.Copy).then_inc(kv_done, 1)
                if back:
                    softmax(*prev, 0)
                if front:
                    wait(act, zb_ready, 3 * t + 2)
                    wait(act, qk_transposed, t)
                    wait(act, aqt_done, t)
                    nc.scalar.activation(aq_row[:, :, 0, :].rearrange("p (j g) d -> p j g d", g=2), by_pairs(zb1[:, :]),
                                         ACT.Copy).then_inc(aq_hi, 1)
                if back:
                    p_out(*prev, 0)
                    softmax(*prev, 1)
                if front:
                    wait(act, zb_ready, 3 * t + 3)
                    wait(act, gate_turned, t - 1)
                    nc.scalar.activation(a_gates[u][:, :].rearrange("p (j g d) -> p j g d", j=4, g=2), by_pairs(zb2[:, :]),
                                         ACT.Tanh, scale=0.5).then_inc(ag_tanh, 1)
                if static(i) and t == 0:
                    split_hi(act, B_OUT_LATE)
                if back:
                    p_out(*prev, 1)
                    wait(act, ya_done, t)
                    wait(act, o1_ready, t - 1)
                    nc.scalar.activation(yh[:, 4:8, :].rearrange("p k r -> p (k r)"), ya_f[:, :], ACT.Copy).then_inc(ya_hi, 1)
                if front:
                    wait(act, qk_transposed, t + 1)
                    wait(act, sb_ready, 2 * t)
                    for b, src in enumerate((t0_b, t1_b)):
                        last = nc.scalar.activation(aq_t[:, 4 * b:4 * b + 4, :].rearrange("p k r -> p (k r)"), src[:, :],
                                                    ACT.Copy)
                    last.then_inc(aqt_done, 1)
                    if static(i) and t == SAMPLE:
                        nc.scalar.activation(ak_h[:, :, 0:P], s1_b[:, 2 * P:4 * P].rearrange("p (g r) -> p g r", g=2), ACT.Copy)
                    else:
                        wait(act, k_shifted, t)
                    nc.scalar.activation(ak_h[:, :, P:2 * P], s1_b[:, 0:2 * P].rearrange("p (g r) -> p g r", g=2),
                                         ACT.Copy).then_inc(ak_hi, 1)
                if static(i) and t == 0:
                    split_hi(act, B_OUT_LATE + 1)
                if back:
                    xr = xts[1 - u]
                    wait(act, x0_added, t)
                    wait(act, ag_done, t + 1 if front else t)
                    wait(act, fsum_done, t - 1)
                    nc.scalar.activation(zb2[:, :], xr[:, 0:COLS], ACT.Square, scale=D ** -0.5, accum_out=ssq[:, 0:1]).then_inc(fsq0_done, 1)
                    wait(act, x1_added, t)
                    wait(act, fsq0_done, t)
                    nc.scalar.activation(zb2[:, :], xr[:, COLS:D], ACT.Square, scale=D ** -0.5, accum_out=ssq[:, 1:2]).then_inc(fsq_done, 1)

            phase_tiles(act, slot_b, SAMPLE + 1)

        @block.vector
        def _(dve):
            V = nc.vector
            dve.wait_ge(c_tanh, 1)
            dve.wait_ge(wide_set, 1)
            cT = c_in.rearrange("p c k -> p k c")
            tT = c_th.rearrange("p c k -> p k c")
            V.scalar_tensor_tensor(c_silu, tT, 1.0, cT, ALU.add, ALU.mult).then_inc(c_ready, 1)
            dve.wait_ge(c_ready, 1)
            V.tensor_scalar(c_wide[:, :, 0:2], c_silu, 0.5, None, ALU.mult)
            V.tensor_scalar(c_silu, c_silu, 0.5, None, ALU.mult).then_inc(c_ready, 1)

            def normalise(i, u):
                t = 2 * i + u
                wait(dve, rstd_done, t + 1)
                V.tensor_scalar(xn[:, :], xt0[:, :], rstd, None, ALU.mult).then_inc(xn_done, 1)

            def split_h(i, u):
                t = 2 * i + u
                wait(dve, h_done, t + 1)
                wait(dve, za_ready, 4 * (t - 1))
                V.tensor_copy(hhs[u][:, :, :], hf[:, :, :]).then_inc(hi_done, 1)
                wait(dve, hi_done, t + 1)
                V.tensor_tensor(hls[u][:, :, :], hf[:, :, :], hhs[u][:, :, :].bitcast(F32), ALU.subtract).then_inc(lo_done, 1)

            def split_hb(i, u):
                t = 2 * i + u
                wait(dve, hb_loaded, 16 * (t + 1))
                if static(i) and t == 0:
                    dve.wait_ge(za_ready, 4 * (SAMPLE + 1))
                wait(dve, zb_ready, 3 * t)
                V.tensor_copy(hh0[:, :, :], hf[:, :, :]).then_inc(bh_hi, 1)
                wait(dve, bh_hi, t + 1)
                V.tensor_tensor(hl0[:, :, :], hf[:, :, :], hh0[:, :, :].bitcast(F32), ALU.subtract).then_inc(b_split, 1)

            def rotate(t, z, row, zread, mul, done):
                z4 = z[:, :].rearrange("p (h e d) -> p h e d", h=RH, e=2)
                sin = rope[:, 64:192].rearrange("p (e d) -> p e d", e=2).unsqueeze(1).to_broadcast([P, RH, 2, 64])
                cos = rope[:, 0:64].unsqueeze(1).to_broadcast([P, 2 * RH, 64])
                V.tensor_tensor(swap[:, :].rearrange("p (h e d) -> p h e d", h=RH, e=2), z4[:, :, ::-1, :], sin,
                                ALU.mult).then_inc(mul, 1)
                V.tensor_tensor(heads(row[:, :], 8), heads(z[:, :], 8), cos, ALU.mult).then_inc(zread, 1)
                wait(dve, mul, t + 1)
                wait(dve, zread, t + 1)
                V.tensor_tensor(row[:, :], row[:, :], swap[:, :], ALU.add).then_inc(done, 1)

            def slot(i, u):
                t = 2 * i + u
                front = not static(i) or t <= SAMPLE
                back = not static(i) or t >= 1
                nxt = (i + (u + 1) // 2, (u + 1) % 2)
                more = not static(i) or t + 1 <= SAMPLE
                if more:
                    normalise(*nxt)
                if front:
                    wait(dve, za_ready, 4 * t + 1)
                    wait(dve, rope_loaded, 16 * (t + 1))
                    wait(dve, q_transposed, t)
                    wait(dve, k_done, t)
                    rotate(t, za0, q_row, zq_read, q_mul, q_done)
                if static(i) and t == SAMPLE:
                    for n in range(B_Q, B_GATE):
                        split_lo(dve, n)
                if static(i) and t == SAMPLE + 1:
                    split_hb(0, 0)
                if static(i) and t == 0:
                    for n in range(FIRST_W + 4, FIRST_GATE):
                        split_lo(dve, n)
                if back:
                    wait(dve, out_ready, t)
                    wait(dve, gn_mv_done, t - 1)
                    for h in range(RH):
                        last = V.bn_stats(gn_stats[:, h, :], out_b[:, h * DK:(h + 1) * DK])
                    last.then_inc(gn_stat_done, 1)
                    wait(dve, gn_stat_done, t)
                    wait(dve, gn_var_done, t - 1)
                    wait(dve, upd_ready, t)
                    st = state_s if static(i) and t - 1 == SAMPLE else state
                    for h in range(RH):
                        cols = slice(h * DK, (h + 1) * DK)
                        last = V.scalar_tensor_tensor(st[:, cols], st[:, cols], GAMMA[h] ** P, upd_b[:, cols], ALU.mult, ALU.add)
                    last.then_inc(state_done, 1)
                    for h in range(RH):
                        last = V.bn_aggr(gn_mv[:, h, :], gn_stats[:, h, :])
                    last.then_inc(gn_mv_done, 1)
                    wait(dve, gn_rstd_done, t)
                    wait(dve, yr_transposed, t - 1)
                    for h in range(RH):
                        cols = slice(h * DK, (h + 1) * DK)
                        last = V.tensor_scalar(r_out[:, cols], out_b[:, cols], gn_mv[:, h, 0:1], gn_rstd[:, h:h + 1],
                                               ALU.subtract, ALU.mult)
                    last.then_inc(gn_done, 1)
                    wait(dve, gn_done, t)
                    wait(dve, rg_done, t)
                    V.scalar_tensor_tensor(r_out[:, :], r_out[:, :], 0.5, r_gate[:, :], ALU.mult, ALU.mult).then_inc(yr_done, 1)
                if more and not (static(i) and t == 0):
                    split_h(*nxt)
                if front:
                    wait(dve, za_ready, 4 * t + 2)
                    wait(dve, upd_ready, t)
                    wait(dve, q_done, t + 1)
                    rotate(t, za1, k_row, zk_read, k_mul, k_done)
                    if static(i) and t == 0:
                        dve.wait_ge(tab_loaded, 48)
                    wait(dve, q_transposed, t + 1)
                    wait(dve, out_ready, t)
                    V.tensor_tensor(q_t[:, :], qs_b[:, :], qdec[:, :], ALU.mult).then_inc(qt_done, 1)
                if static(i) and t == 0:
                    split_h(*nxt)
                if static(i) and t == 0:
                    dve.wait_ge(state_loaded, 16)
                    for h in range(RH):
                        V.tensor_scalar(state_s[:, h * DK:(h + 1) * DK], state_s[:, h * DK:(h + 1) * DK],
                                        GAMMA[h] ** -HALF, None, ALU.mult)
                if front:
                    wait(dve, za_ready, 4 * t + 3)
                    V.tensor_tensor(heads(v_dec[:, :]), heads(za0[:, :]), vdec.unsqueeze(2).to_broadcast([P, RH, DK]),
                                    ALU.mult).then_inc(vdec_done, 1)
                    if static(i) and t == SAMPLE:
                        for n in range(B_GATE, B_OUT):
                            split_lo(dve, n)
                    wait(dve, rg_tanh, t + 1)
                    V.scalar_tensor_tensor(r_gate[:, :], r_gate[:, :], 1.0, za1[:, :], ALU.add, ALU.mult).then_inc(rg_done, 1)
                    wait(dve, s_ready, t + 1)
                    wait(dve, out_ready, t)
                    V.tensor_tensor(s_t[:, :], qs_b[:, :], decay[:, :], ALU.mult).then_inc(st_done, 1)
                if static(i) and t == NT - 2:
                    split_lo(dve, B_KV)
                if static(i) and t == SAMPLE + 1:
                    for n in range(B_OUT, B_OUT_LATE):
                        split_lo(dve, n)
                if static(i) and t == 1:
                    dve.wait_ge(ada_used, KC + 4)
                    dve.wait_ge(b_rows_loaded, 32)
                    for j in range(2):
                        rows = slice(32 * j, 32 * j + 2)
                        last = V.tensor_tensor(bias_rows[rows, :], upd_b[rows, :], bias_rows[rows, :], ALU.add)
                    last.then_inc(gate_rows, 1)

            normalise(0, 0)
            dve.wait_ge(ada_used, KC)
            V.tensor_copy(mod_rows[:, :], out_b[:, :]).then_inc(mod_rows_out, 1)
            dve.wait_ge(mod_transposed, 1)
            dve.wait_ge(mod_loaded, 32)
            turned = upd_b[:, :].rearrange("p (b r) -> p b r", b=4)
            for j in range(4):
                dst = (h_shift if j < 2 else h_scale)[:, 4 * (j % 2):4 * (j % 2) + 4, :]
                bias = b_col[:, 4 * j:4 * j + 4].unsqueeze(2).to_broadcast([P, 4, 2])
                last = V.tensor_tensor(dst, turned[:, :, 32 * j:32 * j + 2], bias, ALU.add)
            last.then_inc(mod_rows_out, 1)
            dve.wait_ge(mod_rows_out, 2)
            V.scalar_tensor_tensor(h_scale, h_scale, 1.0, g_col.unsqueeze(2).to_broadcast([P, KC, 2]), ALU.add,
                                   ALU.mult).then_inc(mod_ready, 1)
            split_lo(dve, FIRST_W)
            split_h(0, 0)
            for n in range(FIRST_W + 1, FIRST_W + 4):
                split_lo(dve, n)
            phase_tiles(dve, slot, SAMPLE + 1)

            dve.wait_ge(b_set, 2)

            def mask_max(i, u, half):
                t = 2 * i + u
                n = 2 * t + half + 1
                wait(dve, p_transposed, n - 1)
                wait(dve, sb_ready, n)
                wait(dve, sarg_done, n - 1)
                m = mask[:, 1 if static(i) and t == 0 else 0, :]
                V.memset(spare, 0.0)
                for j in range(4):
                    h = 4 * half + j
                    src = (s0_b, s1_b)[j // 2][:, (j % 2) * 2 * P:(j % 2 + 1) * 2 * P]
                    last = V.tensor_tensor_reduce(out=s_row[:, j, :], in0=src, in1=m, scale=1.0, scalar=MASKED,
                                                  op0=ALU.add, op1=ALU.max, accum_out=s_max[:, h:h + 1])
                last.then_inc(s_masked, 1)
                hs = slice(4 * half, 4 * half + 4)
                wait(dve, s_masked, n)
                wait(dve, exp_done, n - 2)
                V.scalar_tensor_tensor(s_bias[:, hs], s_max[:, hs], -SCORE_SCALE, neg_sink[:, hs], ALU.mult,
                                       ALU.min).then_inc(bias_done, 1)
                wait(dve, bias_done, n)
                V.tensor_tensor(sink_arg[:, hs], s_bias[:, hs], neg_sink[:, hs], ALU.subtract).then_inc(sarg_done, 1)

            def p_out(i, u, half):
                t = 2 * i + u
                wait(dve, p_transposed, 2 * t + half + 1)
                wait(dve, pv_ready, 2 * t + half)
                V.tensor_copy(p_t[:, 1].rearrange("p b r -> p (b r)"), t1_b[:, :]).then_inc(pt1_done, 1)

            def final(i, u):
                t = 2 * i + u
                wait(dve, frstd_done, t + 1)
                V.scalar_tensor_tensor(xts[u][:, :], xts[u][:, :], rstd, fin_g[:, :], ALU.mult, ALU.mult).then_inc(fin_done, 1)

            def slot_b(i, u):
                t = 2 * i + u
                front = not static(i) or t <= SAMPLE
                back = not static(i) or 1 <= t <= SAMPLE + 1
                prev = (i + (u - 1) // 2, (u + 1) % 2)
                nxt = (i + (u + 1) // 2, (u + 1) % 2)
                if static(i) and t == 1:
                    dve.wait_ge(fixed_loaded, 80)
                    V.tensor_scalar(neg_sink, neg_sink, -1.0, None, ALU.mult).then_inc(const_set, 1)
                    dve.wait_ge(const_set, 3)
                if back:
                    mask_max(*prev, 0)
                if not static(i) or t >= 2:
                    final(i - 1, u)
                if back:
                    p_out(*prev, 0)
                    mask_max(*prev, 1)
                if front:
                    wait(dve, aq_hi, t + 1)
                    V.tensor_tensor(aq_row[:, :, 1, :].rearrange("p (j g) d -> p j g d", g=2), by_pairs(zb1[:, :]),
                                    aq_row[:, :, 0, :].rearrange("p (j g) d -> p j g d", g=2).bitcast(F32),
                                    ALU.subtract).then_inc(aq_lo, 1)
                    wait(dve, ag_tanh, t + 1)
                    for g in range(2):
                        ag = a_gates[u][:, :].rearrange("p (j g d) -> p j g d", j=4, g=2)[:, :, g, :]
                        last = V.scalar_tensor_tensor(ag, ag, 1.0, heads(zb2[:, g * KV:(g + 1) * KV]), ALU.add, ALU.mult)
                    last.then_inc(ag_done, 1)
                if back:
                    wait(dve, exp_done, 2 * t)
                    wait(dve, gate_scaled, t - 1)
                    V.tensor_tensor(den, row_sum, sink_exp, ALU.add).then_inc(den_done, 1)
                    wait(dve, den_done, t)
                    V.reciprocal(rden, den).then_inc(rden_done, 1)
                    wait(dve, rden_done, t)
                    wait(dve, ag_done, t)
                    V.scalar_tensor_tensor(heads(a_gates[1 - u][:, :], QH), heads(a_gates[1 - u][:, :], QH), 0.5,
                                           rden.unsqueeze(2).to_broadcast([P, QH, HD]), ALU.mult,
                                           ALU.mult).then_inc(gate_scaled, 1)
                    p_out(*prev, 1)
                if not static(i) or t + 1 <= SAMPLE:
                    split_hb(*nxt)
                if back:
                    wait(dve, gate_turned, t)
                    wait(dve, pv_ready, 2 * t)
                    wait(dve, ya_hi, t - 1)
                    wait(dve, ya_lo, t - 1)
                    V.tensor_copy(gate_t[:, :], s0_b[:, :]).then_inc(gate_out, 1)
                    wait(dve, gate_out, t)
                    V.tensor_tensor(ya_f[:, :], pv_b[:, :], gate_t[:, :], ALU.mult).then_inc(ya_done, 1)
                    wait(dve, ya_hi, t)
                    wait(dve, ya_done, t)
                    V.tensor_tensor(yl[:, 4:8, :].rearrange("p k r -> p (k r)"), ya_f[:, :],
                                    yh[:, 4:8, :].rearrange("p k r -> p (k r)").bitcast(F32), ALU.subtract).then_inc(ya_lo, 1)
                if front:
                    wait(dve, ak_hi, t + 1)
                    wait(dve, k_shifted, min(t, SAMPLE - 1) if static(i) else t)
                    if static(i) and t == SAMPLE:
                        V.tensor_tensor(ak_l[:, :, 0:P], s1_b[:, 2 * P:4 * P].rearrange("p (g r) -> p g r", g=2),
                                        ak_h[:, :, 0:P].bitcast(F32), ALU.subtract)
                    V.tensor_tensor(ak_l[:, :, P:2 * P], s1_b[:, 0:2 * P].rearrange("p (g r) -> p g r", g=2),
                                    ak_h[:, :, P:2 * P].bitcast(F32), ALU.subtract).then_inc(ak_lo, 1)
                if static(i) and t == 0:
                    for n in range(B_OUT_LATE, len(pieces)):
                        split_lo(dve, n)
                if front:
                    wait(dve, yr_loaded, 16 * (t + 1))
                    wait(dve, yr_used, t)
                    V.tensor_copy(yh[:, 0:4, :], yr_in[:, :, :]).then_inc(yr_hi, 1)
                    wait(dve, yr_hi, t + 1)
                    V.tensor_tensor(yl[:, 0:4, :], yr_in[:, :, :], yh[:, 0:4, :].bitcast(F32), ALU.subtract).then_inc(yr_split, 1)
                if back:
                    if static(i) and t == SAMPLE + 1:
                        dve.wait_ge(fixed_loaded, 96)
                    wait(dve, o0_ready, t)
                    wait(dve, x0_added, t - 1)
                    V.tensor_tensor(o_part[:, :], zb0[:, :], out_gate[:, 0:COLS], ALU.mult).then_inc(o0_read, 1)
                    wait(dve, o1_ready, t)
                    wait(dve, x1_added, t - 1)
                    V.tensor_tensor(o_part1[:, :], zb1[:, :], out_gate[:, COLS:D], ALU.mult).then_inc(o1_read, 1)

            phase_tiles(dve, slot_b, SAMPLE + 2)

        @block.tensor
        def _(pe):
            mm = nc.tensor.matmul

            def dense(out, xh, xl, weights, part=(0, 1, 2), chunks=range(KC), first=True, last=True):
                w_hi, w_lo = weights
                passes = [(xh, w_hi), (xh, w_lo), (xl, w_hi)]
                for n in part:
                    a, b = passes[n]
                    for k in chunks:
                        ins = mm(out, a[:, k, :], b[:, k, :], start=first and n == part[0] and k == chunks[0],
                                 stop=last and n == part[-1] and k == chunks[-1])
                return ins

            def group(g):
                return wh[:, g], wl[:, g]

            def transpose_x(i, u):
                t = 2 * i + u
                wait(pe, xn_done, t + 1)
                wait(pe, h_done, t)
                for k in range(KC):
                    last = nc.tensor.transpose((xb0 if k < 4 else xb1)[:, (k % 4) * P:(k % 4 + 1) * P],
                                               xn[:, k * P:(k + 1) * P], ident[:, :])
                last.then_inc(x_transposed, 1)

            pe.wait_ge(c_ready, 2)
            pe.wait_ge(c_loaded, 48)
            transpose_x(0, 0)
            for k in range(KC):
                arrived(pe, k)
                for j in range(4):
                    last = mm(out_b[32 * j:32 * j + 32, :], c_wide[:, k, :], stages[slot_of[k]][:, j * COLS:(j + 1) * COLS],
                              start=k == 0, stop=k == KC - 1, tile_position=(0, 32 * j))
                last.then_inc(ada_used, 1)
            pe.wait_ge(mod_rows_out, 1)
            for b in range(4):
                last = nc.tensor.transpose(upd_b[:, b * P:(b + 1) * P], mod_rows[:, b * P:(b + 1) * P], ident[:, :])
            last.then_inc(mod_transposed, 1)

            def dense_kv(i, u):
                t = 2 * i + u
                wait(pe, b_split, t + 1)
                wait(pe, o0_read, t - 1)
                if static(i) and t == 0:
                    pe.wait_ge(w_lo_done, split_no[B_KV] + 1)
                    pe.wait_ge(v_done, SAMPLE + 1)
                dense(zb0[:, 0:KV], hh0, hl0, (wkvh, wkvl)).then_inc(zb_ready, 1)

            def slot(i, u):
                t = 2 * i + u
                front = not static(i) or t <= SAMPLE
                back = not static(i) or t >= 1
                h_hi, h_lo = hhs[u], hls[u]
                if front:
                    wait(pe, lo_done, t + 1)
                    wait(pe, v_done, t)
                    if static(i) and t == 0:
                        pe.wait_ge(w_lo_done, 2)
                    dense(za0[:, :], h_hi, h_lo, group(0)).then_inc(za_ready, 1)
                if back:
                    wait(pe, st_done, t)
                    wait(pe, state_done, t - 1)
                    wait(pe, gn_done, t - 1)
                    wait(pe, v_done, t)
                    st = state_s if static(i) and t - 1 == SAMPLE else state
                    for h in range(RH):
                        c = slice(h * DK, (h + 1) * DK)
                        mm(out_b[:, c], s_t[:, c], v_row[:, c], start=True, stop=False)
                        last = mm(out_b[:, c], q_t[:, c], st[:, c], start=False, stop=True)
                    last.then_inc(out_ready, 1)
                    for h in range(RH):
                        c = slice(h * DK, (h + 1) * DK)
                        last = mm(upd_b[:, c], k_row[:, c], v_dec[:, c], start=True, stop=True)
                    last.then_inc(upd_ready, 1)
                if static(i) and t == SAMPLE + 1:
                    dense_kv(0, 0)
                    pe.wait_ge(w_lo_done, split_no[B_GATE - 1] + 1)
                    pe.wait_ge(rg_done, SAMPLE + 1)
                    dense(zb1[:, :], hh0, hl0, group(0), part=(0, 1), last=False)
                if not static(i) or t + 1 <= SAMPLE:
                    transpose_x(i + (u + 1) // 2, (u + 1) % 2)
                if front:
                    wait(pe, rg_done, t)
                    if static(i) and t == 0:
                        pe.wait_ge(w_lo_done, 4)
                    dense(za1[:, :], h_hi, h_lo, group(1)).then_inc(za_ready, 1)
                    wait(pe, q_done, t + 1)
                    wait(pe, st_done, t)
                    for h in range(RH):
                        c = slice(h * DK, (h + 1) * DK)
                        last = nc.tensor.transpose(qs_b[:, c], q_row[:, c], ident[:, :])
                    last.then_inc(q_transposed, 1)
                    wait(pe, zq_read, t + 1)
                    if static(i) and t == 0:
                        pe.wait_ge(w_lo_done, 6)
                    dense(za0[:, :], h_hi, h_lo, group(2)).then_inc(za_ready, 1)
                if back:
                    wait(pe, yr_done, t)
                    wait(pe, kt_done, t)
                    for h in range(RH):
                        c = slice(h * DK, (h + 1) * DK)
                        last = nc.tensor.transpose(ky_b[:, c], r_out[:, c], ident[:, :])
                    last.then_inc(yr_transposed, 1)
                if static(i) and t == SAMPLE + 1:
                    dense(zb1[:, :], hh0, hl0, group(0), part=(2,), first=False).then_inc(zb_ready, 1)
                    pe.wait_ge(w_lo_done, split_no[B_OUT - 1] + 1)
                    dense(zb2[:, :], hh0, hl0, group(1)).then_inc(zb_ready, 1)
                if front:
                    wait(pe, zk_read, t + 1)
                    if static(i) and t == 0:
                        pe.wait_ge(w_lo_done, 8)
                    dense(za1[:, :], h_hi, h_lo, group(3), part=(0, 1), last=False)
                    wait(pe, k_done, t + 1)
                    wait(pe, yrt_done, t)
                    for h in range(RH):
                        c = slice(h * DK, (h + 1) * DK)
                        last = nc.tensor.transpose(ky_b[:, c], k_row[:, c], ident[:, :])
                    last.then_inc(k_transposed, 1)
                    dense(za1[:, :], h_hi, h_lo, group(3), part=(2,), first=False).then_inc(za_ready, 1)
                    wait(pe, qt_done, t + 1)
                    wait(pe, kt_done, t + 1)
                    for h in range(RH):
                        c = slice(h * DK, (h + 1) * DK)
                        last = mm(qs_b[:, c], k_t[:, c], q_t[:, c], start=True, stop=True)
                    last.then_inc(s_ready, 1)
                if static(i) and t == 1:
                    pe.wait_ge(state_done, 1)
                    for s in range(4):
                        n = FIRST_GATE + s
                        arrived(pe, n)
                        for kk in range(2):
                            for j in range(2):
                                last = mm(upd_b[32 * j:32 * j + 2, :], c_silu[:, 2 * s + kk, :],
                                          stage_view(n)[:, kk, j * COLS:(j + 1) * COLS], start=s == 0 and kk == 0,
                                          stop=s == 3 and kk == 1, tile_position=(0, 32 * j))
                        last.then_inc(ada_used, 1)
                    pe.wait_ge(gate_rows, 1)

            phase_tiles(pe, slot, SAMPLE + 1)

            def scores(i, u, half):
                t = 2 * i + u
                if half == 0:
                    wait(pe, aqt_done, t + 1)
                    wait(pe, ak_hi, t + 1)
                    wait(pe, ak_lo, t + 1)
                    wait(pe, gate_out, t)
                wait(pe, s_masked, 2 * t + half)
                for j in range(4):
                    dst = (s0_b, s1_b)[j // 2][:, (j % 2) * 2 * P:(j % 2 + 1) * 2 * P]
                    q = aq_t[:, 4 * half + j, :]
                    mm(dst, q, ak_h[:, j % 2, :], start=True, stop=False)
                    last = mm(dst, q, ak_l[:, j % 2, :], start=False, stop=True)
                last.then_inc(sb_ready, 1)

            def turn_p(i, u, half):
                t = 2 * i + u
                wait(pe, exp_done, 2 * t + half + 1)
                wait(pe, pt0_done, 2 * t + half)
                wait(pe, pt1_done, 2 * t + half)
                for j in range(4):
                    at = 2 * (j % 2) + j // 2
                    for s in range(2):
                        last = nc.tensor.transpose((t0_b, t1_b)[s][:, at * P:(at + 1) * P],
                                                   s_row[:, j, s * P:(s + 1) * P], ident[:, :])
                last.then_inc(p_transposed, 1)

            def weigh(i, u, half):
                t = 2 * i + u
                wait(pe, pt0_done, 2 * t + half + 1)
                wait(pe, pt1_done, 2 * t + half + 1)
                if half == 0:
                    wait(pe, v_shifted, t)
                    wait(pe, ya_done, t)
                for s in range(2):
                    for g in range(2):
                        cols = slice(g * HD, (g + 1) * HD)
                        v = v_prev[:, cols] if s == 0 else kv_rows[u][:, 2 * P + g * HD:2 * P + (g + 1) * HD]
                        last = mm(pv_b[cols, half * 2 * P:(half + 1) * 2 * P], v, p_t[:, s, 2 * g:2 * g + 2, :],
                                  start=s == 0, stop=s == 1, tile_position=(0, g * HD))
                last.then_inc(pv_ready, 1)

            def slot_b(i, u):
                t = 2 * i + u
                front = not static(i) or t <= SAMPLE
                back = not static(i) or t >= 1
                prev = (i + (u - 1) // 2, (u + 1) % 2)

                def retention_out_0():
                    wait(pe, yr_split, t)
                    wait(pe, kv_done, t + 1 if front else t)
                    if static(i) and t == 1:
                        pe.wait_ge(w_lo_done, len(split_pieces))
                    dense(zb0[:, :], yh, yl, group(2), chunks=range(4), last=False)

                def retention_out_1():
                    wait(pe, aq_lo, t + 1 if front else t)
                    dense(zb1[:, :], yh, yl, group(3), chunks=range(4), last=False).then_inc(yr_used, 1)

                first = static(i) and t == 0
                if front and not first:
                    dense_kv(i, u)
                if back:
                    scores(*prev, 0)
                    if not front:
                        wait(pe, o0_read, t - 1)
                        retention_out_0()
                if front and not first:
                    wait(pe, o1_read, t - 1)
                    dense(zb1[:, :], hh0, hl0, group(0)).then_inc(zb_ready, 1)
                if back:
                    turn_p(*prev, 0)
                    scores(*prev, 1)
                    if not front:
                        wait(pe, o1_read, t - 1)
                        retention_out_1()
                if front and not first:
                    wait(pe, ag_done, t)
                    wait(pe, fsq_done, t - 1)
                    dense(zb2[:, :], hh0, hl0, group(1), part=(0,), last=False)
                if back:
                    weigh(*prev, 0)
                if front and not first:
                    dense(zb2[:, :], hh0, hl0, group(1), part=(1, 2), first=False).then_inc(zb_ready, 1)
                if back:
                    turn_p(*prev, 1)
                    if front:
                        retention_out_0()
                    wait(pe, gate_scaled, t)
                    wait(pe, s_masked, 2 * t)
                    for b in range(4):
                        last = nc.tensor.transpose(s0_b[:, b * P:(b + 1) * P], a_gates[1 - u][:, b * P:(b + 1) * P], ident[:, :])
                    last.then_inc(gate_turned, 1)
                    weigh(*prev, 1)
                    if front:
                        retention_out_1()
                if front:
                    wait(pe, aq_hi, t + 1)
                    wait(pe, aq_lo, t + 1)
                    wait(pe, kv_done, t + 1)
                    wait(pe, pt0_done, 2 * t)
                    wait(pe, pt1_done, 2 * t)
                    for h in range(QH):
                        nc.tensor.transpose((t0_b, t1_b)[h // 4][:, (h % 4) * P:(h % 4 + 1) * P],
                                            aq_row[:, h, :, :].rearrange("p e d -> p (e d)").bitcast(F32), ident[:, :])
                    sources = [kv_rows[u]]
                    if static(i) and t == SAMPLE:
                        pe.wait_ge(cache_loaded, 6 * 16)
                        pe.wait_ge(newer_loaded, 3 * 16)
                        sources.append(kv_cache)
                    wait(pe, s_masked, 2 * t)
                    wait(pe, ak_lo, t)
                    for s, src in enumerate(sources):
                        for g in range(2):
                            last = nc.tensor.transpose(s1_b[:, (2 * s + g) * P:(2 * s + g + 1) * P],
                                                       src[:, g * P:(g + 1) * P], ident[:, :])
                    last.then_inc(qk_transposed, 1)
                if back:
                    wait(pe, ya_lo, t)
                    dense(zb0[:, :], yh, yl, group(2), chunks=range(4, 8), first=False).then_inc(o0_ready, 1)
                    dense(zb1[:, :], yh, yl, group(3), chunks=range(4, 8), first=False).then_inc(o1_ready, 1)

            phase_tiles(pe, slot_b, SAMPLE + 1)


def tables():
    import numpy as np
    f = np.float32
    inv = f(1) / np.power(10000.0, (np.arange(0, DK, 2, dtype=f) / f(DK)).astype(np.float64)).astype(f)
    row = np.arange((NT + 1) * P).astype(f)
    row[SAMPLE * P + HALF:] = SEQ + np.arange(HALF)
    ang = (row[:, None] * inv[None, :]).astype(np.float64)
    cos, sin = np.cos(ang), np.sin(ang)
    rope = np.concatenate([cos, -sin, sin], axis=1).astype(f).reshape(NT + 1, P, 192)
    p = np.arange(P)
    g = np.array(GAMMA)
    causal = (p[:, None] <= p[None, :]).astype(np.float64)
    decay = np.concatenate([causal * g[h] ** -(p[:, None] + 1.0) * DK ** -0.5 for h in range(RH)], axis=1).astype(f)
    qdec = np.concatenate([g[h] ** (p + 1.0) for h in range(RH)]).astype(f)[None, :]
    vdec = np.stack([g[h] ** (P - 1.0 - p) * DK ** -0.5 for h in range(RH)], axis=1).astype(f)
    key = np.arange(2 * P)[None, :]
    seen = np.where(p[:, None] < HALF, key < P + HALF, key >= HALF)
    mask = np.stack([np.where(seen, 0.0, MASKED), np.where(seen & (key >= P), 0.0, MASKED)], axis=1).astype(f)
    return {"rope_tab": rope, "ident_tab": np.eye(P, dtype=f), "decay_tab": decay, "qdec_tab": qdec, "vdec_tab": vdec,
            "mask_tab": mask}


_OUTS = [("y_prompt", (SEQ, D), (1, SEQ, D)), ("y_sample", (HALF, D), (1, HALF, D)),
         ("ret_prompt", (RH, DK, DK), (1, 1, RH, DK, DK)), ("k_prompt", (P, P), (1, 1, P, 2, HD)),
         ("v_prompt", (P, P), (1, 1, P, 2, HD)), ("ret_sample", (RH, DK, DK), (1, 1, RH, DK, DK)),
         ("k_sample", (P, P), (1, 1, P, 2, HD)), ("v_sample", (P, P), (1, 1, P, 2, HD))]
_SHAPES = {"x_prompt": (SEQ, D), "x_sample": (HALF, D), "c_prompt": (1, D), "c_sample": (1, D),
           "state_ret": (RH, DK, DK), "cache_k": (P, P), "cache_v": (P, P), "norm_g": (1, D), "w_ada": (D, 3 * D),
           "b_ada": (1, 3 * D), "w_in": (D, IN_W), "sink": (1, QH), "w_out": (D, D), "final_g": (1, D)}


def kernel(**inputs):
    import numpy as np
    import concourse.bacc as bacc
    from concourse.bass_utils import run_bass_kernel_spmd

    nc = bacc.Bacc("TRN2", target_bir_lowering=False, num_devices=1, dynamic_dma_scratch_size=1024)
    arrays, args = {}, []
    given = {n: np.ascontiguousarray(inputs[n]).reshape(s) for n, s in _SHAPES.items()}
    given.update(tables())
    for name, a in given.items():
        arrays["in_" + name] = a
        args.append(nc.dram_tensor("in_" + name, a.shape, F32, kind="ExternalInput").ap())
    for i, (name, shape, _) in enumerate(_OUTS):
        args.append(nc.dram_tensor(f"out_{i}", shape, F32, kind="ExternalOutput").ap())
    args.append(nc.dram_tensor("h_scratch", (NT + 1, P, D), F32, kind="Internal").ap())
    args.append(nc.dram_tensor("yr_scratch", (NT + 1, P, COLS), F32, kind="Internal").ap())
    args.append(nc.dram_tensor("gate_scratch", (2, D), F32, kind="Internal").ap())
    build_program(nc, *args)
    r = run_bass_kernel_spmd(nc, [arrays], core_ids=[0])
    return tuple(r.results[0][f"out_{i}"].reshape(full) for i, (_, _, full) in enumerate(_OUTS))
```

```python
from contextlib import ExitStack

import concourse.bass as bass
from concourse import mybir

F32 = mybir.dt.float32
F32R = mybir.dt.float32r
ALU = mybir.AluOpType
ACT = mybir.ActivationFunctionType

P = 128
D = 1024
KC = D // P
SEQ = 4096
NT = SEQ // P
SAMPLE = NT
HALF = P // 2
COLS = 512
RH = 4
DK = 128
HD = 64
QH = 8
IN_W = 3328
OFF_RQ, OFF_RK, OFF_RV, OFF_RG, OFF_AQ, OFF_KV, OFF_AG = 0, 512, 1024, 1536, 2048, 2560, 2816
KV = 256
NORM_EPS = 1e-6
GN_EPS = 1e-5
GAMMA = [1.0 - 2.0 ** (-5 - h) for h in range(RH)]
SCORE_SCALE = HD ** -0.5
MASKED = -1e30


def build_program(nc, x_prompt, x_sample, c_prompt, c_sample, state_ret, cache_k, cache_v, norm_g, w_ada,
                  b_ada, w_in, sink, w_out, final_g, rope_tab, ident_tab, decay_tab, qdec_tab, vdec_tab,
                  mask_tab, y_prompt, y_sample, ret_prompt, k_prompt, v_prompt, ret_sample, k_sample,
                  v_sample, xn_dram, q_dram, aq_dram, h_dram, yr_dram,
                  gate_dram):
    ctx = ExitStack()
    with ctx:
        def sb(name, shape, dt=F32, where=ctx):
            return where.enter_context(nc.sbuf_tensor(name, shape, dt))

        def sem(name):
            return ctx.enter_context(nc.semaphore(name))

        wh = sb("wh", [P, 4, KC, COLS], F32R)
        wl = sb("wl", [P, 4, KC, COLS], F32R)
        hf = sb("hf", [P, KC, P])
        hh0 = sb("hh0", [P, KC, P], F32R)
        hl0 = sb("hl0", [P, KC, P], F32R)
        xt0 = sb("xt0", [P, D])
        ident = sb("ident", [P, P])
        small = sb("small", [P, 40])
        neg_half = small[:, 0:8]
        ssq = small[:, 8:10]
        meansq = small[:, 10:11]
        rstd = small[:, 11:12]
        gn_var = small[:, 12:16]
        gn_rstd = small[:, 16:20]
        norm_eps = small[:, 20:21]
        gn_eps = small[:, 21:25]
        zero = small[:, 25:26]
        spare = small[:, 26:27]

        phase_a = ExitStack()
        stage23 = sb("stage23", [P, 2, 2048], F32, phase_a)
        stage01 = sb("stage01", [P, 2, 2048], F32, phase_a)
        hh1 = sb("hh1", [P, KC, P], F32R, phase_a)
        hl1 = sb("hl1", [P, KC, P], F32R, phase_a)
        xn = sb("xn", [P, D], F32, phase_a)
        rope = sb("rope", [P, 192], F32, phase_a)
        xp = sb("xp", [P, D], F32, phase_a)
        q_row = sb("q_row", [P, COLS], F32, phase_a)
        k_row = sb("k_row", [P, COLS], F32, phase_a)
        q_t = sb("q_t", [P, COLS], F32, phase_a)
        k_t = sb("k_t", [P, COLS], F32, phase_a)
        v_row = sb("v_row", [P, COLS], F32, phase_a)
        v_dec = sb("v_dec", [P, COLS], F32, phase_a)
        s_t = sb("s_t", [P, COLS], F32, phase_a)
        state = sb("state", [P, COLS], F32, phase_a)
        state_s = sb("state_s", [P, COLS], F32, phase_a)
        r_gate = sb("r_gate", [P, COLS], F32, phase_a)
        r_out = sb("r_out", [P, COLS], F32, phase_a)
        decay = sb("decay", [P, COLS], F32, phase_a)
        qdec = sb("qdec", [P, COLS], F32, phase_a)
        tiny_a = sb("tiny_a", [P, 176], F32, phase_a)
        vdec = tiny_a[:, 0:4]
        gn_stats = tiny_a[:, 4:28].rearrange("p (h s) -> p h s", h=RH)
        gn_mv = tiny_a[:, 28:36].rearrange("p (h s) -> p h s", h=RH)
        c_in = tiny_a[:, 36:52].rearrange("p (c k) -> p c k", c=2)
        c_th = tiny_a[:, 52:68].rearrange("p (c k) -> p c k", c=2)
        c_silu = tiny_a[:, 68:84].rearrange("p (k c) -> p k c", c=2)
        g_col = tiny_a[:, 84:92]
        b_col = tiny_a[:, 92:108]
        h_scale = tiny_a[:, 108:124].rearrange("p (k c) -> p k c", c=2)
        h_shift = tiny_a[:, 124:140].rearrange("p (k c) -> p k c", c=2)
        mod_rows = s_t
        c_wide = k_t[:, 0:KC * 32].rearrange("p (k c) -> p k c", k=KC)
        bias_rows = sb("bias_rows", [P, COLS], F32, phase_a)
        phase_a.close()

        wkvh = sb("wkvh", [P, KC, KV], F32R)
        wkvl = sb("wkvl", [P, KC, KV], F32R)
        p_t = sb("p_t", [P, 2, 4, P])
        s_row = sb("s_row", [P, 4, 2 * P])
        aq_f = sb("aq_f", [P, D])
        o_part = aq_f[:, 0:COLS]
        ya_f = aq_f[:, COLS:D]
        o_part1 = sb("o_part1", [P, COLS])
        yl = sb("yl", [P, KC, P], F32R)
        out_gate = sb("out_gate", [P, D])
        xt1 = sb("xt1", [P, D])
        yr_in = sb("yr_in", [P, COLS])
        yr_f = sb("yr_f", [P, 4, P])
        yh = sb("yh", [P, KC, P], F32R)
        aq_row = sb("aq_row", [P, QH, 2, HD], F32R)
        aq_flat = aq_row[:, :, :, :].rearrange("p h e d -> p (h e d)")
        kv_rows = [sb(f"kv_row{u}", [P, 3 * P]) for u in range(2)]
        v_prev = sb("v_prev", [P, P])
        aq_t = sb("aq_t", [P, QH, P], F32R)
        ak_h = sb("ak_h", [P, 2, 2 * P], F32R)
        ak_l = sb("ak_l", [P, 2, 2 * P], F32R)
        a_gates = [sb(f"a_gate{u}", [P, COLS]) for u in range(2)]
        fin_g = sb("fin_g", [P, D])
        mask = sb("mask", [P, 2, 2 * P])
        kv_cache = sb("kv_cache", [P, 3 * P])
        tiny_b = sb("tiny_b", [P, 64])
        neg_sink = tiny_b[:, 0:8]
        s_max = tiny_b[:, 8:16]
        s_bias = tiny_b[:, 16:24]
        sink_arg = tiny_b[:, 24:32]
        sink_exp = tiny_b[:, 32:40]
        row_sum = tiny_b[:, 40:48]
        den = tiny_b[:, 48:56]
        rden = tiny_b[:, 56:64]
        xts = [xt0, xt1]
        hhs, hls = [hh0, hh1], [hl0, hl1]
        stages = [stage01[:, 0], stage01[:, 1], stage23[:, 0], stage23[:, 1]]

        bank = [ctx.enter_context(nc.psum_tensor(f"bank{i}", [P, COLS], F32)) for i in range(8)]
        za0, za1, xb0, xb1, qs_b, ky_b, out_b, upd_b = bank
        swap = xb1
        x_banks = (xb0, xb1), (out_b, upd_b)
        zb0, zb1, zb2, s0_b, s1_b, t0_b, t1_b, pv_b = bank

        c_loaded, mod_loaded, tab_loaded, state_loaded = (sem(n) for n in ("c_loaded", "mod_loaded", "tab_loaded", "state_loaded"))
        stage_loaded = [sem(f"stage{n}_loaded") for n in range(4)]
        c_tanh, c_ready, const_set, ada_used, mod_rows_out, mod_transposed, mod_ready = (
            sem(n) for n in ("c_tanh", "c_ready", "const_set", "ada_used", "mod_rows_out",
                             "mod_transposed", "mod_ready"))
        w_hi_done, w_lo_done, gate_rows, gate_stored, b_rows_loaded = (
            sem(n) for n in ("w_hi_done", "w_lo_done", "gate_rows", "gate_stored", "b_rows_loaded"))
        x_loaded, rope_loaded, h_stored, yr_stored = (sem(n) for n in ("x_loaded", "rope_loaded", "h_stored", "yr_stored"))
        ssq_done, rstd_mean, rstd_done, xn_done, x_transposed, h_done, hi_done, lo_done = (
            sem(n) for n in ("ssq_done", "rstd_mean", "rstd_done", "xn_done", "x_transposed", "h_done", "hi_done", "lo_done"))
        za_ready = sem("za_ready")
        zq_read, q_done, qt_done, zk_read, k_done, k_transposed, kt_done = (
            sem(n) for n in ("zq_read", "q_done", "qt_done", "zk_read", "k_done", "k_transposed", "kt_done"))
        q_mul, k_mul = sem("q_mul"), sem("k_mul")
        vdec_done, v_done, rg_tanh, rg_done, s_ready, st_done, out_ready, upd_ready, state_done = (
            sem(n) for n in ("vdec_done", "v_done", "rg_tanh", "rg_done", "s_ready", "st_done", "out_ready",
                             "upd_ready", "state_done"))
        gn_stat_done, gn_mv_done, gn_var_done, gn_rstd_done, gn_done, yr_done = (
            sem(n) for n in ("gn_stat_done", "gn_mv_done", "gn_var_done", "gn_rstd_done", "gn_done", "yr_done"))
        state_out, wide_set, h_first = sem("state_out"), sem("wide_set"), sem("h_first")
        fixed_loaded, hb_loaded, yr_loaded, cache_loaded, newer_loaded, kv_out = (
            sem(n) for n in ("fixed_loaded", "hb_loaded", "yr_loaded", "cache_loaded", "newer_loaded", "kv_out"))
        xb_loaded = [sem(f"xb{u}_loaded") for u in range(2)]
        y_stored = [sem(f"y{u}_stored") for u in range(2)]
        b_set, b_split, bh_hi, zb_ready = (sem(n) for n in ("b_set", "b_split", "bh_hi", "zb_ready"))
        kv_done, aq_hi, aq_lo, qk_transposed, aqt_done, ak_hi, ak_lo, k_shifted, v_shifted = (
            sem(n) for n in ("kv_done", "aq_hi", "aq_lo", "qk_transposed", "aqt_done", "ak_hi", "ak_lo", "k_shifted",
                             "v_shifted"))
        sb_ready, s_masked, bias_done, sarg_done, exp_done, p_transposed, pt0_done, pt1_done, pv_ready = (
            sem(n) for n in ("sb_ready", "s_masked", "bias_done", "sarg_done", "exp_done", "p_transposed", "pt0_done",
                             "pt1_done", "pv_ready"))
        ag_tanh, ag_done, den_done, rden_done, gate_scaled, gate_turned, ya_done, ya_hi, ya_lo = (
            sem(n) for n in ("ag_tanh", "ag_done", "den_done", "rden_done", "gate_scaled", "gate_turned", "ya_done",
                             "ya_hi", "ya_lo"))
        gate_out, yr_turned = sem("gate_out"), sem("yr_turned")
        q_stored, q_loaded, q_turned = sem("q_stored"), sem("q_loaded"), sem("q_turned")
        aq_stored, aq_loaded, aq_turned = sem("aq_stored"), sem("aq_loaded"), sem("aq_turned")
        xn_stored, xp_loaded, x_turned = sem("xn_stored"), sem("xp_loaded"), sem("x_turned")
        yr_hi, yr_split, yr_used, o0_ready, o1_ready, o0_read, o1_read, x0_added, x1_added = (
            sem(n) for n in ("yr_hi", "yr_split", "yr_used", "o0_ready", "o1_ready", "o0_read", "o1_read", "x0_added",
                             "x1_added"))
        fsq0_done, fsq_done, fsum_done, fmean_done, frstd_done, fin_done = (
            sem(n) for n in ("fsq0_done", "fsq_done", "fsum_done", "fmean_done", "frstd_done", "fin_done"))
        block = ctx.enter_context(nc.Block())

        def wait(eng, s, value):
            if not (isinstance(value, int) and value <= 0):
                eng.wait_ge(s, value)

        def phase_a_over(eng):
            eng.wait_ge(yr_done, SAMPLE + 1)
            eng.wait_ge(yr_stored, 16 * (SAMPLE + 1))
            eng.wait_ge(state_out, 32)

        def heads(ap, n=RH):
            return ap.rearrange("p (h d) -> p h d", h=n)

        w_in_k = w_in.rearrange("(k p) n -> p k n", p=P)
        w_out_k = w_out.rearrange("(k p) n -> p k n", p=P)
        w_out_a = [w_out[COLS + g * KV:COLS + (g + 1) * KV, :].rearrange("(j d) n -> d j n", d=HD) for g in range(2)]
        w_ada_k = w_ada.rearrange("(p k) n -> p k n", k=KC)
        pieces = [("ada", w_ada_k[:, k, 0:2 * D]) for k in range(KC)]
        pieces += [("w", w_in_k[:, 4 * s:4 * s + 4, off:off + COLS], g, 4 * s)
                   for g, off in enumerate((OFF_RQ, OFF_RK, OFF_RV, OFF_RG)) for s in range(2)]
        pieces += [("gate", w_ada_k[:, 2 * s:2 * s + 2, 2 * D:3 * D]) for s in range(4)]
        N_EARLY = len(pieces)
        pieces += [("kv", w_in_k[:, :, OFF_KV:OFF_KV + KV])]
        pieces += [("w", w_in_k[:, 4 * s:4 * s + 4, off:off + COLS], g, 4 * s)
                   for g, off in ((0, OFF_AQ), (1, OFF_AG)) for s in range(2)]
        for g, off in ((2, 0), (3, COLS)):
            pieces += [("w", w_out_k[:, 0:4, off:off + COLS], g, 0)]
            pieces += [("w", [w[:, :, off:off + COLS] for w in w_out_a], g, 4)]
        slot_of, turn_of, turns = [], [], [0] * 4
        for n in range(len(pieces)):
            s = n % 4 if n < N_EARLY else n % 2
            slot_of.append(s)
            turns[s] += len(pieces[n][1]) if isinstance(pieces[n][1], list) else 1
            turn_of.append(turns[s])
        split_pieces = [n for n, p in enumerate(pieces) if p[0] in ("w", "kv")]
        split_no = {n: i for i, n in enumerate(split_pieces)}
        ada_no = {n: i for i, n in enumerate(n for n, p in enumerate(pieces) if p[0] in ("ada", "gate"))}

        def stage_view(n):
            ap = stages[slot_of[n]]
            if pieces[n][0] == "ada":
                return ap
            width = {"w": COLS, "gate": D, "kv": KV}[pieces[n][0]]
            return ap.rearrange("p (k n) -> p k n", n=width)

        def wait_piece_used(eng, n):
            if n in split_no:
                eng.wait_ge(w_lo_done, split_no[n] + 1)
            else:
                eng.wait_ge(ada_used, ada_no[n] + 1)

        def load_piece(eng, n):
            before = [m for m in range(n) if slot_of[m] == slot_of[n]]
            if before:
                wait_piece_used(eng, before[-1])
            if isinstance(pieces[n][1], list):
                for g, src in enumerate(pieces[n][1]):
                    eng.dma_start(stage_view(n)[g * HD:(g + 1) * HD], src).then_inc(stage_loaded[slot_of[n]], 16)
            else:
                eng.dma_start(stage_view(n), pieces[n][1]).then_inc(stage_loaded[slot_of[n]], 16)

        def arrived(eng, n):
            eng.wait_ge(stage_loaded[slot_of[n]], 16 * turn_of[n])

        def part_of(n, low):
            if pieces[n][0] == "kv":
                return (wkvl if low else wkvh)[:, :, :]
            g, k = pieces[n][2:]
            return (wl if low else wh)[:, g, k:k + 4, :]

        def free_of_phase_a(eng, n):
            if n > N_EARLY:
                eng.wait_ge(za_ready, 4 * SAMPLE + pieces[n][2] + 1)

        def split_hi(act, n):
            arrived(act, n)
            free_of_phase_a(act, n)
            nc.scalar.activation(part_of(n, False), stage_view(n), ACT.Copy).then_inc(w_hi_done, 1)

        def split_lo(dve, n):
            dve.wait_ge(w_hi_done, split_no[n] + 1)
            nc.vector.tensor_tensor(part_of(n, True), stage_view(n), part_of(n, False).bitcast(F32),
                                    ALU.subtract).then_inc(w_lo_done, 1)

        FIRST_W, FIRST_GATE = KC, KC + 8
        B_KV, B_Q, B_GATE, B_OUT, B_OUT_LATE = N_EARLY, N_EARLY + 1, N_EARLY + 3, N_EARLY + 5, N_EARLY + 7

        def phase_tiles(eng, slot, last):
            slot(0, 0)
            slot(0, 1)
            with eng.Fori(1, NT // 2 - 1) as i:
                slot(i, 0)
                slot(i, 1)
            for t in range(NT - 2, last + 1):
                slot(t // 2, t % 2)

        def key_rows(rows, e):
            return rows[:, 0:2 * P].rearrange("p (g e d) -> p g e d", g=2, e=2)[:, :, e, :]

        def cached(rows, half, newer):
            at = slice(HALF * half, HALF * (half + 1))
            of = slice(HALF * newer, HALF * (newer + 1))
            keys = cache_k[of, :].rearrange("p (g d) -> p g d", g=2)
            return [(key_rows(rows, e)[at], keys) for e in range(2)] + [(rows[at, 2 * P:3 * P], cache_v[of, :])]

        def by_pairs(ap):
            return ap.rearrange("p (g j d) -> p j g d", g=2, j=4)

        def static(i):
            return isinstance(i, int)

        def pe_turns(i, t):
            return static(i) and t in (0, SAMPLE)

        @block.sync
        def _(sp):
            for c, src in enumerate((c_prompt, c_sample)):
                sp.dma_start(c_in[:, c, :], src.rearrange("b (p k) -> (b p) k", k=KC)).then_inc(c_loaded, 16)
            sp.dma_start(ident[:, :], ident_tab).then_inc(c_loaded, 16)
            sp.dma_start(xt0[:, :], x_prompt[0:P, :]).then_inc(x_loaded, 16)
            for n in range(4):
                load_piece(sp, n)
            with nc.allow_non_contiguous_dma(reason="a few short columns"):
                sp.dma_start(g_col, norm_g.rearrange("a (k p) -> (a p) k", p=P)).then_inc(mod_loaded, 16)
                sp.dma_start(b_col, b_ada[:, 0:2 * D].rearrange("a (k p) -> (a p) k", p=P)).then_inc(mod_loaded, 16)
            for n in range(4, FIRST_W + 2):
                load_piece(sp, n)
            sp.dma_start(rope[:, :], rope_tab[0]).then_inc(rope_loaded, 16)
            sp.dma_start(decay[:, :], decay_tab).then_inc(tab_loaded, 16)
            sp.dma_start(qdec[:, :], qdec_tab.partition_broadcast(P)).then_inc(tab_loaded, 16)
            sp.dma_start(vdec, vdec_tab).then_inc(tab_loaded, 16)
            for n in range(FIRST_W + 2, FIRST_W + 4):
                load_piece(sp, n)
            sp.wait_ge(xn_done, 1)
            sp.dma_start(xt0[:, :], x_prompt[P:2 * P, :]).then_inc(x_loaded, 16)
            for n in range(FIRST_W + 4, FIRST_GATE):
                load_piece(sp, n)

            def load_blocks(dst, src, loaded):
                for j in range(4):
                    sp.dma_start(dst[32 * j:32 * (j + 1), :].rearrange("r (k i c) -> r k i c", i=4, c=32),
                                 src.rearrange("(i r) (k j c) -> r k i j c", r=32, j=4, c=32)[:, :, :, j, :]
                                 ).then_inc(loaded, 16)

            def slot(i, u):
                t = 2 * i + u
                if static(i) and t == SAMPLE:
                    for n in range(B_GATE, B_OUT):
                        load_piece(sp, n)
                    sp.wait_ge(h_stored, 16 * (SAMPLE + 1))
                    sp.wait_ge(lo_done, SAMPLE + 1)
                    sp.dma_start(hf[:, :, :].rearrange("p k r -> p (k r)"), h_dram[0]).then_inc(hb_loaded, 16)
                if not static(i) or 1 <= t < SAMPLE:
                    wait(sp, xn_done, t + 2)
                    sp.dma_start(xn_dram[t + 1], xn[:, :]).then_inc(xn_stored, 16)
                if static(i) and t == 0:
                    sp.dma_start(heads(state_s[:, :]), state_ret.rearrange("h k v -> k h v")).then_inc(state_loaded, 16)
                    sp.wait_ge(h_done, 1)
                    sp.wait_ge(h_first, 1)
                    sp.dma_start(h_dram[0], hf[:, :, :].rearrange("p k r -> p (k r)")).then_inc(h_stored, 16)
                if not static(i) or t + 2 < SAMPLE:
                    wait(sp, xn_done, t + 2)
                    sp.dma_start(xt0[:, :], x_prompt[bass.ts(t + 2, P), :]).then_inc(x_loaded, 16)
                if not static(i) or 1 <= t < SAMPLE:
                    wait(sp, xn_stored, 16 * t)
                    load_blocks(xp, xn_dram[t + 1], xp_loaded)
                if not pe_turns(i, t) and (not static(i) or t < SAMPLE):
                    wait(sp, q_done, t + 1)
                    sp.dma_start(q_dram[t], q_row[:, :]).then_inc(q_stored, 16)
                    wait(sp, q_stored, 16 * t)
                    load_blocks(q_row, q_dram[t], q_loaded)
                if static(i) and t + 2 == SAMPLE:
                    sp.wait_ge(b_set, 1)
                    sp.dma_start(xt0[HALF:P, :], x_sample).then_inc(x_loaded, 16)
                if not static(i) or t + 1 <= SAMPLE:
                    wait(sp, h_done, t + 2)
                    sp.dma_start(h_dram[t + 1], hf[:, :, :].rearrange("p k r -> p (k r)")).then_inc(h_stored, 16)
                    wait(sp, zk_read, t + 1)
                    sp.dma_start(rope[:, :], rope_tab[t + 1]).then_inc(rope_loaded, 16)
                if static(i) and t == SAMPLE + 1:
                    sp.wait_ge(b_split, 1)
                    sp.dma_start(hf[:, :, :].rearrange("p k r -> p (k r)"), h_dram[1]).then_inc(hb_loaded, 16)
                if not static(i) or t >= 1:
                    wait(sp, yr_done, t)
                    sp.dma_start(yr_dram[t - 1], r_out[:, :]).then_inc(yr_stored, 16)
                if static(i) and t == 0:
                    for n in range(FIRST_GATE, N_EARLY):
                        load_piece(sp, n)
                    for j in range(2):
                        sp.dma_start(bias_rows[32 * j:32 * j + 2, :],
                                     b_ada[:, 2 * D + j * COLS:2 * D + (j + 1) * COLS].partition_broadcast(2)
                                     ).then_inc(b_rows_loaded, 16)
                if static(i) and t == 1:
                    sp.wait_ge(gate_rows, 1)
                    for j in range(2):
                        sp.dma_start(gate_dram[:, j * COLS:(j + 1) * COLS], bias_rows[32 * j:32 * j + 2, :]
                                     ).then_inc(gate_stored, 16)
                    for n in range(B_KV, B_Q + 1):
                        load_piece(sp, n)
                if static(i) and t == NT - 2:
                    load_piece(sp, B_Q + 1)
                if static(i) and t == SAMPLE:
                    sp.wait_ge(state_done, NT)
                    sp.dma_start(ret_prompt.rearrange("h k v -> k h v"), heads(state[:, :])).then_inc(state_out, 16)
                    for n in range(B_OUT, B_OUT_LATE):
                        load_piece(sp, n)

            phase_tiles(sp, slot, SAMPLE + 1)
            sp.wait_ge(state_done, NT + 1)
            sp.dma_start(ret_sample.rearrange("h k v -> k h v"), heads(state_s[:, :])).then_inc(state_out, 16)

            for n in range(B_OUT_LATE, len(pieces)):
                load_piece(sp, n)
            phase_a_over(sp)
            sp.wait_ge(gate_stored, 32)
            load_blocks(yr_in, yr_dram[0], yr_loaded)
            sp.dma_start(mask[:, :, :], mask_tab).then_inc(fixed_loaded, 16)
            with nc.allow_non_contiguous_dma(reason="eight sinks, in the heads' order of the pairs"):
                for g in range(2):
                    sp.dma_start(neg_sink.rearrange("p (j g) -> p j g", g=2)[:, :, g],
                                 sink[:, 4 * g:4 * g + 4].partition_broadcast(P)).then_inc(fixed_loaded, 16)
            sp.dma_start(out_gate[:, :], gate_dram[0:1, :].partition_broadcast(P)).then_inc(fixed_loaded, 16)
            sp.dma_start(fin_g[:, :], final_g.partition_broadcast(P)).then_inc(fixed_loaded, 16)

            def slot_b(i, u):
                t = 2 * i + u
                front = not static(i) or t <= SAMPLE
                if not static(i) or t >= 2:
                    wait(sp, fin_done, t - 1)
                    if static(i) and t - 2 == SAMPLE:
                        sp.dma_start(y_sample, xts[u][HALF:P, :]).then_inc(y_stored[u], 16)
                    else:
                        sp.dma_start(y_prompt[bass.ts(t - 2, P), :], xts[u][:, :]).then_inc(y_stored[u], 16)
                if static(i) and t == SAMPLE + 1:
                    sp.wait_ge(o1_read, NT)
                    sp.dma_start(out_gate[:, :], gate_dram[1:2, :].partition_broadcast(P)).then_inc(fixed_loaded, 16)
                if front:
                    if not (static(i) and t == 0):
                        wait(sp, yr_turned, t)
                        load_blocks(yr_in, yr_dram[t], yr_loaded)
                    wait(sp, y_stored[u], 16 * i)
                    if static(i) and t == SAMPLE:
                        wait(sp, pv_ready, 2 * (t - 1))
                        wait(sp, v_shifted, t - 1)
                        for dst, src in cached(kv_rows[u], 0, 1):
                            sp.dma_start(dst, src).then_inc(newer_loaded, 16)
                        sp.wait_ge(b_set, 3)
                        sp.dma_start(xts[u][HALF:P, :], x_sample).then_inc(xb_loaded[u], 16)
                    else:
                        sp.dma_start(xts[u][:, :], x_prompt[bass.ts(t, P), :]).then_inc(xb_loaded[u], 16)
                if not static(i) or 1 <= t < SAMPLE:
                    wait(sp, b_split, t + 1)
                    sp.dma_start(hf[:, :, :].rearrange("p k r -> p (k r)"), h_dram[t + 1]).then_inc(hb_loaded, 16)
                if front and not pe_turns(i, t):
                    wait(sp, aq_lo, t + 1)
                    sp.dma_start(aq_dram[t], aq_flat.bitcast(F32)).then_inc(aq_stored, 16)
                    wait(sp, aq_stored, 16 * t)
                    load_blocks(aq_flat.bitcast(F32), aq_dram[t], aq_loaded)
                if static(i) and t == 0:
                    for half in range(2):
                        for dst, src in cached(kv_cache, half, 0):
                            sp.dma_start(dst, src).then_inc(cache_loaded, 16)
                if static(i) and t in (NT - 1, SAMPLE):
                    sp.wait_ge(kv_done, t + 1)
                    if t == SAMPLE:
                        sp.wait_ge(newer_loaded, 3 * 16)
                    k_new, v_new = (k_prompt, v_prompt) if t == NT - 1 else (k_sample, v_sample)
                    sp.dma_start(k_new.rearrange("p (g d) -> p g d", g=2), key_rows(kv_rows[u], 0)).then_inc(kv_out, 16)
                    sp.dma_start(v_new, kv_rows[u][:, 2 * P:3 * P]).then_inc(kv_out, 16)

            phase_tiles(sp, slot_b, SAMPLE + 2)
            sp.wait_ge(kv_out, 64)
            sp.wait_ge(y_stored[0], 16 * (NT // 2 + 1))
            sp.wait_ge(y_stored[1], 16 * (NT // 2))
            sp.wait_ge(state_out, 32)

        @block.gpsimd
        def _(pool):
            nc.gpsimd.memset(c_wide[:, :, :], 0.0).then_inc(wide_set, 1)
            nc.gpsimd.memset(neg_half, -0.5)
            nc.gpsimd.memset(norm_eps, NORM_EPS)
            nc.gpsimd.memset(gn_eps, GN_EPS)
            nc.gpsimd.memset(zero, 0.0).then_inc(const_set, 1)
            nc.gpsimd.memset(state[:, :], 0.0).then_inc(const_set, 1)

            def prep(i, u):
                t = 2 * i + u
                wait(pool, ssq_done, t + 1)
                nc.gpsimd.tensor_tensor(meansq, ssq[:, 0:1], norm_eps, ALU.add).then_inc(rstd_mean, 1)
                wait(pool, rstd_mean, t + 1)
                wait(pool, xn_done, t)
                nc.gpsimd.tensor_tensor(rstd, meansq, neg_half[:, 0:1], ALU.pow).then_inc(rstd_done, 1)

            def slot(i, u):
                t = 2 * i + u
                if not static(i) or t + 1 <= SAMPLE:
                    prep(i + (u + 1) // 2, (u + 1) % 2)
                if not static(i) or t >= 1:
                    wait(pool, gn_mv_done, t)
                    wait(pool, gn_done, t - 1)
                    nc.gpsimd.tensor_tensor(gn_var, gn_mv[:, :, 1], gn_eps, ALU.add).then_inc(gn_var_done, 1)
                    wait(pool, gn_var_done, t)
                    nc.gpsimd.tensor_tensor(gn_rstd, gn_var, neg_half[:, 0:4], ALU.pow).then_inc(gn_rstd_done, 1)
                if static(i) and t == NT - 2:
                    pool.wait_ge(xn_done, NT)
                    nc.gpsimd.memset(xt0[0:HALF, :], 0.0).then_inc(b_set, 1)

            pool.wait_ge(const_set, 2)
            prep(0, 0)
            phase_tiles(pool, slot, SAMPLE + 1)

            phase_a_over(pool)
            for ak in (ak_h, ak_l):
                nc.gpsimd.tensor_tensor(ak[:, :, 0:P], zero.unsqueeze(1).to_broadcast([P, 2, P]),
                                        zero.unsqueeze(1).to_broadcast([P, 2, P]), ALU.add)
            nc.gpsimd.memset(v_prev[:, :], 0.0).then_inc(b_set, 1)

            def slot_b(i, u):
                t = 2 * i + u
                front = not static(i) or t <= SAMPLE
                back = not static(i) or 1 <= t <= SAMPLE + 1
                if front and (not static(i) or 1 <= t < SAMPLE):
                    wait(pool, sb_ready, 2 * t)
                    wait(pool, ak_hi, t)
                    wait(pool, ak_lo, t)
                    for ak in (ak_h, ak_l):
                        last = nc.gpsimd.tensor_tensor(ak[:, :, 0:P], ak[:, :, P:2 * P].bitcast(F32),
                                                       zero.unsqueeze(1).to_broadcast([P, 2, P]), ALU.add)
                    last.then_inc(k_shifted, 1)
                if front and (not static(i) or t >= 1):
                    wait(pool, pv_ready, 2 * t)
                    if static(i) and t == SAMPLE:
                        pool.wait_ge(cache_loaded, 6 * 16)
                        nc.gpsimd.tensor_copy(v_prev[:, :], kv_cache[:, 2 * P:3 * P]).then_inc(v_shifted, 1)
                    else:
                        nc.gpsimd.tensor_tensor(v_prev[:, :], kv_rows[1 - u][:, 2 * P:3 * P], zero.to_broadcast([P, P]),
                                                ALU.add).then_inc(v_shifted, 1)
                if static(i) and t == SAMPLE:
                    pool.wait_ge(y_stored[0], 16 * (NT // 2))
                    nc.gpsimd.memset(xt0[0:HALF, :], 0.0).then_inc(b_set, 1)
                if back:
                    wait(pool, fsq_done, t)
                    wait(pool, fin_done, t - 1)
                    nc.gpsimd.tensor_tensor(meansq, ssq[:, 0:1], ssq[:, 1:2], ALU.add).then_inc(fsum_done, 1)
                    wait(pool, fsum_done, t)
                    nc.gpsimd.tensor_tensor(meansq, meansq, norm_eps, ALU.add).then_inc(fmean_done, 1)
                    wait(pool, fmean_done, t)
                    nc.gpsimd.tensor_tensor(rstd, meansq, neg_half[:, 0:1], ALU.pow).then_inc(frstd_done, 1)

            phase_tiles(pool, slot_b, SAMPLE + 2)

        @block.scalar
        def _(act):
            act.wait_ge(c_loaded, 48)
            nc.scalar.activation(c_th, c_in, ACT.Tanh, scale=0.5).then_inc(c_tanh, 1)

            def square(i, u):
                t = 2 * i + u
                wait(act, x_loaded, 16 * (t + 1))
                if static(i) and 1 <= t <= 2:
                    act.wait_ge(x_transposed, t)
                wait(act, rstd_mean, t)
                nc.scalar.activation(xn[:, :], xt0[:, :], ACT.Square, scale=D ** -0.5, accum_out=ssq[:, 0:1]).then_inc(ssq_done, 1)

            def modulate(i, u, sample=False, chunks=range(KC)):
                t = 2 * i + u
                if static(i) and t <= 1:
                    act.wait_ge(x_transposed, t + 1)
                else:
                    wait(act, x_turned, t - 1)
                wait(act, h_stored, 16 * t)
                wait(act, lo_done, t)
                c, lo = (1, HALF) if sample else (0, 0)
                if sample:
                    nc.scalar.activation(hf[:, :, 0:HALF], heads(xn[:, :], KC)[:, :, 0:HALF], ACT.Copy)
                for k in chunks:
                    if static(i) and t <= 1:
                        b, at = x_banks[t][k // 4], (k % 4) * P
                    else:
                        b, at = xn, k * P
                    src = b[:, at + lo:at + P]
                    last = nc.scalar.activation(hf[:, k, lo:P], src, ACT.Identity, bias=h_shift[:, k, c:c + 1],
                                                scale=h_scale[:, k, c:c + 1])
                last.then_inc(h_done, 1)

            def split_hb(i, u):
                t = 2 * i + u
                wait(act, hb_loaded, 16 * (t + 1))
                if static(i) and t == 0:
                    act.wait_ge(za_ready, 4 * (SAMPLE + 1))
                wait(act, zb_ready, 3 * t)
                nc.scalar.activation(hh0[:, :, :], hf[:, :, :], ACT.Copy).then_inc(bh_hi, 1)

            def slot(i, u):
                t = 2 * i + u
                front = not static(i) or t <= SAMPLE
                back = not static(i) or t >= 1
                nxt = (i + (u + 1) // 2, (u + 1) % 2)
                if not static(i) or t + 1 <= SAMPLE:
                    square(*nxt)
                    if static(i) and t == 0:
                        for n in range(FIRST_W + 4, FIRST_GATE):
                            split_hi(act, n)
                    modulate(*nxt, sample=static(i) and t + 1 == SAMPLE)
                if static(i) and t == NT - 2:
                    split_hi(act, B_KV)
                if static(i) and t == SAMPLE:
                    for n in range(B_Q, B_OUT):
                        split_hi(act, n)
                if front:
                    wait(act, vdec_done, t + 1)
                    wait(act, out_ready, t)
                    nc.scalar.activation(v_row[:, :], za0[:, :], ACT.Copy).then_inc(v_done, 1)
                if static(i) and t == SAMPLE + 1:
                    split_hb(0, 0)
                    for n in range(B_OUT, B_OUT_LATE):
                        split_hi(act, n)
                if front:
                    wait(act, k_transposed, t + 1)
                    wait(act, s_ready, t)
                    nc.scalar.activation(k_t[:, :], ky_b[:, :], ACT.Copy).then_inc(kt_done, 1)
                    wait(act, za_ready, 4 * t + 4)
                    wait(act, yr_done, t)
                    nc.scalar.activation(r_gate[:, :], za1[:, :], ACT.Tanh, scale=0.5).then_inc(rg_tanh, 1)

            square(0, 0)
            split_hi(act, FIRST_W)
            act.wait_ge(mod_ready, 1)
            modulate(0, 0, chunks=range(KC // 2))
            for n in range(FIRST_W + 1, FIRST_W + 4):
                split_hi(act, n)
            phase_tiles(act, slot, SAMPLE + 1)

            phase_a_over(act)

            def softmax(i, u, half):
                t = 2 * i + u
                n = 2 * t + half + 1
                wait(act, bias_done, n)
                for j in range(4):
                    h = 4 * half + j
                    nc.scalar.activation(s_row[:, j, :], s_row[:, j, :], ACT.Exp, bias=s_bias[:, h:h + 1],
                                         scale=SCORE_SCALE, accum_out=row_sum[:, h:h + 1])
                wait(act, sarg_done, n)
                nc.scalar.activation(sink_exp[:, 4 * half:4 * half + 4], sink_arg[:, 4 * half:4 * half + 4],
                                     ACT.Exp).then_inc(exp_done, 1)

            def p_out(i, u, half):
                t = 2 * i + u
                wait(act, p_transposed, 2 * t + half + 1)
                wait(act, pv_ready, 2 * t + half)
                nc.scalar.activation(p_t[:, 0].rearrange("p b r -> p (b r)"), t0_b[:, :], ACT.Copy).then_inc(pt0_done, 1)

            def slot_b(i, u):
                t = 2 * i + u
                front = not static(i) or t <= SAMPLE
                back = not static(i) or 1 <= t <= SAMPLE + 1
                prev = (i + (u - 1) // 2, (u + 1) % 2)
                if front:
                    wait(act, zb_ready, 3 * t + 1)
                    wait(act, pv_ready, 2 * (t - 1))
                    wait(act, v_shifted, t - 1)
                    lo = HALF if static(i) and t == SAMPLE else 0
                    keys = zb0[lo:P, 0:P].rearrange("p (g d) -> p g d", g=2).unsqueeze(2).to_broadcast([P - lo, 2, 2, HD])
                    nc.scalar.activation(kv_rows[u][lo:P, 0:2 * P].rearrange("p (g e d) -> p g e d", g=2, e=2), keys, ACT.Copy)
                    nc.scalar.activation(kv_rows[u][lo:P, 2 * P:3 * P], zb0[lo:P, P:2 * P], ACT.Copy).then_inc(kv_done, 1)
                if back:
                    softmax(*prev, 0)
                if front:
                    wait(act, zb_ready, 3 * t + 2)
                    wait(act, qk_transposed, t)
                    wait(act, aqt_done, t)
                    nc.scalar.activation(aq_row[:, :, 0, :].rearrange("p (j g) d -> p j g d", g=2), by_pairs(zb1[:, :]),
                                         ACT.Copy).then_inc(aq_hi, 1)
                if back:
                    p_out(*prev, 0)
                    softmax(*prev, 1)
                if front:
                    wait(act, zb_ready, 3 * t + 3)
                    wait(act, ya_done, t - 1)
                    nc.scalar.activation(a_gates[u][:, :].rearrange("p (j g d) -> p j g d", j=4, g=2), by_pairs(zb2[:, :]),
                                         ACT.Tanh, scale=0.5).then_inc(ag_tanh, 1)
                if not static(i) or t + 1 <= SAMPLE:
                    split_hb(i + (u + 1) // 2, (u + 1) % 2)
                if static(i) and t == 0:
                    split_hi(act, B_OUT_LATE)
                if back:
                    p_out(*prev, 1)
                    wait(act, gate_turned, t)
                    nc.scalar.activation(a_gates[1 - u][:, :], s0_b[:, :], ACT.Copy).then_inc(gate_out, 1)
                    wait(act, ya_done, t)
                    wait(act, o1_ready, t - 1)
                    nc.scalar.activation(yh[:, 4:8, :].rearrange("p k r -> p (k r)"), ya_f[:, :], ACT.Copy).then_inc(ya_hi, 1)
                if front:
                    wait(act, qk_transposed, t + 1)
                    wait(act, sb_ready, 2 * t)
                    if static(i) and t == SAMPLE:
                        nc.scalar.activation(ak_h[:, :, 0:P], s1_b[:, 2 * P:4 * P].rearrange("p (g r) -> p g r", g=2), ACT.Copy)
                    else:
                        wait(act, k_shifted, t)
                    nc.scalar.activation(ak_h[:, :, P:2 * P], s1_b[:, 0:2 * P].rearrange("p (g r) -> p g r", g=2),
                                         ACT.Copy).then_inc(ak_hi, 1)
                    if pe_turns(i, t):
                        for b, src in enumerate((t0_b, t1_b)):
                            last = nc.scalar.activation(aq_t[:, 4 * b:4 * b + 4, :].rearrange("p k r -> p (k r)"), src[:, :],
                                                        ACT.Copy)
                        last.then_inc(aqt_done, 1)
                    else:
                        wait(act, aq_turned, t)
                        nc.scalar.activation(aq_t[:, :, :].rearrange("p k r -> p (k r)"), aq_f[:, :], ACT.Copy).then_inc(aqt_done, 1)
                if static(i) and t == 0:
                    split_hi(act, B_OUT_LATE + 1)
                if back:
                    xr = xts[1 - u]
                    wait(act, x0_added, t)
                    wait(act, ag_done, t + 1 if front else t)
                    wait(act, fsum_done, t - 1)
                    nc.scalar.activation(zb2[:, :], xr[:, 0:COLS], ACT.Square, scale=D ** -0.5, accum_out=ssq[:, 0:1]).then_inc(fsq0_done, 1)
                    wait(act, x1_added, t)
                    wait(act, fsq0_done, t)
                    nc.scalar.activation(zb2[:, :], xr[:, COLS:D], ACT.Square, scale=D ** -0.5, accum_out=ssq[:, 1:2]).then_inc(fsq_done, 1)

            phase_tiles(act, slot_b, SAMPLE + 1)

        @block.vector
        def _(dve):
            V = nc.vector
            dve.wait_ge(c_tanh, 1)
            dve.wait_ge(wide_set, 1)
            cT = c_in.rearrange("p c k -> p k c")
            tT = c_th.rearrange("p c k -> p k c")
            V.scalar_tensor_tensor(c_silu, tT, 1.0, cT, ALU.add, ALU.mult).then_inc(c_ready, 1)
            dve.wait_ge(c_ready, 1)
            V.tensor_scalar(c_wide[:, :, 0:2], c_silu, 0.5, None, ALU.mult)
            V.tensor_scalar(c_silu, c_silu, 0.5, None, ALU.mult).then_inc(c_ready, 1)

            def normalise(i, u):
                t = 2 * i + u
                wait(dve, rstd_done, t + 1)
                V.tensor_scalar(xn[:, :], xt0[:, :], rstd, None, ALU.mult).then_inc(xn_done, 1)

            def turn_x(i, u):
                t = 2 * i + u
                wait(dve, xp_loaded, 4 * 16 * (t - 1))
                V.transpose(xn[:, :], xp[:, :]).then_inc(x_turned, 1)

            def split_h(i, u):
                t = 2 * i + u
                wait(dve, h_done, t + 1)
                wait(dve, za_ready, 4 * (t - 1))
                V.tensor_copy(hhs[u][:, :, :], hf[:, :, :]).then_inc(hi_done, 1)
                wait(dve, hi_done, t + 1)
                V.tensor_tensor(hls[u][:, :, :], hf[:, :, :], hhs[u][:, :, :].bitcast(F32), ALU.subtract).then_inc(lo_done, 1)

            def split_hb(i, u):
                t = 2 * i + u
                wait(dve, bh_hi, t + 1)
                V.tensor_tensor(hl0[:, :, :], hf[:, :, :], hh0[:, :, :].bitcast(F32), ALU.subtract).then_inc(b_split, 1)

            def rotate(t, z, row, zread, mul, done):
                z4 = z[:, :].rearrange("p (h e d) -> p h e d", h=RH, e=2)
                sin = rope[:, 64:192].rearrange("p (e d) -> p e d", e=2).unsqueeze(1).to_broadcast([P, RH, 2, 64])
                cos = rope[:, 0:64].unsqueeze(1).to_broadcast([P, 2 * RH, 64])
                V.tensor_tensor(swap[:, :].rearrange("p (h e d) -> p h e d", h=RH, e=2), z4[:, :, ::-1, :], sin,
                                ALU.mult).then_inc(mul, 1)
                V.tensor_tensor(heads(row[:, :], 8), heads(z[:, :], 8), cos, ALU.mult).then_inc(zread, 1)
                wait(dve, mul, t + 1)
                wait(dve, zread, t + 1)
                V.tensor_tensor(row[:, :], row[:, :], swap[:, :], ALU.add).then_inc(done, 1)

            def slot(i, u):
                t = 2 * i + u
                front = not static(i) or t <= SAMPLE
                back = not static(i) or t >= 1
                nxt = (i + (u + 1) // 2, (u + 1) % 2)
                more = not static(i) or t + 1 <= SAMPLE
                if more:
                    normalise(*nxt)
                if front:
                    wait(dve, za_ready, 4 * t + 1)
                    wait(dve, rope_loaded, 16 * (t + 1))
                    wait(dve, q_turned, t)
                    wait(dve, k_done, t)
                    rotate(t, za0, q_row, zq_read, q_mul, q_done)
                if static(i) and t == SAMPLE:
                    for n in range(B_Q, B_GATE):
                        split_lo(dve, n)
                if static(i) and t == SAMPLE + 1:
                    split_hb(0, 0)
                if static(i) and t == 0:
                    for n in range(FIRST_W + 4, FIRST_W + 6):
                        split_lo(dve, n)
                if back:
                    wait(dve, out_ready, t)
                    wait(dve, gn_mv_done, t - 1)
                    for h in range(RH):
                        last = V.bn_stats(gn_stats[:, h, :], out_b[:, h * DK:(h + 1) * DK])
                    last.then_inc(gn_stat_done, 1)
                    wait(dve, gn_stat_done, t)
                    wait(dve, gn_var_done, t - 1)
                    wait(dve, upd_ready, t)
                    st = state_s if static(i) and t - 1 == SAMPLE else state
                    for h in range(RH):
                        cols = slice(h * DK, (h + 1) * DK)
                        last = V.scalar_tensor_tensor(st[:, cols], st[:, cols], GAMMA[h] ** P, upd_b[:, cols], ALU.mult, ALU.add)
                    last.then_inc(state_done, 1)
                    for h in range(RH):
                        last = V.bn_aggr(gn_mv[:, h, :], gn_stats[:, h, :])
                    last.then_inc(gn_mv_done, 1)
                if more and not (static(i) and t == 0):
                    turn_x(*nxt)
                if back:
                    wait(dve, gn_rstd_done, t)
                    wait(dve, yr_stored, 16 * (t - 1))
                    for h in range(RH):
                        cols = slice(h * DK, (h + 1) * DK)
                        last = V.tensor_scalar(r_out[:, cols], out_b[:, cols], gn_mv[:, h, 0:1], gn_rstd[:, h:h + 1],
                                               ALU.subtract, ALU.mult)
                    last.then_inc(gn_done, 1)
                    wait(dve, gn_done, t)
                    wait(dve, rg_done, t)
                    V.scalar_tensor_tensor(r_out[:, :], r_out[:, :], 0.5, r_gate[:, :], ALU.mult, ALU.mult).then_inc(yr_done, 1)
                if front:
                    wait(dve, za_ready, 4 * t + 2)
                    wait(dve, upd_ready, t)
                    wait(dve, q_done, t + 1)
                    rotate(t, za1, k_row, zk_read, k_mul, k_done)
                    if static(i) and t == 0:
                        dve.wait_ge(tab_loaded, 48)
                    wait(dve, out_ready, t)
                    if pe_turns(i, t):
                        wait(dve, q_turned, t + 1)
                        V.tensor_tensor(q_t[:, :], qs_b[:, :], qdec[:, :], ALU.mult).then_inc(qt_done, 1)
                    else:
                        wait(dve, q_loaded, 4 * 16 * t)
                        V.transpose(q_t[:, :], q_row[:, :]).then_inc(q_turned, 1)
                        wait(dve, q_turned, t + 1)
                        V.tensor_tensor(q_t[:, :], q_t[:, :], qdec[:, :], ALU.mult).then_inc(qt_done, 1)
                if static(i) and t == 0:
                    for n in range(FIRST_W + 6, FIRST_GATE):
                        split_lo(dve, n)
                if static(i) and t == NT - 2:
                    split_lo(dve, B_KV)
                if more:
                    split_h(*nxt)
                if static(i) and t == 0:
                    dve.wait_ge(state_loaded, 16)
                    for h in range(RH):
                        V.tensor_scalar(state_s[:, h * DK:(h + 1) * DK], state_s[:, h * DK:(h + 1) * DK],
                                        GAMMA[h] ** -HALF, None, ALU.mult)
                if front:
                    wait(dve, za_ready, 4 * t + 3)
                    V.tensor_tensor(heads(v_dec[:, :]), heads(za0[:, :]), vdec.unsqueeze(2).to_broadcast([P, RH, DK]),
                                    ALU.mult).then_inc(vdec_done, 1)
                    if static(i) and t == SAMPLE:
                        for n in range(B_GATE, B_OUT):
                            split_lo(dve, n)
                    wait(dve, s_ready, t + 1)
                    wait(dve, out_ready, t)
                    V.tensor_tensor(s_t[:, :], qs_b[:, :], decay[:, :], ALU.mult).then_inc(st_done, 1)
                    wait(dve, rg_tanh, t + 1)
                    V.scalar_tensor_tensor(r_gate[:, :], r_gate[:, :], 1.0, za1[:, :], ALU.add, ALU.mult).then_inc(rg_done, 1)
                if static(i) and t == SAMPLE + 1:
                    for n in range(B_OUT, B_OUT_LATE):
                        split_lo(dve, n)
                if static(i) and t == 1:
                    dve.wait_ge(ada_used, KC + 4)
                    dve.wait_ge(b_rows_loaded, 32)
                    for j in range(2):
                        rows = slice(32 * j, 32 * j + 2)
                        last = V.tensor_tensor(bias_rows[rows, :], xb0[rows, :], bias_rows[rows, :], ALU.add)
                    last.then_inc(gate_rows, 1)

            normalise(0, 0)
            dve.wait_ge(ada_used, KC)
            V.tensor_copy(mod_rows[:, :], out_b[:, :]).then_inc(mod_rows_out, 1)
            dve.wait_ge(mod_transposed, 1)
            dve.wait_ge(mod_loaded, 32)
            turned = upd_b[:, :].rearrange("p (b r) -> p b r", b=4)
            for j in range(4):
                dst = (h_shift if j < 2 else h_scale)[:, 4 * (j % 2):4 * (j % 2) + 4, :]
                bias = b_col[:, 4 * j:4 * j + 4].unsqueeze(2).to_broadcast([P, 4, 2])
                last = V.tensor_tensor(dst, turned[:, :, 32 * j:32 * j + 2], bias, ALU.add)
            last.then_inc(mod_rows_out, 1)
            dve.wait_ge(mod_rows_out, 2)
            V.scalar_tensor_tensor(h_scale, h_scale, 1.0, g_col.unsqueeze(2).to_broadcast([P, KC, 2]), ALU.add,
                                   ALU.mult).then_inc(mod_ready, 1)
            dve.wait_ge(mod_ready, 1)
            dve.wait_ge(x_transposed, 1)
            for k in range(KC // 2, KC):
                last = V.tensor_scalar(hf[:, k, :], xb1[:, (k % 4) * P:(k % 4 + 1) * P], h_scale[:, k, 0:1],
                                       h_shift[:, k, 0:1], ALU.mult, ALU.add)
            last.then_inc(h_first, 1)
            dve.wait_ge(h_first, 1)
            split_h(0, 0)
            for n in range(FIRST_W, FIRST_W + 4):
                split_lo(dve, n)
            phase_tiles(dve, slot, SAMPLE + 1)

            phase_a_over(dve)

            def mask_max(i, u, half):
                t = 2 * i + u
                n = 2 * t + half + 1
                wait(dve, p_transposed, n - 1)
                wait(dve, sb_ready, n)
                wait(dve, sarg_done, n - 1)
                m = mask[:, 1 if static(i) and t == 0 else 0, :]
                V.memset(spare, 0.0)
                for j in range(4):
                    h = 4 * half + j
                    src = (s0_b, s1_b)[j // 2][:, (j % 2) * 2 * P:(j % 2 + 1) * 2 * P]
                    last = V.tensor_tensor_reduce(out=s_row[:, j, :], in0=src, in1=m, scale=1.0, scalar=MASKED,
                                                  op0=ALU.add, op1=ALU.max, accum_out=s_max[:, h:h + 1])
                last.then_inc(s_masked, 1)
                hs = slice(4 * half, 4 * half + 4)
                wait(dve, s_masked, n)
                wait(dve, exp_done, n - 2)
                V.scalar_tensor_tensor(s_bias[:, hs], s_max[:, hs], -SCORE_SCALE, neg_sink[:, hs], ALU.mult,
                                       ALU.min).then_inc(bias_done, 1)
                wait(dve, bias_done, n)
                V.tensor_tensor(sink_arg[:, hs], s_bias[:, hs], neg_sink[:, hs], ALU.subtract).then_inc(sarg_done, 1)

            def p_out(i, u, half):
                t = 2 * i + u
                wait(dve, p_transposed, 2 * t + half + 1)
                wait(dve, pv_ready, 2 * t + half)
                V.tensor_copy(p_t[:, 1].rearrange("p b r -> p (b r)"), t1_b[:, :]).then_inc(pt1_done, 1)

            def split_yr(i, u):
                t = 2 * i + u
                wait(dve, yr_loaded, 4 * 16 * (t + 1))
                wait(dve, yr_split, t)
                V.transpose(yr_f[:, :, :].rearrange("p k r -> p (k r)"),
                            yr_in[:, :]).then_inc(yr_turned, 1)
                wait(dve, yr_turned, t + 1)
                wait(dve, yr_used, t)
                V.tensor_copy(yh[:, 0:4, :], yr_f[:, :, :]).then_inc(yr_hi, 1)
                wait(dve, yr_hi, t + 1)
                V.tensor_tensor(yl[:, 0:4, :], yr_f[:, :, :], yh[:, 0:4, :].bitcast(F32), ALU.subtract).then_inc(yr_split, 1)

            def final(i, u):
                t = 2 * i + u
                wait(dve, frstd_done, t + 1)
                V.scalar_tensor_tensor(xts[u][:, :], xts[u][:, :], rstd, fin_g[:, :], ALU.mult, ALU.mult).then_inc(fin_done, 1)

            def slot_b(i, u):
                t = 2 * i + u
                front = not static(i) or t <= SAMPLE
                back = not static(i) or 1 <= t <= SAMPLE + 1
                prev = (i + (u - 1) // 2, (u + 1) % 2)
                nxt = (i + (u + 1) // 2, (u + 1) % 2)
                if static(i) and t == 1:
                    dve.wait_ge(fixed_loaded, 80)
                    V.tensor_scalar(neg_sink, neg_sink, -1.0, None, ALU.mult).then_inc(const_set, 1)
                    dve.wait_ge(const_set, 3)
                if back:
                    mask_max(*prev, 0)
                if static(i) and t == 1:
                    split_yr(0, 0)
                if not static(i) or t >= 2:
                    final(i - 1, u)
                if back:
                    p_out(*prev, 0)
                    mask_max(*prev, 1)
                if front:
                    wait(dve, aq_hi, t + 1)
                    V.tensor_tensor(aq_row[:, :, 1, :].rearrange("p (j g) d -> p j g d", g=2), by_pairs(zb1[:, :]),
                                    aq_row[:, :, 0, :].rearrange("p (j g) d -> p j g d", g=2).bitcast(F32),
                                    ALU.subtract).then_inc(aq_lo, 1)
                    wait(dve, ag_tanh, t + 1)
                    for g in range(2):
                        ag = a_gates[u][:, :].rearrange("p (j g d) -> p j g d", j=4, g=2)[:, :, g, :]
                        last = V.scalar_tensor_tensor(ag, ag, 1.0, heads(zb2[:, g * KV:(g + 1) * KV]), ALU.add, ALU.mult)
                    last.then_inc(ag_done, 1)
                if back:
                    wait(dve, exp_done, 2 * t)
                    wait(dve, gate_scaled, t - 1)
                    V.tensor_tensor(den, row_sum, sink_exp, ALU.add).then_inc(den_done, 1)
                    wait(dve, den_done, t)
                    V.reciprocal(rden, den).then_inc(rden_done, 1)
                    wait(dve, rden_done, t)
                    wait(dve, ag_done, t)
                    V.scalar_tensor_tensor(heads(a_gates[1 - u][:, :], QH), heads(a_gates[1 - u][:, :], QH), 0.5,
                                           rden.unsqueeze(2).to_broadcast([P, QH, HD]), ALU.mult,
                                           ALU.mult).then_inc(gate_scaled, 1)
                    p_out(*prev, 1)
                if not static(i) or t + 1 <= SAMPLE:
                    split_hb(*nxt)
                if back:
                    wait(dve, pv_ready, 2 * t)
                    wait(dve, ya_hi, t - 1)
                    wait(dve, ya_lo, t - 1)
                    wait(dve, gate_out, t)
                    V.tensor_tensor(ya_f[:, :], pv_b[:, :], a_gates[1 - u][:, :], ALU.mult).then_inc(ya_done, 1)
                    wait(dve, ya_hi, t)
                    wait(dve, ya_done, t)
                    V.tensor_tensor(yl[:, 4:8, :].rearrange("p k r -> p (k r)"), ya_f[:, :],
                                    yh[:, 4:8, :].rearrange("p k r -> p (k r)").bitcast(F32), ALU.subtract).then_inc(ya_lo, 1)
                if front:
                    if not pe_turns(i, t):
                        wait(dve, aq_loaded, 4 * 16 * t)
                        wait(dve, ya_lo, t)
                        wait(dve, x0_added, t - 1)
                        V.transpose(aq_f[:, :], aq_flat.bitcast(F32)).then_inc(aq_turned, 1)
                    wait(dve, ak_hi, t + 1)
                    wait(dve, k_shifted, min(t, SAMPLE - 1) if static(i) else t)
                    if static(i) and t == SAMPLE:
                        V.tensor_tensor(ak_l[:, :, 0:P], s1_b[:, 2 * P:4 * P].rearrange("p (g r) -> p g r", g=2),
                                        ak_h[:, :, 0:P].bitcast(F32), ALU.subtract)
                    V.tensor_tensor(ak_l[:, :, P:2 * P], s1_b[:, 0:2 * P].rearrange("p (g r) -> p g r", g=2),
                                    ak_h[:, :, P:2 * P].bitcast(F32), ALU.subtract).then_inc(ak_lo, 1)
                if static(i) and t == 0:
                    for n in range(B_OUT_LATE, len(pieces)):
                        split_lo(dve, n)
                if front and not (static(i) and t == 0):
                    split_yr(i, u)
                if back:
                    if static(i) and t == SAMPLE + 1:
                        dve.wait_ge(fixed_loaded, 96)
                    xr = xts[1 - u]
                    if front:
                        wait(dve, aqt_done, t + 1)
                    wait(dve, o0_ready, t)
                    wait(dve, x0_added, t - 1)
                    V.tensor_tensor(o_part[:, :], zb0[:, :], out_gate[:, 0:COLS], ALU.mult).then_inc(o0_read, 1)
                    wait(dve, xb_loaded[1 - u], 16 * (i + u))
                    wait(dve, o0_read, t)
                    V.tensor_tensor(xr[:, 0:COLS], xr[:, 0:COLS], o_part[:, :], ALU.add).then_inc(x0_added, 1)
                    wait(dve, o1_ready, t)
                    wait(dve, x1_added, t - 1)
                    V.tensor_tensor(o_part1[:, :], zb1[:, :], out_gate[:, COLS:D], ALU.mult).then_inc(o1_read, 1)
                    wait(dve, o1_read, t)
                    V.tensor_tensor(xr[:, COLS:D], xr[:, COLS:D], o_part1[:, :], ALU.add).then_inc(x1_added, 1)

            phase_tiles(dve, slot_b, SAMPLE + 2)

        @block.tensor
        def _(pe):
            mm = nc.tensor.matmul

            def dense(out, xh, xl, weights, part=(0, 1, 2), chunks=range(KC), first=True, last=True):
                w_hi, w_lo = weights
                passes = [(xh, w_hi), (xh, w_lo), (xl, w_hi)]
                for n in part:
                    a, b = passes[n]
                    for k in chunks:
                        ins = mm(out, a[:, k, :], b[:, k, :], start=first and n == part[0] and k == chunks[0],
                                 stop=last and n == part[-1] and k == chunks[-1])
                return ins

            def group(g):
                return wh[:, g], wl[:, g]

            def transpose_x(t):
                pe.wait_ge(xn_done, t + 1)
                for k in range(KC):
                    last = nc.tensor.transpose(x_banks[t][k // 4][:, (k % 4) * P:(k % 4 + 1) * P],
                                               xn[:, k * P:(k + 1) * P], ident[:, :])
                last.then_inc(x_transposed, 1)

            pe.wait_ge(c_ready, 2)
            pe.wait_ge(c_loaded, 48)
            transpose_x(0)
            for k in range(KC):
                arrived(pe, k)
                for j in range(4):
                    last = mm(out_b[32 * j:32 * j + 32, :], c_wide[:, k, :], stages[slot_of[k]][:, j * COLS:(j + 1) * COLS],
                              start=k == 0, stop=k == KC - 1, tile_position=(0, 32 * j))
                last.then_inc(ada_used, 1)
            pe.wait_ge(mod_rows_out, 1)
            for b in range(4):
                last = nc.tensor.transpose(upd_b[:, b * P:(b + 1) * P], mod_rows[:, b * P:(b + 1) * P], ident[:, :])
            last.then_inc(mod_transposed, 1)

            def dense_first(out, g):
                pe.wait_ge(w_hi_done, 2 * g + 2)
                if g == 0:
                    pe.wait_ge(hi_done, 1)
                dense(out, hh0, hl0, group(g), part=(0,), last=False)
                pe.wait_ge(lo_done, 1)
                dense(out, hh0, hl0, group(g), part=(2,), first=False, last=False)
                pe.wait_ge(w_lo_done, 2 * g + 2)
                return dense(out, hh0, hl0, group(g), part=(1,), first=False)

            def dense_kv(i, u):
                t = 2 * i + u
                wait(pe, b_split, t + 1)
                wait(pe, o0_read, t - 1)
                if static(i) and t == 0:
                    pe.wait_ge(w_lo_done, split_no[B_KV] + 1)
                    pe.wait_ge(v_done, SAMPLE + 1)
                dense(zb0[:, 0:KV], hh0, hl0, (wkvh, wkvl)).then_inc(zb_ready, 1)

            def slot(i, u):
                t = 2 * i + u
                front = not static(i) or t <= SAMPLE
                back = not static(i) or t >= 1
                first = static(i) and t == 0
                h_hi, h_lo = hhs[u], hls[u]
                if front:
                    if first:
                        dense_first(za0[:, :], 0).then_inc(za_ready, 1)
                    else:
                        wait(pe, lo_done, t + 1)
                        wait(pe, v_done, t)
                        dense(za0[:, :], h_hi, h_lo, group(0)).then_inc(za_ready, 1)
                if back:
                    wait(pe, st_done, t)
                    wait(pe, state_done, t - 1)
                    wait(pe, gn_done, t - 1)
                    wait(pe, v_done, t)
                    st = state_s if static(i) and t - 1 == SAMPLE else state
                    for h in range(RH):
                        c = slice(h * DK, (h + 1) * DK)
                        mm(out_b[:, c], s_t[:, c], v_row[:, c], start=True, stop=False)
                        last = mm(out_b[:, c], q_t[:, c], st[:, c], start=False, stop=True)
                    last.then_inc(out_ready, 1)
                    for h in range(RH):
                        c = slice(h * DK, (h + 1) * DK)
                        last = mm(upd_b[:, c], k_row[:, c], v_dec[:, c], start=True, stop=True)
                    last.then_inc(upd_ready, 1)
                if static(i) and t == SAMPLE + 1:
                    dense_kv(0, 0)
                    pe.wait_ge(w_lo_done, split_no[B_GATE - 1] + 1)
                    pe.wait_ge(rg_done, SAMPLE + 1)
                    dense(zb1[:, :], hh0, hl0, group(0)).then_inc(zb_ready, 1)
                    pe.wait_ge(w_lo_done, split_no[B_OUT - 1] + 1)
                    dense(zb2[:, :], hh0, hl0, group(1)).then_inc(zb_ready, 1)
                if first:
                    transpose_x(1)
                if front:
                    wait(pe, rg_done, t)
                    if first:
                        dense_first(za1[:, :], 1).then_inc(za_ready, 1)
                    else:
                        dense(za1[:, :], h_hi, h_lo, group(1)).then_inc(za_ready, 1)
                    if pe_turns(i, t):
                        wait(pe, q_done, t + 1)
                        wait(pe, st_done, t)
                        for h in range(RH):
                            c = slice(h * DK, (h + 1) * DK)
                            last = nc.tensor.transpose(qs_b[:, c], q_row[:, c], ident[:, :])
                        last.then_inc(q_turned, 1)
                    wait(pe, zq_read, t + 1)
                    if first:
                        dense_first(za0[:, :], 2).then_inc(za_ready, 1)
                    else:
                        dense(za0[:, :], h_hi, h_lo, group(2)).then_inc(za_ready, 1)
                if front:
                    wait(pe, zk_read, t + 1)
                    early, late = ((0, 2), (1,)) if first else ((0, 1), (2,))
                    if first:
                        pe.wait_ge(w_hi_done, 8)
                    dense(za1[:, :], h_hi, h_lo, group(3), part=early, last=False)
                    wait(pe, k_done, t + 1)
                    wait(pe, kt_done, t)
                    for h in range(RH):
                        c = slice(h * DK, (h + 1) * DK)
                        last = nc.tensor.transpose(ky_b[:, c], k_row[:, c], ident[:, :])
                    last.then_inc(k_transposed, 1)
                    if first:
                        pe.wait_ge(w_lo_done, 8)
                    dense(za1[:, :], h_hi, h_lo, group(3), part=late, first=False).then_inc(za_ready, 1)
                    wait(pe, st_done, t)
                    wait(pe, qt_done, t + 1)
                    wait(pe, kt_done, t + 1)
                    for h in range(RH):
                        c = slice(h * DK, (h + 1) * DK)
                        last = mm(qs_b[:, c], k_t[:, c], q_t[:, c], start=True, stop=True)
                    last.then_inc(s_ready, 1)
                if static(i) and t == 1:
                    for s in range(4):
                        n = FIRST_GATE + s
                        arrived(pe, n)
                        for kk in range(2):
                            for j in range(2):
                                last = mm(xb0[32 * j:32 * j + 2, :], c_silu[:, 2 * s + kk, :],
                                          stage_view(n)[:, kk, j * COLS:(j + 1) * COLS], start=s == 0 and kk == 0,
                                          stop=s == 3 and kk == 1, tile_position=(0, 32 * j))
                        last.then_inc(ada_used, 1)

            phase_tiles(pe, slot, SAMPLE + 1)

            def scores(i, u, half):
                t = 2 * i + u
                if half == 0:
                    if static(i) and t == 0:
                        pe.wait_ge(b_set, 2)
                    wait(pe, aqt_done, t + 1)
                    wait(pe, ak_hi, t + 1)
                    wait(pe, ak_lo, t + 1)
                    wait(pe, gate_out, t)
                wait(pe, s_masked, 2 * t + half)
                for j in range(4):
                    dst = (s0_b, s1_b)[j // 2][:, (j % 2) * 2 * P:(j % 2 + 1) * 2 * P]
                    q = aq_t[:, 4 * half + j, :]
                    mm(dst, q, ak_h[:, j % 2, :], start=True, stop=False)
                    last = mm(dst, q, ak_l[:, j % 2, :], start=False, stop=True)
                last.then_inc(sb_ready, 1)

            def turn_p(i, u, half):
                t = 2 * i + u
                wait(pe, exp_done, 2 * t + half + 1)
                wait(pe, pt0_done, 2 * t + half)
                wait(pe, pt1_done, 2 * t + half)
                for j in range(4):
                    at = 2 * (j % 2) + j // 2
                    for s in range(2):
                        last = nc.tensor.transpose((t0_b, t1_b)[s][:, at * P:(at + 1) * P],
                                                   s_row[:, j, s * P:(s + 1) * P], ident[:, :])
                last.then_inc(p_transposed, 1)

            def weigh(i, u, half):
                t = 2 * i + u
                wait(pe, pt0_done, 2 * t + half + 1)
                wait(pe, pt1_done, 2 * t + half + 1)
                if half == 0:
                    wait(pe, v_shifted, t)
                    wait(pe, ya_done, t)
                for s in range(2):
                    for g in range(2):
                        cols = slice(g * HD, (g + 1) * HD)
                        v = v_prev[:, cols] if s == 0 else kv_rows[u][:, 2 * P + g * HD:2 * P + (g + 1) * HD]
                        last = mm(pv_b[cols, half * 2 * P:(half + 1) * 2 * P], v, p_t[:, s, 2 * g:2 * g + 2, :],
                                  start=s == 0, stop=s == 1, tile_position=(0, g * HD))
                last.then_inc(pv_ready, 1)

            def slot_b(i, u):
                t = 2 * i + u
                front = not static(i) or t <= SAMPLE
                back = not static(i) or t >= 1
                prev = (i + (u - 1) // 2, (u + 1) % 2)

                def retention_out_0():
                    wait(pe, yr_split, t)
                    wait(pe, kv_done, t + 1 if front else t)
                    if static(i) and t == 1:
                        pe.wait_ge(w_lo_done, len(split_pieces))
                    dense(zb0[:, :], yh, yl, group(2), chunks=range(4), last=False)

                def retention_out_1(part=(0, 1, 2)):
                    wait(pe, aq_lo, t + 1 if front else t)
                    ins = dense(zb1[:, :], yh, yl, group(3), part=part, chunks=range(4), first=part[0] == 0, last=False)
                    if part[-1] == 2:
                        ins.then_inc(yr_used, 1)

                first = static(i) and t == 0
                if front and not first:
                    dense_kv(i, u)
                if back:
                    scores(*prev, 0)
                    if not front:
                        wait(pe, o0_read, t - 1)
                        retention_out_0()
                if front and not first:
                    wait(pe, o1_read, t - 1)
                    dense(zb1[:, :], hh0, hl0, group(0)).then_inc(zb_ready, 1)
                if back:
                    turn_p(*prev, 0)
                    scores(*prev, 1)
                    if not front:
                        wait(pe, o1_read, t - 1)
                        retention_out_1()
                if front and not first:
                    wait(pe, ag_done, t)
                    wait(pe, fsq_done, t - 1)
                    dense(zb2[:, :], hh0, hl0, group(1), part=(0,), last=False)
                if back:
                    weigh(*prev, 0)
                if front and not first:
                    dense(zb2[:, :], hh0, hl0, group(1), part=(1, 2), first=False).then_inc(zb_ready, 1)
                if back:
                    turn_p(*prev, 1)
                    if front:
                        retention_out_0()
                    wait(pe, gate_scaled, t)
                    wait(pe, s_masked, 2 * t)
                    for b in range(4):
                        last = nc.tensor.transpose(s0_b[:, b * P:(b + 1) * P], a_gates[1 - u][:, b * P:(b + 1) * P], ident[:, :])
                    last.then_inc(gate_turned, 1)
                    weigh(*prev, 1)
                    if front:
                        retention_out_1(part=(0, 1))
                if front:
                    wait(pe, kv_done, t + 1)
                    if pe_turns(i, t):
                        wait(pe, aq_hi, t + 1)
                        wait(pe, aq_lo, t + 1)
                        wait(pe, pt0_done, 2 * t)
                        wait(pe, pt1_done, 2 * t)
                        for h in range(QH):
                            nc.tensor.transpose((t0_b, t1_b)[h // 4][:, (h % 4) * P:(h % 4 + 1) * P],
                                                aq_row[:, h, :, :].rearrange("p e d -> p (e d)").bitcast(F32), ident[:, :])
                    sources = [kv_rows[u]]
                    if static(i) and t == SAMPLE:
                        pe.wait_ge(cache_loaded, 6 * 16)
                        pe.wait_ge(newer_loaded, 3 * 16)
                        sources.append(kv_cache)
                    wait(pe, s_masked, 2 * t)
                    wait(pe, ak_lo, t)
                    for s, src in enumerate(sources):
                        for g in range(2):
                            last = nc.tensor.transpose(s1_b[:, (2 * s + g) * P:(2 * s + g + 1) * P],
                                                       src[:, g * P:(g + 1) * P], ident[:, :])
                    last.then_inc(qk_transposed, 1)
                if back:
                    if front:
                        retention_out_1(part=(2,))
                    wait(pe, ya_lo, t)
                    dense(zb0[:, :], yh, yl, group(2), chunks=range(4, 8), first=False).then_inc(o0_ready, 1)
                    dense(zb1[:, :], yh, yl, group(3), chunks=range(4, 8), first=False).then_inc(o1_ready, 1)

            phase_tiles(pe, slot_b, SAMPLE + 1)


def tables():
    import numpy as np
    f = np.float32
    inv = f(1) / np.power(10000.0, (np.arange(0, DK, 2, dtype=f) / f(DK)).astype(np.float64)).astype(f)
    row = np.arange((NT + 1) * P).astype(f)
    row[SAMPLE * P + HALF:] = SEQ + np.arange(HALF)
    ang = (row[:, None] * inv[None, :]).astype(np.float64)
    cos, sin = np.cos(ang), np.sin(ang)
    rope = np.concatenate([cos, -sin, sin], axis=1).astype(f).reshape(NT + 1, P, 192)
    p = np.arange(P)
    g = np.array(GAMMA)
    causal = (p[:, None] <= p[None, :]).astype(np.float64)
    decay = np.concatenate([causal * g[h] ** -(p[:, None] + 1.0) * DK ** -0.5 for h in range(RH)], axis=1).astype(f)
    qdec = np.concatenate([g[h] ** (p + 1.0) for h in range(RH)]).astype(f)[None, :]
    vdec = np.stack([g[h] ** (P - 1.0 - p) * DK ** -0.5 for h in range(RH)], axis=1).astype(f)
    key = np.arange(2 * P)[None, :]
    seen = np.where(p[:, None] < HALF, key < P + HALF, key >= HALF)
    mask = np.stack([np.where(seen, 0.0, MASKED), np.where(seen & (key >= P), 0.0, MASKED)], axis=1).astype(f)
    return {"rope_tab": rope, "ident_tab": np.eye(P, dtype=f), "decay_tab": decay, "qdec_tab": qdec, "vdec_tab": vdec,
            "mask_tab": mask}


_OUTS = [("y_prompt", (SEQ, D), (1, SEQ, D)), ("y_sample", (HALF, D), (1, HALF, D)),
         ("ret_prompt", (RH, DK, DK), (1, 1, RH, DK, DK)), ("k_prompt", (P, P), (1, 1, P, 2, HD)),
         ("v_prompt", (P, P), (1, 1, P, 2, HD)), ("ret_sample", (RH, DK, DK), (1, 1, RH, DK, DK)),
         ("k_sample", (P, P), (1, 1, P, 2, HD)), ("v_sample", (P, P), (1, 1, P, 2, HD))]
_SHAPES = {"x_prompt": (SEQ, D), "x_sample": (HALF, D), "c_prompt": (1, D), "c_sample": (1, D),
           "state_ret": (RH, DK, DK), "cache_k": (P, P), "cache_v": (P, P), "norm_g": (1, D), "w_ada": (D, 3 * D),
           "b_ada": (1, 3 * D), "w_in": (D, IN_W), "sink": (1, QH), "w_out": (D, D), "final_g": (1, D)}


def kernel(**inputs):
    import numpy as np
    import concourse.bacc as bacc
    from concourse.bass_utils import run_bass_kernel_spmd

    nc = bacc.Bacc("TRN2", target_bir_lowering=False, num_devices=1, dynamic_dma_scratch_size=1024)
    arrays, args = {}, []
    given = {n: np.ascontiguousarray(inputs[n]).reshape(s) for n, s in _SHAPES.items()}
    given.update(tables())
    for name, a in given.items():
        arrays["in_" + name] = a
        args.append(nc.dram_tensor("in_" + name, a.shape, F32, kind="ExternalInput").ap())
    for i, (name, shape, _) in enumerate(_OUTS):
        args.append(nc.dram_tensor(f"out_{i}", shape, F32, kind="ExternalOutput").ap())
    args.append(nc.dram_tensor("xn_scratch", (NT + 1, P, D), F32, kind="Internal").ap())
    args.append(nc.dram_tensor("q_scratch", (NT + 1, P, COLS), F32, kind="Internal").ap())
    args.append(nc.dram_tensor("aq_scratch", (NT + 1, P, 2 * COLS), F32, kind="Internal").ap())
    args.append(nc.dram_tensor("h_scratch", (NT + 1, P, D), F32, kind="Internal").ap())
    args.append(nc.dram_tensor("yr_scratch", (NT + 1, P, COLS), F32, kind="Internal").ap())
    args.append(nc.dram_tensor("gate_scratch", (2, D), F32, kind="Internal").ap())
    build_program(nc, *args)
    r = run_bass_kernel_spmd(nc, [arrays], core_ids=[0])
    return tuple(r.results[0][f"out_{i}"].reshape(full) for i, (_, _, full) in enumerate(_OUTS))
```
